# Optimizing a Trainium2 kernel written in Bass

```python
import math
import jax, jax.numpy as jnp
from jax import lax
import numpy as np

D_MODEL = 1024
BATCH = 1
SEQ = 512
DEPTH = 1
DEC_BATCH = 8
DEC_SEQ = 1
PAST_LEN = 1024
PAGE_SIZE = 128

D_RNN = D_MODEL
LRU_BLOCKS = 16
LRU_BW = D_RNN // LRU_BLOCKS
CONV_W = 4
LRU_C = 8.0
N_HEADS = 8
HEAD_DIM = 64
N_KV = 2
GROUP = N_HEADS // N_KV
D_Q = N_HEADS * HEAD_DIM
D_KV = N_KV * HEAD_DIM
ROPE_DIM = HEAD_DIM // 4
ROPE_THETA = 500000.0
CMP_LEN = 32
CMP_STRIDE = 16
CMP_HID = 256
SLC_BLOCK = 64
N_SEL = 16
WINDOW = 512
Q_BLOCK = 64
N_EXPERTS = 32
TOP_K = 4
D_FF = D_MODEL
SWIGLU_LIMIT = 7.0
SWIGLU_ALPHA = 1.702
EPS = 1e-6
NEG = -1e30
BIG = 1e30

kernel_name = 'hawk_nsa_moe_step'

def rms_norm(x, g):
    xf = x.astype(jnp.float32)
    y = xf * lax.rsqrt(jnp.mean(xf * xf, axis=-1, keepdims=True) + EPS)
    return (y * g.astype(jnp.float32)).astype(x.dtype)

def rope(x, pos):
    half = ROPE_DIM // 2
    inv = ROPE_THETA ** (-jnp.arange(half, dtype=jnp.float32) / half)
    ang = pos.astype(jnp.float32)[:, None] * inv[None, :]
    cos, sin = jnp.cos(ang)[:, None, :], jnp.sin(ang)[:, None, :]
    xr = x[..., :ROPE_DIM].astype(jnp.float32)
    x1, x2 = xr[..., :half], xr[..., half:]
    rot = jnp.concatenate([x1 * cos - x2 * sin, x1 * sin + x2 * cos], axis=-1).astype(x.dtype)
    return jnp.concatenate([rot, x[..., ROPE_DIM:]], axis=-1)

def masked_softmax(s, mask):
    s = jnp.where(mask, s.astype(jnp.float32), NEG)
    m = jnp.max(s, axis=-1, keepdims=True)
    p = jnp.where(mask, jnp.exp(s - m), 0.0)
    return p / jnp.maximum(jnp.sum(p, axis=-1, keepdims=True), 1e-30)

def split_proj(h, w_in):
    sizes = (D_RNN, D_RNN, D_Q) + (D_KV,) * 6 + (3 * N_HEADS, D_MODEL, D_MODEL)
    cuts = np.cumsum(sizes)[:-1].tolist()
    return jnp.split(h @ w_in, cuts, axis=-1)

def mixer_inputs(h, pos, w_in, g_q, g_k_cmp, g_k_slc, g_k_win):
    n, s = h.shape[:2]
    ar, ag, q, kc, vc, ks, vs, kw, vw, ng, ga, gb = split_proj(h, w_in)
    heads = lambda t, nh: t.reshape(n, s, nh, HEAD_DIM)
    q = rope(rms_norm(heads(q, N_HEADS), g_q), pos).reshape(n, s, N_KV, GROUP, HEAD_DIM)
    kc = rope(rms_norm(heads(kc, N_KV), g_k_cmp), pos)
    ks = rope(rms_norm(heads(ks, N_KV), g_k_slc), pos)
    kw = rope(rms_norm(heads(kw, N_KV), g_k_win), pos)
    vc, vs, vw = heads(vc, N_KV), heads(vs, N_KV), heads(vw, N_KV)
    ng = ng.reshape(n, s, N_KV, GROUP, 3)
    return ar, ag, q, kc, vc, ks, vs, kw, vw, ng, ga, gb

def merge_branches(y_lru, o_nsa, ga, gb, w_proj_a, w_proj_b, w_out):
    return (jax.nn.sigmoid(ga) * (y_lru @ w_proj_a) + jax.nn.sigmoid(gb) * (o_nsa @ w_proj_b)) @ w_out

def _lin_combine(c1, c2):
    a1, b1 = c1
    a2, b2 = c2
    return a1 * a2, a2 * b1 + b2

def rglru(xr, gate_in, conv_buf, h0, conv_w, conv_b, wa, ba, wx, bx, lam):
    n, s, _ = xr.shape
    xp = jnp.concatenate([conv_buf.astype(xr.dtype), xr], axis=1)
    xc = conv_b + sum(conv_w[k] * xp[:, k:k + s] for k in range(CONV_W))
    xb = xc.reshape(n, s, LRU_BLOCKS, LRU_BW)
    r = jax.nn.sigmoid((jnp.einsum('nsbi,bij->nsbj', xb, wa) + ba).astype(jnp.float32)).reshape(n, s, D_RNN)
    i = jax.nn.sigmoid((jnp.einsum('nsbi,bij->nsbj', xb, wx) + bx).astype(jnp.float32)).reshape(n, s, D_RNN)
    log_a = -LRU_C * r * jax.nn.softplus(-lam.astype(jnp.float32))
    a = jnp.exp(log_a)
    u = jnp.sqrt(-jnp.expm1(2.0 * log_a)) * (i * xc.astype(jnp.float32))
    u = u.at[:, 0].add(a[:, 0] * h0.astype(jnp.float32))
    _, h = lax.associative_scan(_lin_combine, (a, u), axis=1)
    y = (h * jax.nn.gelu(gate_in.astype(jnp.float32))).astype(xr.dtype)
    return y, xp[:, s:], h[:, -1]

def compress(rows, pos_emb, w1, w2):
    n, l = rows.shape[:2]
    r_ = CMP_LEN // CMP_STRIDE
    nch = l // CMP_STRIDE
    ch = rows[:, :nch * CMP_STRIDE].reshape(n, nch, CMP_STRIDE, N_KV, HEAD_DIM)
    w1b = w1.reshape(r_, CMP_STRIDE, HEAD_DIM, CMP_HID)
    part = jnp.einsum('nclhd,pldf->pnchf', ch, w1b)
    nc = nch - r_ + 1
    hid = jnp.einsum('ld,ldf->f', pos_emb, w1) + sum(part[p, :, p:p + nc] for p in range(r_))
    return jnp.einsum('nchf,fd->nchd', jax.nn.gelu(hid), w2)

def block_scores(p_cmp, nsb):
    nc = p_cmp.shape[-1]
    ratio = SLC_BLOCK // CMP_STRIDE
    ovl = CMP_LEN // CMP_STRIDE - 1
    widths = [(0, 0)] * (p_cmp.ndim - 1) + [(ovl, ratio * (nsb + 1) - nc - ovl)]
    pp = jnp.pad(p_cmp, widths).reshape(*p_cmp.shape[:-1], nsb + 1, ratio)
    return pp[..., :nsb, :].sum(-1) + pp[..., 1:, :ovl].sum(-1)

def select_blocks(scores, pos, nsb):
    j = jnp.arange(nsb, dtype=jnp.int32)
    cur = (pos // SLC_BLOCK)[:, None, None]
    forced = (j == 0) | (j == cur) | (j == cur - 1)
    s = jnp.where(forced, BIG, jnp.where(j <= cur, scores, NEG))
    top, idx = lax.top_k(s, min(N_SEL, nsb))
    return idx, top > NEG / 2

def nsa_attend(q, pos, cmp_k, cmp_v, gather_slc, nsb, win_k, win_v, win_pos, gates):
    n, qn = q.shape[:2]
    scale = HEAD_DIM ** -0.5
    nc = cmp_k.shape[1]
    s = jnp.einsum('nqhgd,nchd->nqhgc', q, cmp_k) * scale
    cmp_end = jnp.arange(nc, dtype=jnp.int32) * CMP_STRIDE + CMP_LEN - 1
    p_c = masked_softmax(s, cmp_end <= pos[:, None, None, None])
    o_cmp = jnp.einsum('nqhgc,nchd->nqhgd', p_c.astype(cmp_v.dtype), cmp_v)
    idx, valid = select_blocks(block_scores(p_c.sum(3), nsb), pos, nsb)
    k_g, v_g = gather_slc(idx)
    kk = idx.shape[-1] * SLC_BLOCK
    kpos = idx[..., None] * SLC_BLOCK + jnp.arange(SLC_BLOCK, dtype=jnp.int32)
    smask = (valid[..., None] & (kpos <= pos[:, None, None, None])).reshape(n, qn, N_KV, 1, kk)
    s = jnp.einsum('nqhgd,nqhkd->nqhgk', q, k_g.reshape(n, qn, N_KV, kk, HEAD_DIM)) * scale
    p_s = masked_softmax(s, smask)
    o_slc = jnp.einsum('nqhgk,nqhkd->nqhgd', p_s.astype(v_g.dtype), v_g.reshape(n, qn, N_KV, kk, HEAD_DIM))
    s = jnp.einsum('nqhgd,nkhd->nqhgk', q, win_k) * scale
    dpos = pos[:, None] - win_pos[None, :]
    wmask = (dpos >= 0) & (dpos < WINDOW) & (win_pos >= 0)[None, :]
    p_w = masked_softmax(s, wmask[:, None, None, :])
    o_win = jnp.einsum('nqhgk,nkhd->nqhgd', p_w.astype(win_v.dtype), win_v)
    g = jax.nn.sigmoid(gates)
    return g[..., 0:1] * o_cmp + g[..., 1:2] * o_slc + g[..., 2:3] * o_win

def nsa_prompt(q, kc, vc, ks, vs, kw, vw, ng, pos_k, w1_k, w2_k, pos_v, w1_v, w2_v):
    n, s = q.shape[:2]
    cmp_k = compress(kc, pos_k, w1_k, w2_k)
    cmp_v = compress(vc, pos_v, w1_v, w2_v)
    nsb = s // SLC_BLOCK
    kb = ks.reshape(n, nsb, SLC_BLOCK, N_KV, HEAD_DIM)
    vb = vs.reshape(n, nsb, SLC_BLOCK, N_KV, HEAD_DIM)
    bi = jnp.arange(n)[:, None, None, None]
    hi = jnp.arange(N_KV)[None, None, :, None]

    def gather(idx):
        return kb[bi, idx, :, hi], vb[bi, idx, :, hi]

    pad = ((0, 0), (WINDOW, 0), (0, 0), (0, 0))
    kw_pad, vw_pad = jnp.pad(kw, pad), jnp.pad(vw, pad)

    def block(i):
        start = i * Q_BLOCK
        sl = lambda t, size: lax.dynamic_slice_in_dim(t, start, size, axis=1)
        pos = start + jnp.arange(Q_BLOCK, dtype=jnp.int32)
        wpos = start - WINDOW + jnp.arange(WINDOW + Q_BLOCK, dtype=jnp.int32)
        return nsa_attend(sl(q, Q_BLOCK), pos, cmp_k, cmp_v, gather, nsb,
                          sl(kw_pad, WINDOW + Q_BLOCK), sl(vw_pad, WINDOW + Q_BLOCK), wpos, sl(ng, Q_BLOCK))

    o = lax.map(block, jnp.arange(s // Q_BLOCK, dtype=jnp.int32))
    return jnp.moveaxis(o, 0, 1).reshape(n, s, D_Q)

def nsa_sample(q, kc, vc, ks, vs, kw, vw, ng, page_table, ck_cmp, cv_cmp, ck_slc, cv_slc, ck_win, cv_win,
               pos_k, w1_k, w2_k, pos_v, w1_v, w2_v):
    n, ds = q.shape[:2]
    pos = PAST_LEN + jnp.arange(ds, dtype=jnp.int32)

    def past(pool):
        return pool[page_table].reshape(n, PAST_LEN, N_KV, HEAD_DIM)

    cmp_k = compress(jnp.concatenate([past(ck_cmp), kc], axis=1), pos_k, w1_k, w2_k)
    cmp_v = compress(jnp.concatenate([past(cv_cmp), vc], axis=1), pos_v, w1_v, w2_v)
    past_blocks = PAST_LEN // SLC_BLOCK
    new_blocks = -(-ds // SLC_BLOCK)
    nsb = past_blocks + new_blocks
    bpp = PAGE_SIZE // SLC_BLOCK
    view = lambda pool: pool.reshape(pool.shape[0], bpp, SLC_BLOCK, N_KV, HEAD_DIM)
    pk, pv = view(ck_slc), view(cv_slc)
    padn = ((0, 0), (0, new_blocks * SLC_BLOCK - ds), (0, 0), (0, 0))
    nk = jnp.pad(ks, padn).reshape(n, new_blocks, SLC_BLOCK, N_KV, HEAD_DIM)
    nv = jnp.pad(vs, padn).reshape(n, new_blocks, SLC_BLOCK, N_KV, HEAD_DIM)
    bi = jnp.arange(n)[:, None, None, None]
    hi = jnp.arange(N_KV)[None, None, :, None]

    def gather(idx):
        jp = jnp.minimum(idx, past_blocks - 1)
        phys = page_table[bi, jp // bpp]
        sub = jp % bpp
        jn = jnp.clip(idx - past_blocks, 0, new_blocks - 1)
        is_new = (idx >= past_blocks)[..., None, None]
        return (jnp.where(is_new, nk[bi, jn, :, hi], pk[phys, sub, :, hi]),
                jnp.where(is_new, nv[bi, jn, :, hi], pv[phys, sub, :, hi]))

    wb = ck_win.shape[1]
    wk = jnp.concatenate([ck_win, kw], axis=1)
    wv = jnp.concatenate([cv_win, vw], axis=1)
    wpos = PAST_LEN - wb + jnp.arange(wb + ds, dtype=jnp.int32)
    o = nsa_attend(q, pos, cmp_k, cmp_v, gather, nsb, wk, wv, wpos, ng)
    return o.reshape(n, ds, D_Q), wk[:, -wb:], wv[:, -wb:]

def moe(h, router_w, router_b, w_up, b_up, w_down, b_down):
    shp = h.shape
    t = h.reshape(-1, D_MODEL)
    n_tok = t.shape[0]
    logits = (t @ router_w).astype(jnp.float32) + router_b.astype(jnp.float32)
    top_v, top_e = lax.top_k(logits, TOP_K)
    gate = jax.nn.softmax(top_v, axis=-1)
    n_asg = n_tok * TOP_K
    blk = int(min(512, max(8, n_asg // N_EXPERTS)))
    n_blocks = -(-n_asg // blk) + N_EXPERTS
    e_flat = top_e.reshape(-1)
    tok_flat = jnp.repeat(jnp.arange(n_tok, dtype=jnp.int32), TOP_K)
    g_flat = gate.reshape(-1)
    order = jnp.argsort(e_flat)
    e_sorted = e_flat[order]
    counts = jnp.bincount(e_flat, length=N_EXPERTS)
    padded = (counts + blk - 1) // blk * blk
    pad_end = jnp.cumsum(padded)
    pad_start = pad_end - padded
    starts = jnp.cumsum(counts) - counts
    dest = pad_start[e_sorted] + jnp.arange(n_asg, dtype=jnp.int32) - starts[e_sorted]
    slot_tok = jnp.full((n_blocks * blk,), n_tok, jnp.int32).at[dest].set(tok_flat[order])
    slot_gate = jnp.zeros((n_blocks * blk,), jnp.float32).at[dest].set(g_flat[order])
    blk_expert = jnp.minimum(jnp.searchsorted(pad_end, jnp.arange(n_blocks, dtype=jnp.int32) * blk, side='right'),
                             N_EXPERTS - 1)
    t_pad = jnp.concatenate([t, jnp.zeros((1, D_MODEL), t.dtype)], axis=0)

    def run_block(args):
        tok, g, e = args
        gu = t_pad[tok] @ w_up[e] + b_up[e]
        a = jnp.minimum(gu[:, :D_FF], SWIGLU_LIMIT)
        u = jnp.clip(gu[:, D_FF:], -SWIGLU_LIMIT, SWIGLU_LIMIT)
        y = ((u + 1.0) * a * jax.nn.sigmoid(SWIGLU_ALPHA * a)) @ w_down[e] + b_down[e]
        return (y * g[:, None]).astype(t.dtype)

    ys = lax.map(run_block, (slot_tok.reshape(n_blocks, blk), slot_gate.reshape(n_blocks, blk), blk_expert))
    out = jnp.zeros((n_tok + 1, D_MODEL), t.dtype).at[slot_tok].add(ys.reshape(-1, D_MODEL))
    return out[:n_tok].reshape(shp)

def setup_inputs(seed: int = 0) -> dict:
    keys = list(jax.random.split(jax.random.key(seed), 64))

    def nrm(shape, scale):
        return jax.random.normal(keys.pop(), shape, jnp.float32) * scale

    def gain(n):
        return 1.0 + nrm((DEPTH, n), 0.05)

    n_pages = PAST_LEN // PAGE_SIZE
    n_phys = (DEC_BATCH * n_pages * 5) // 4
    wb = min(WINDOW, PAST_LEN)
    page_table = jax.random.permutation(keys.pop(), n_phys)[:DEC_BATCH * n_pages]
    page_table = page_table.reshape(DEC_BATCH, n_pages).astype(jnp.int32)
    a0 = jax.random.uniform(keys.pop(), (DEPTH, D_RNN), jnp.float32, 0.9, 0.999)
    n_in = 2 * D_RNN + D_Q + 6 * D_KV + 3 * N_HEADS + 2 * D_MODEL
    pool = (DEPTH, n_phys, PAGE_SIZE, N_KV, HEAD_DIM)
    win = (DEPTH, DEC_BATCH, wb, N_KV, HEAD_DIM)
    return {
        'x_prompt': nrm((BATCH, SEQ, D_MODEL), 1.0),
        'x_sample': nrm((DEC_BATCH, DEC_SEQ, D_MODEL), 1.0),
        'page_table': page_table,
        'cache_k_cmp': nrm(pool, 1.0),
        'cache_v_cmp': nrm(pool, 1.0),
        'cache_k_slc': nrm(pool, 1.0),
        'cache_v_slc': nrm(pool, 1.0),
        'cache_k_win': nrm(win, 1.0),
        'cache_v_win': nrm(win, 1.0),
        'state_h': nrm((DEPTH, DEC_BATCH, D_RNN), 0.3),
        'state_conv': nrm((DEPTH, DEC_BATCH, CONV_W - 1, D_RNN), 1.0),
        'g_mix': gain(D_MODEL),
        'w_in': nrm((DEPTH, D_MODEL, n_in), D_MODEL ** -0.5),
        'conv_w': nrm((DEPTH, CONV_W, D_RNN), CONV_W ** -0.5),
        'conv_b': nrm((DEPTH, D_RNN), 0.01),
        'lru_wa': nrm((DEPTH, LRU_BLOCKS, LRU_BW, LRU_BW), LRU_BW ** -0.5),
        'lru_ba': nrm((DEPTH, LRU_BLOCKS, LRU_BW), 0.01),
        'lru_wx': nrm((DEPTH, LRU_BLOCKS, LRU_BW, LRU_BW), LRU_BW ** -0.5),
        'lru_bx': nrm((DEPTH, LRU_BLOCKS, LRU_BW), 0.01),
        'lru_lambda': jnp.log(a0) - jnp.log1p(-a0),
        'g_q': gain(HEAD_DIM),
        'g_k_cmp': gain(HEAD_DIM),
        'g_k_slc': gain(HEAD_DIM),
        'g_k_win': gain(HEAD_DIM),
        'cmp_pos_k': nrm((DEPTH, CMP_LEN, HEAD_DIM), 0.02),
        'cmp_w1_k': nrm((DEPTH, CMP_LEN, HEAD_DIM, CMP_HID), (CMP_LEN * HEAD_DIM) ** -0.5),
        'cmp_w2_k': nrm((DEPTH, CMP_HID, HEAD_DIM), CMP_HID ** -0.5),
        'cmp_pos_v': nrm((DEPTH, CMP_LEN, HEAD_DIM), 0.02),
        'cmp_w1_v': nrm((DEPTH, CMP_LEN, HEAD_DIM, CMP_HID), (CMP_LEN * HEAD_DIM) ** -0.5),
        'cmp_w2_v': nrm((DEPTH, CMP_HID, HEAD_DIM), CMP_HID ** -0.5),
        'w_proj_a': nrm((DEPTH, D_RNN, D_MODEL), D_RNN ** -0.5),
        'w_proj_b': nrm((DEPTH, D_Q, D_MODEL), D_Q ** -0.5),
        'w_out': nrm((DEPTH, D_MODEL, D_MODEL), D_MODEL ** -0.5),
        'g_ffn': gain(D_MODEL),
        'router_w': nrm((DEPTH, D_MODEL, N_EXPERTS), D_MODEL ** -0.5),
        'router_b': nrm((DEPTH, N_EXPERTS), 0.01),
        'exp_w_up': nrm((DEPTH, N_EXPERTS, D_MODEL, 2 * D_FF), D_MODEL ** -0.5),
        'exp_b_up': nrm((DEPTH, N_EXPERTS, 2 * D_FF), 0.01),
        'exp_w_down': nrm((DEPTH, N_EXPERTS, D_FF, D_MODEL), D_FF ** -0.5),
        'exp_b_down': nrm((DEPTH, N_EXPERTS, D_MODEL), 0.01),
    }

def reference(x_prompt, x_sample, page_table, cache_k_cmp, cache_v_cmp, cache_k_slc, cache_v_slc,
              cache_k_win, cache_v_win, state_h, state_conv, g_mix, w_in, conv_w, conv_b, lru_wa, lru_ba,
              lru_wx, lru_bx, lru_lambda, g_q, g_k_cmp, g_k_slc, g_k_win, cmp_pos_k, cmp_w1_k, cmp_w2_k,
              cmp_pos_v, cmp_w1_v, cmp_w2_v, w_proj_a, w_proj_b, w_out, g_ffn, router_w, router_b,
              exp_w_up, exp_b_up, exp_w_down, exp_b_down):
    xp, xs = x_prompt, x_sample
    bp, sp = xp.shape[:2]
    pos_p = jnp.arange(sp, dtype=jnp.int32)
    pos_s = PAST_LEN + jnp.arange(xs.shape[1], dtype=jnp.int32)
    layer_states = []
    for l in range(DEPTH):
        cmp_w = (cmp_pos_k[l], cmp_w1_k[l], cmp_w2_k[l], cmp_pos_v[l], cmp_w1_v[l], cmp_w2_v[l])
        lru_w = (conv_w[l], conv_b[l], lru_wa[l], lru_ba[l], lru_wx[l], lru_bx[l], lru_lambda[l])
        ar, ag, q, kc, vc, ks, vs, kw, vw, ng, ga, gb = mixer_inputs(
            rms_norm(xp, g_mix[l]), pos_p, w_in[l], g_q[l], g_k_cmp[l], g_k_slc[l], g_k_win[l])
        y_lru, p_conv, p_h = rglru(ar, ag, jnp.zeros((bp, CONV_W - 1, D_RNN), xp.dtype),
                                   jnp.zeros((bp, D_RNN), jnp.float32), *lru_w)
        o_nsa = nsa_prompt(q, kc, vc, ks, vs, kw, vw, ng, *cmp_w)
        xp = xp + merge_branches(y_lru, o_nsa, ga, gb, w_proj_a[l], w_proj_b[l], w_out[l])
        wbp = min(WINDOW, sp)
        p_states = (kc, vc, ks, vs, kw[:, -wbp:], vw[:, -wbp:], p_h, p_conv)
        ar, ag, q, kc, vc, ks, vs, kw, vw, ng, ga, gb = mixer_inputs(
            rms_norm(xs, g_mix[l]), pos_s, w_in[l], g_q[l], g_k_cmp[l], g_k_slc[l], g_k_win[l])
        y_lru, s_conv_l, s_h_l = rglru(ar, ag, state_conv[l], state_h[l], *lru_w)
        o_nsa, s_kw_l, s_vw_l = nsa_sample(q, kc, vc, ks, vs, kw, vw, ng, page_table, cache_k_cmp[l],
                                           cache_v_cmp[l], cache_k_slc[l], cache_v_slc[l],
                                           cache_k_win[l], cache_v_win[l], *cmp_w)
        xs = xs + merge_branches(y_lru, o_nsa, ga, gb, w_proj_a[l], w_proj_b[l], w_out[l])
        s_states = (kc, vc, ks, vs, s_kw_l, s_vw_l, s_h_l, s_conv_l)
        moe_w = (router_w[l], router_b[l], exp_w_up[l], exp_b_up[l], exp_w_down[l], exp_b_down[l])
        xp = xp + moe(rms_norm(xp, g_ffn[l]), *moe_w)
        xs = xs + moe(rms_norm(xs, g_ffn[l]), *moe_w)
        layer_states.append(p_states + s_states)
    (p_k_cmp, p_v_cmp, p_k_slc, p_v_slc, p_k_win, p_v_win, p_h, p_conv,
     s_k_cmp, s_v_cmp, s_k_slc, s_v_slc, s_k_win, s_v_win, s_h, s_conv) = [jnp.stack(z) for z in zip(*layer_states)]
    return (xp, xs, p_k_cmp, p_v_cmp, p_k_slc, p_v_slc, p_k_win, p_v_win, p_h, p_conv,
            s_k_cmp, s_v_cmp, s_k_slc, s_v_slc, s_k_win, s_v_win, s_h, s_conv)


_drawn_inputs = setup_inputs


def setup_inputs(seed=0):
    import zlib

    import numpy as np

    out = dict(_drawn_inputs(seed))
    spreads = {}
    factors = {'cache_v_slc': 3.499,
     'lru_ba': 22.934,
     'lru_bx': 7.457,
     'g_q': 5.774,
     'cmp_pos_k': 8.0,
     'cmp_pos_v': 6.033,
     'exp_b_up': 8.0,
     'exp_b_down': 8.0}
    for name, (base, spread) in spreads.items():
        noise = np.random.default_rng([zlib.crc32(name.encode()), seed]).standard_normal(out[name].shape)
        drawn = base * np.exp(spread * noise) if base else spread * noise
        out[name] = __import__('jax').numpy.asarray(drawn.astype(out[name].dtype))
    for name, factor in factors.items():
        out[name] = (out[name] * factor).astype(out[name].dtype)
    return out
```

```python
from contextlib import ExitStack
import math

import numpy as np

import concourse.bass as bass
from concourse import mybir

ALU = mybir.AluOpType
ACT = mybir.ActivationFunctionType
AX = mybir.AxisListType.X
F32 = mybir.dt.float32
I32 = mybir.dt.int32
U32 = mybir.dt.uint32

P = 128
D = 1024
KD = D // P
NPR = 512
NSA = 8
NT = NPR + NSA
HN = NT // 2
QT_N = NPR // P
TT = QT_N + 1
PAST = 1024
PAGE = 128
NPG = PAST // PAGE
NPAGES = NSA * NPG
HD = 64
NKV = 2
NG = 4
NH = NKV * NG
NROW = NSA * NH
NHN = NH + 3 * NKV
QC = NH * HD
KVC = 6 * NKV * HD
TC = QC + KVC + 3 * NH
LP = 8
NCH = 32
CHS = PAST // 16
CF = 256
WIN = 512
NE = 32
TOPK = 4
RT = 5
RN = NT // RT
SLOTS = 5 * P
TRASH = NT
SCALE = HD ** -0.5
NEG = -1e30
EPS = 1e-6
LIMIT = 7.0
ALPHA = 1.702
SLOT = 4096
NSLOT = 6
SMALL_IN = 32
ROUTER_IN = 80
VC = 3 * NKV * HD


class Steps:

    def __init__(self, eng, own):
        self.eng, self.own, self.n, self.last = eng, own, {}, None

    def __call__(self, ins, sem=None):
        sem = self.own if sem is None else sem
        self.n[id(sem)] = self.n.get(id(sem), 0) + 1
        ins.then_inc(sem, 1)
        self.last = (sem, self.n[id(sem)])

    def settle(self):
        self.eng.wait_ge(*self.last)


def ring_plan():
    return [("ar0", 1), ("ag0", 1), ("ar1", 1), ("ag1", 1),
            ("xsk", 2), ("w1k", 1), ("xsv", 2), ("w1v", 1),
            ("kslc", 2), ("vslc", 2), ("kwin", 1), ("vwin", 1),
            ("ga0", 1), ("gb0", 1), ("pa0", 1), ("pb0", 1),
            ("ga1", 1), ("gb1", 1), ("pa1", 1), ("pb1", 1),
            ("wo0", 1), ("wo1", 1)]


def build(nc, d):
    ctx = ExitStack()
    with ctx:
        def sb(name, shape, dt=F32):
            return ctx.enter_context(nc.sbuf_tensor(name, shape, dt))

        def sem(name):
            return ctx.enter_context(nc.semaphore(name))

        ring = sb("ring", [P, NSLOT * SLOT])
        slab = sb("slab", [P, KD * TC])
        xn = sb("xn", [P, KD, NT])
        qraw = sb("qraw", [P, TT, QC])
        kvraw = sb("kvraw", [P, TT, KVC + 3 * NH])
        qT = sb("qT", [P, NG, NT])
        kT = sb("kT", [P, 3, NT])
        oT_st = sb("oT", [P, NG * NT])
        oT = oT_st[:, :].rearrange("p (g t) -> p g t", g=NG)
        ident = sb("ident", [P, P])
        SMALL = 1670
        small = sb("small", [P, SMALL])
        bank = ctx.enter_context(nc.psum_tensor("bank", [P, 8, 512], F32))

        at = [0]

        def part(n):
            at[0] += n
            assert at[0] <= SMALL
            return small[:, at[0] - n:at[0]]

        cmask = part(4 * 32).rearrange("p (q c) -> p q c", q=4)
        rope = part(TT * 16).rearrange("p (t x) -> p t x", t=TT)
        gmix = part(KD)
        lruv = part(KD * 8).rearrange("p (m x) -> p m x", m=KD)
        h0 = part(KD * NSA).rearrange("p (m n) -> p m n", m=KD)
        xps = part(KD * NSA * 4).rearrange("p (m n k) -> p m n k", m=KD, n=NSA)
        causal = part(P)
        onesm = part(P)
        sel16 = part(16)
        sel8 = part(8)
        selh = part(8)
        selv = part(2)
        rmat = part(NROW)
        emat = part(NROW)
        posc = part(4 * LP).rearrange("p (v l x) -> p v l x", v=2, l=LP)
        iota16 = part(16)
        pconv = part(KD * 3).rearrange("p (m k) -> p m k", m=KD)
        hout = part(KD * 9).rearrange("p (m k) -> p m k", m=KD)
        pagetab = part(NPAGES)
        hb = part(2 * KD).rearrange("p (x m) -> p x m", x=2)
        c2 = part(2 * KD).rearrange("p (x m) -> p x m", x=2)
        lt = part(4 * KD).rearrange("p (x m) -> p x m", x=4)
        ssq = part(TT * NHN).rearrange("p (t h) -> p t h", t=TT)
        rsq = part(TT * NHN).rearrange("p (t h) -> p t h", t=TT)
        eps1 = part(1)
        stat = part(32)
        cbias = part(4)
        ovf = part(2)
        entf = [part(2), part(2)]
        negc = part(4 * 32).rearrange("p (q c) -> p q c", q=4)
        ent = [e.bitcast(I32) for e in entf]

        slot_of, count_of, order_of, j = {}, {}, {}, 0
        loads = [0] * NSLOT
        for name, n in ring_plan():
            slot_of[name], order_of[name] = j % NSLOT, j
            assert j % NSLOT + n <= NSLOT
            if n == 1 and name != "vwin":
                loads[j % NSLOT] += 1
                count_of[name] = 16 * loads[j % NSLOT]
            j += n
        NFRONT = j
        eslot = [(NFRONT + c) % NSLOT for c in range(6)]
        ebase = [16 * loads[s] for s in eslot]

        def chunk(name, n=1):
            s = slot_of[name]
            return ring[:, s * SLOT:(s + n) * SLOT]

        def w8(name):
            return chunk(name).rearrange("p (k n) -> p k n", k=KD)

        xsq = ring[:, 4 * SLOT:4 * SLOT + KD * NT].rearrange("p (k t) -> p k t", k=KD)
        rstd = ring[:, 4 * SLOT + KD * NT:4 * SLOT + KD * NT + NT]
        wtok = slab[:, :].rearrange("p (k n) -> p k n", k=KD)
        A = slab[:, 0:4 * NT].rearrange("p (m t) -> p m t", m=4)
        V = slab[:, 4 * NT:8 * NT].rearrange("p (m t) -> p m t", m=4)
        IX = slab[:, 8 * NT:12 * NT].rearrange("p (m t) -> p m t", m=4)
        Y = slab[:, 12 * NT:20 * NT].rearrange("p (m t) -> p m t", m=KD)
        gh = slab[:, 0:4096].rearrange("p (v f h c) -> p v f h c", v=2, f=2, h=2)
        p1c = slab[:, 4096:5120].rearrange("p (b c) -> p b c", b=2)
        hrep = slab[:, 5120:5632].rearrange("p (f h r c) -> p f h r c", f=2, h=2, r=4)
        ghp = slab[:, 5632:6144].rearrange("p (v f c) -> p v f c", v=2, f=2)[:, :, :, 0:64]
        ckT = slab[:, 4096:4608]
        cv = slab[:, 4608:5120].rearrange("p (t c) -> p t c", t=4)
        PR = slab[:, 0:2048].rearrange("p (b h k) -> p b h k", b=2, h=2)
        PT = slab[:, 2048:4096].rearrange("p (b h k) -> p b h k", b=2, h=2)
        OA = slab[:, 5120:5632].rearrange("p (g v e) -> p g v e", g=NG, v=NKV)
        qbd = slab[:, 5632:5696]
        qz = slab[:, 5696:6208]
        sqt = oT_st[:, 0:NHN * HD].rearrange("p (h c) -> p h c", h=NHN)
        gain = oT_st[:, NHN * HD:2 * NHN * HD].rearrange("p (h c) -> p h c", h=NHN)
        bd = oT_st[:, 0:2 * KD * P].rearrange("p (x m c) -> p x m c", x=2, m=KD)
        qf = qraw[:, :, :].rearrange("p t c -> p (t c)")
        xpp = qf[:, 0:2 * 515].rearrange("p (b c) -> p b c", b=2)
        xc = qf[:, 1030:1030 + 2 * NT].rearrange("p (b c) -> p b c", b=2)
        xp = qf[:, 0:LP * 66 * 2].rearrange("p (v l c) -> p v l c", v=2, l=LP)
        w2 = qf[:, 1056:1056 + 2 * 2 * 3 * HD].rearrange("p (v f c) -> p v f c", v=2, f=2)
        ckTp = qf[:, 2016:2048]
        cvp = qf[:, 2048:2560].rearrange("p (v g e) -> p v g e", v=2, g=4)
        smask = qf[:, 0:512]
        oS = qf[:, 512:576]
        sw = qf[:, 576:576 + 1024]
        sw2 = slab[:, 0:1024]
        sw2o = slab[:, 1024:1088]
        mT = slab[:, 0:KD * NT].rearrange("p (k t) -> p k t", k=KD)
        sg = slab[:, 4160:4160 + 2 * NT].rearrange("p (b t) -> p b t", b=2)
        mb = slab[:, 5200:5200 + NT]
        sq_rows = oT_st[:, 0:D]
        xm = slab[:, 5120:5120 + 3 * D].rearrange("p (b n) -> p b n", b=3)
        tn = slab[:, 8288:8288 + 2048].rearrange("p (b n) -> p b n", b=2)
        kvf = kvraw[:, :, :].rearrange("p t c -> p (t c)")
        tT = kvf[:, 0:KD * P].rearrange("p (k t) -> p k t", k=KD)
        xr = kvf[:, 1024:1024 + 2048].rearrange("p (b n) -> p b n", b=2)
        lg = kvf[:, 3072:3072 + RT * NE].rearrange("p (t e) -> p t e", t=RT)
        oh = kvf[:, 3232:3232 + 4 * NE].rearrange("p (k e) -> p k e", k=4)
        gd = kvf[:, 3360:3360 + NE]
        gdT = kvf[:, 3392:3392 + P]
        rj = kvf[:, 3520:3520 + 128]
        gffn = qf[:, 0:D]
        bdn = qf[0:NE, D:2 * D]
        rw = oT_st[:, 0:0]
        qtf = qT[:, :, :].rearrange("p g t -> p (g t)")
        rwt = qtf[:, 0:KD * NE].rearrange("p (k e) -> p k e", k=KD)
        rcon = qtf[:, 256:256 + 4 * NE + 128 + 8]
        rbias, iota_e, slot_e, tri = rcon[:, 0:32], rcon[:, 32:64], rcon[:, 64:96], rcon[:, 96:96 + RN]
        tokid = rcon[:, 200:200 + RT].bitcast(I32)
        m4 = qtf[:, 520:520 + RT * NE].rearrange("p (t e) -> p t e", t=RT)
        mx8 = qtf[:, 680:680 + RT * 8].rearrange("p (t k) -> p t k", t=RT)
        ix8 = qtf[:, 720:720 + RT * 8].rearrange("p (t k) -> p t k", t=RT)
        ixf = qtf[:, 760:760 + RT * 4].rearrange("p (t k) -> p t k", t=RT)
        gate = qtf[:, 780:780 + RT * 4].rearrange("p (t k) -> p t k", t=RT)
        rs = qtf[:, 800:832]
        posn = qtf[:, 832:832 + RT * NE].rearrange("p (t e) -> p t e", t=RT)
        dst = qtf[:, 992:992 + RT * 4].rearrange("p (t k) -> p t k", t=RT)
        dsti = qtf[:, 1012:1012 + RT * 4].rearrange("p (t k) -> p t k", t=RT)
        pairs = qtf[:, 1032:1032 + RT * 8].rearrange("p (t k x) -> p t k x", t=RT, k=4)
        ohall = xn[:, 0:2, :].rearrange("p k t -> p (k t)")[:, 0:RT * 4 * NE]\
            .rearrange("p (t k e) -> p t k e", t=RT, k=4)
        bup = xn[:, 2, 0:512].rearrange("p (e c) -> p e c", e=NE)
        GX = [slab[:, b * D:(b + 1) * D] for b in (0, 1)]
        XT = [slab[:, (2 + b) * D:(3 + b) * D].rearrange("p (k t) -> p k t", k=KD) for b in (0, 1)]
        HT = [slab[:, (4 + b) * D:(5 + b) * D].rearrange("p (k t) -> p k t", k=KD) for b in (0, 1)]
        YR = [slab[:, (6 + b) * D:(7 + b) * D] for b in (0, 1)]
        AA = [slab[:, 8192 + b * 512:8704 + b * 512] for b in (0, 1)]
        UU = [slab[:, 9216 + b * 512:9728 + b * 512] for b in (0, 1)]
        SG = [kvf[:, b * 512:(b + 1) * 512] for b in (0, 1)]
        bu2 = [kvf[:, 1024 + b * 16:1040 + b * 16] for b in (0, 1)]

        trow = nc.dram_tensor("token_rows", (NT + P, D), F32).ap()
        table = nc.dram_tensor("slot_table", (NE * SLOTS, 2), I32).ap()

        S = {n: sem(n) for n in """
            pe_steps act_steps dve_steps pool_steps small_in x_in wtok_in page_in gains_in bd_in
            x_squared x_summed x_root xn_ready rms_free tok_done tok_copied ss_ready rs_root qk_ready qk_turned qk_dve qk_act
            kv_out ar_done ar_copied ag_done ag_gelu r_done i_done th_ready ti_ready xc_ready decay_ready gap_ready
            gap_root y_ready lam_ready lam_exp gates_t gates_ready
            xsk_in xsv_in xsv_in_pool kslc_in vslc_in w2_in
            cs_done p1_copied gh_raw xp_ready vt_done cp_done pp_copied ghp_raw gh_gelu hrep_ready ck_done ck_copied
            att_s att_max att_p att_pc att_ce att_cs att_ta att_td att_pa att_pv att_o rec_free vwin_in
            smp_pe smp_dve smp_act smp_max smask_in bias_ready u_ready ua_ready
            ga_done pa_done gb_done pb_done sg_ready m_ready
            wo_done router_in xm_ready ss2 rstd2 t_ready t_turned t_copied lg_done ex_in ex_done gd_ready gd_turned
            gd_copied bd_done y0_ready m4_ready pos_done ent_ready table_in scattered bup_in ovf_ready
            xg_in ent_in x_turned xt_ready ring_used up_read sig_ready h_ready y_scaled y_added
            outs_done cache_out""".split()}
        x_rows_in, t_out = ([sem(f"{n}{b}") for b in (0, 1)] for n in ("x_rows_in", "t_out"))
        y0_out = [sem(f"y0_out{b}") for b in range(3)]
        ring_in = [sem(f"ring_in{i}") for i in range(NSLOT)]

        block = ctx.enter_context(nc.Block())
        items = []
        for qt in range(QT_N):
            items.append(("cmp", qt, 0, 0))
            items += [("full", qt, b, g) for b in (1, 2) for g in range(NG)]
            items.append(("out", qt, 0, 0))

        n_full = [sum(x[0] == "full" for x in items[:i + 1]) for i in range(len(items))]
        n_cmp = [sum(x[0] == "cmp" for x in items[:i + 1]) for i in range(len(items))]
        n_v = [a + b for a, b in zip(n_full, n_cmp)]

        def halves(pair, n=HN):
            return bank[:, 2 * pair:2 * pair + 2, 0:n]

        def split(x):
            return x.rearrange("p (h t) -> p h t", h=2)

        def fraction(k):
            return P if k < QT_N else NSA

        frees = {"ar0": (S["ar_done"], 4), "ag0": (S["ag_done"], 4), "ar1": (S["ar_done"], 8), "ag1": (S["ag_done"], 8),
                 "xsk": (S["cs_done"], 4), "w1k": (S["cp_done"], 2), "xsv": (S["cs_done"], 8), "w1v": (S["cp_done"], 4),
                 "kslc": (S["smp_pe"], 5), "vslc": (S["smp_pe"], 7), "kwin": (S["smp_pe"], 5), "vwin": (S["smp_pe"], 9),
                 "ga0": (S["ga_done"], 4), "gb0": (S["gb_done"], 4), "pa0": (S["pa_done"], 4), "pb0": (S["pb_done"], 4),
                 "ga1": (S["ga_done"], 8), "gb1": (S["gb_done"], 8), "pa1": (S["pa_done"], 8), "pb1": (S["pb_done"], 8),
                 "wo0": (S["wo_done"], RT), "wo1": (S["wo_done"], RT)}
        owner = {}
        before = {}
        jj = 0
        for name, n in ring_plan():
            sl = [(jj + i) % NSLOT for i in range(n)]
            before[name] = [owner[x] for x in sl if x in owner]
            for x in sl:
                owner[x] = name
            jj += n

        def some_pages(eng, dst, pool, signal, first, n):
            with eng.Fori(first // 4, (first + n) // 4) as i:
                rows = [eng.value_load(pagetab[0:1, bass.ds(4 * i + u, 1)].bitcast(I32), min_val=0, max_val=d["n_phys"] - 1)
                        for u in range(4)]
                for u, page in enumerate(rows):
                    eng.dma_start(dst[:, bass.ds((4 * i + u) * P, P)], pool[bass.ds(page * P, P), :]).then_inc(signal, 16)

        @block.sync
        def _(sp):
            sp.dma_start(xn[:, :, :], d["xT"]).then_inc(S["x_in"], 16)
            for c in range(4):
                sp.dma_start(wtok[:, 2 * c:2 * c + 2, :], d["w_tok"][:, 2 * c:2 * c + 2, :]).then_inc(S["wtok_in"], 16)

            def slots_free(name):
                for other in dict.fromkeys(before[name]):
                    sp.wait_ge(*frees[other])

            def load(name, src):
                slots_free(name)
                sp.dma_start(chunk(name)[:, 0:src.shape[1]], src).then_inc(ring_in[slot_of[name]], 16)

            def load_pages(name, pool, signal, pages=NPAGES):
                slots_free(name)
                some_pages(sp, chunk(name, 2), pool, signal, 0, pages)

            load("ar0", d["w_ch"][0])
            load("ag0", d["w_ch"][2])
            load("ar1", d["w_ch"][1])
            load("ag1", d["w_ch"][3])
            sp.wait_ge(S["page_in"], 16)
            sp.wait_ge(S["rms_free"], 1)
            load_pages("xsk", d["k_cmp"], S["xsk_in"])
            load("w1k", d["w1"][0])
            load_pages("xsv", d["v_cmp"], S["xsv_in"], NPAGES // 2)
            load("w1v", d["w1"][1])
            load_pages("kslc", d["k_slc"], S["kslc_in"])
            load_pages("vslc", d["v_slc"], S["vslc_in"])
            slots_free("kwin")
            sp.dma_start(chunk("kwin").rearrange("p (n k) -> p n k", n=NSA), d["k_win"])\
                .then_inc(ring_in[slot_of["kwin"]], 16)
            slots_free("vwin")
            for n in range(NSA):
                sp.dma_start(chunk("vwin")[:, n * WIN:(n + 1) * WIN].rearrange("p (t c) -> p t c", t=4),
                             d["v_win"][n].rearrange("(t p) c -> p t c", p=P)).then_inc(S["vwin_in"], 16)
            for c in range(2):
                load(f"ga{c}", d["w_ch"][4 + c])
                load(f"gb{c}", d["w_ch"][6 + c])
                load(f"pa{c}", d["w_pa"][c])
                load(f"pb{c}", d["w_pb"][c])
            load("wo0", d["w_out"][0])
            load("wo1", d["w_out"][1])

            up = d["w_up"].rearrange("(e k p) (c n) -> e p c k n", k=KD, p=P, c=4)
            down = d["w_down"].rearrange("(e h f p) n -> e h p f n", h=2, f=4, p=P)
            upflat = d["w_up"]
            order = (0, 2, 1, 3)

            def expert_chunk(e, c):
                dst = ring[:, eslot[c] * SLOT:(eslot[c] + 1) * SLOT]
                if c < 4:
                    q = order[c]
                    src = d["w_up"][bass.ds(e * D, D), q * 512:(q + 1) * 512].rearrange("(k p) n -> p k n", p=P)
                    dst = dst.rearrange("p (k n) -> p k n", k=KD)
                else:
                    src = d["w_down"][bass.ds(e * D + (c - 4) * 512, 512), :].rearrange("(f p) n -> p f n", p=P)
                    dst = dst.rearrange("p (f n) -> p f n", f=4)
                sp.dma_start(dst, src).then_inc(ring_in[eslot[c]], 16)

            for c in range(6):
                sp.wait_ge(*frees[owner[eslot[c]]])
                expert_chunk(0, c)
            with sp.Fori(1, NE) as e:
                for c in range(6):
                    sp.wait_ge(S["ring_used"], 6 * e + c - 5)
                    expert_chunk(e, c)
            sp.wait_ge(S["ovf_ready"], 1)
            most = sp.value_load(ovf[0:1, 1:2].bitcast(I32), min_val=0, max_val=NT)
            with sp.If(most > P):
                with sp.Fori(0, NE) as e:
                    for b in range(4):
                        for c in range(6):
                            sp.wait_ge(S["ring_used"], 24 * e + 6 * (NE + b) + c - 5)
                            expert_chunk(e, c)

        @block.tensor
        def _(pe):
            mm = pe.matmul

            def two_halves(pair, lhsT, rhs, first, last):
                for h in (0, 1):
                    r = mm(bank[:, 2 * pair + h, 0:HN], lhsT, rhs[:, h * HN:(h + 1) * HN], start=first, stop=last)
                return r

            pe.wait_ge(S["small_in"], SMALL_IN)
            for k in range(KD):
                pe.wait_ge(S["x_squared"], k + 1)
                r = two_halves(3, onesm, xsq[:, k, :], k == 0, k == KD - 1)
            r.then_inc(S["x_summed"], 1)
            for t in range(TT):
                if t >= 2:
                    pe.wait_ge(S["tok_copied"], t - 1)
                m = fraction(t)
                for k in range(KD):
                    if t == 0:
                        pe.wait_ge(S["xn_ready"], k + 1)
                        pe.wait_ge(S["wtok_in"], 64)
                    for c, (a, b) in enumerate(((0, 512), (512, 1024), (1024, TC))):
                        r = mm(bank[0:m, 3 * (t % 2) + c, 0:b - a], xn[:, k, t * P:t * P + m], wtok[:, k, a:b],
                               start=k == 0, stop=k == KD - 1)
                r.then_inc(S["tok_done"], 1)
            for t in range(TT):
                pe.wait_ge(S["qk_ready"], t + 1)
                if t == 0:
                    pe.wait_ge(S["tok_copied"], TT)
                m = fraction(t)
                for c in range(7):
                    src = qraw[0:m, t, c * P:(c + 1) * P] if c < NG else kvraw[0:m, t, (c - NG) * P:(c - NG + 1) * P]
                    out = bank[:, c, t * P:(t + 1) * P] if t < QT_N else bank[:, 7, c * NSA:(c + 1) * NSA]
                    r = pe.transpose(out, src, ident[0:m, 0:m])
            r.then_inc(S["qk_turned"], 1)

            def block_gates(m):
                for x, done in ((0, "r_done"), (1, "i_done")):
                    if x == 0:
                        pe.wait_ge(S["xc_ready"], m + 1)
                        if m >= 1:
                            pe.wait_ge(S["th_ready"], m)
                    elif m >= 1:
                        pe.wait_ge(S["ti_ready"], m)
                    two_halves(2 + x, bd[:, x, m, :], xc[:, m % 2, :], True, True).then_inc(S[done], 1)

            pe.wait_ge(S["qk_act"], 1)
            pe.wait_ge(S["qk_dve"], 1)
            pe.wait_ge(S["bd_in"], 16)
            for m in range(KD):
                for name, pair, done, freed in (("ar", 0, "ar_done", "ar_copied"), ("ag", 1, "ag_done", "ag_gelu")):
                    name += str(m // 4)
                    if m % 4 == 0:
                        pe.wait_ge(ring_in[slot_of[name]], count_of[name])
                    if m >= 1:
                        pe.wait_ge(S[freed], m)
                    for k in range(KD):
                        r = two_halves(pair, w8(name)[:, k, (m % 4) * P:(m % 4 + 1) * P], xn[:, k, :],
                                       k == 0, k == KD - 1)
                    r.then_inc(S[done], 1)
                if m >= 1:
                    block_gates(m - 1)
            block_gates(KD - 1)

            def hidden_samples(v):
                xs = chunk(("xsk", "xsv")[v], 2).rearrange("p (g l c) -> p g l c", g=NPAGES, l=2 * LP)
                w1 = chunk(("w1k", "w1v")[v]).rearrange("p (x l f) -> p x l f", x=2, l=LP)
                if v == 0:
                    pe.wait_ge(S["xsk_in"], 16 * NPAGES)
                else:
                    pe.wait_ge(S["xsv_in"], 8 * NPAGES)
                    pe.wait_ge(S["xsv_in_pool"], 8 * NPAGES)
                name = ("w1k", "w1v")[v]
                pe.wait_ge(ring_in[slot_of[name]], count_of[name])
                for f in range(2):
                    for h in range(2):
                        u = 4 * v + 2 * f + h
                        q = u % 3
                        if u >= 3:
                            pe.wait_ge(S["gh_raw"], u - 2)
                        for x in range(2):
                            for l in range(LP):
                                r = mm(bank[:, 2 * q + x, :], w1[:, x, l, f * P:(f + 1) * P], xs[:, :, 2 * l + h, :],
                                       start=l == 0, stop=l == LP - 1)
                        r.then_inc(S["cs_done"], 1)

            def hidden_prompt(v):
                w1 = chunk(("w1k", "w1v")[v]).rearrange("p (x l f) -> p x l f", x=2, l=LP)
                pe.wait_ge(S["xp_ready"], v + 1)
                for f in range(2):
                    if v or f:
                        pe.wait_ge(S["ghp_raw"], 2 * v + f)
                    for x in range(2):
                        for l in range(LP):
                            r = mm(bank[:, 6, 66 * x:66 * x + 66], w1[:, x, l, f * P:(f + 1) * P], xp[:, v, l, :],
                                   start=l == 0, stop=l == LP - 1)
                    r.then_inc(S["cp_done"], 1)

            pe.wait_ge(S["ti_ready"], KD)
            pe.wait_ge(S["th_ready"], KD)
            pe.wait_ge(S["ag_gelu"], KD)
            for t in range(QT_N):
                r = pe.transpose(bank[:, 7, t * P:(t + 1) * P], kvraw[:, t, VC:VC + P], ident[:, :])
            r.then_inc(S["vt_done"], 1)
            hidden_samples(0)
            hidden_prompt(0)
            hidden_samples(1)
            hidden_prompt(1)
            pe.wait_ge(S["w2_in"], 16)
            pe.wait_ge(S["gh_gelu"], 2)
            pe.wait_ge(S["gh_raw"], 8)
            pads = ((HD, 3 * HD), (0, 2 * HD))
            for x in range(4):
                f, h = divmod(x, 2)
                a, b = pads[h]
                mm(bank[:, 0, :], w2[:, 0, f, a:b], gh[:, 0, f, h, :], start=x == 0, stop=x == 3)
            for x in range(4):
                f, h = divmod(x, 2)
                a, b = pads[h]
                r = mm(bank[:, 1, 0:32], w2[:, 0, f, a:b], ghp[:, 0, f, h * 32:(h + 1) * 32], start=x == 0, stop=x == 3)
            r.then_inc(S["ck_done"], 1)
            pe.wait_ge(S["gh_gelu"], 4)
            for t in range(4):
                for h in range(2):
                    for f in range(2):
                        mm(bank[:, 2, t * P + h * HD:t * P + (h + 1) * HD], gh[:, 1, f, h, t * P:(t + 1) * P],
                           w2[:, 1, f, HD:2 * HD], start=f == 0, stop=f == 1)
            pe.wait_ge(S["hrep_ready"], 1)
            for h in range(2):
                for f in range(2):
                    r = mm(bank[:, 3, h * HD:(h + 1) * HD], hrep[:, f, h, :, :].rearrange("p r c -> p (r c)"),
                           w2[:, 1, f, HD:2 * HD], start=f == 0, stop=f == 1)
            r.then_inc(S["ck_done"], 1)

            def scores(i):
                kind, qt, b, g = items[i]
                if kind == "out":
                    return
                if i >= 2 and items[i - 2][0] == "full":
                    pe.wait_ge(S["att_p"], n_full[i - 2])
                elif i >= 2 and items[i - 2][0] == "cmp":
                    pe.wait_ge(S["att_pc"], n_cmp[i - 2])
                s0 = 2 * (i % 2)
                q = slice(qt * P, (qt + 1) * P)
                for kv in range(NKV):
                    r0 = slice(HD * kv, HD * (kv + 1))
                    if kind == "cmp":
                        for gg in range(NG):
                            r = mm(bank[:, s0 + kv, gg * 32:gg * 32 + 32], qT[r0, gg, q], ckTp[r0, :], start=True, stop=True)
                    else:
                        r = mm(bank[:, s0 + kv, 0:(qt + 1) * P], qT[r0, g, q], kT[r0, b, 0:(qt + 1) * P],
                               start=True, stop=True)
                r.then_inc(S["att_s"], 1)

            def turn(i):
                kind, qt, b, g = items[i]
                if kind == "out":
                    pe.wait_ge(S["att_o"], n_v[i])
                elif kind == "full":
                    pe.wait_ge(S["att_p"], n_full[i])
                else:
                    pe.wait_ge(S["att_pc"], n_cmp[i])
                if i >= 1:
                    pe.wait_ge(S["att_ta"], i)
                    if n_full[i - 1]:
                        pe.wait_ge(S["att_td"], n_full[i - 1])
                if kind == "out":
                    for gg in range(NG):
                        r = pe.transpose(bank[:, 4, gg * P:(gg + 1) * P], OA[:, gg, :, :].rearrange("p v e -> p (v e)"),
                                         ident[:, :])
                elif kind == "cmp":
                    for kv in range(NKV):
                        r = pe.transpose(bank[:, 4, kv * P:(kv + 1) * P], PR[:, i % 2, 0, kv * P:(kv + 1) * P], ident[:, :])
                else:
                    for kv in range(NKV):
                        for t in range(qt + 1):
                            r = pe.transpose(bank[:, 4 + kv, t * P:(t + 1) * P], PR[:, i % 2, kv, t * P:(t + 1) * P],
                                             ident[:, :])
                r.then_inc(S["att_pa"], 1)

            def values(i):
                kind, qt, b, g = items[i]
                if kind == "out":
                    return
                pe.wait_ge(S["att_ta"], i + 1)
                if n_full[i]:
                    pe.wait_ge(S["att_td"], n_full[i])
                if n_v[i] >= 3:
                    pe.wait_ge(S["att_o"], n_v[i] - 2)
                o = 6 + n_v[i] % 2
                if kind == "cmp":
                    for kv in range(NKV):
                        r = mm(bank[:, o, kv * 256:(kv + 1) * 256], PT[:, i % 2, 0, kv * P:(kv + 1) * P],
                               cvp[:, kv, :, :].rearrange("p g e -> p (g e)"), start=True, stop=True)
                else:
                    for kv in range(NKV):
                        for t in range(qt + 1):
                            c = VC + b * P + kv * HD
                            r = mm(bank[:, o, kv * HD:(kv + 1) * HD], PT[:, i % 2, kv, t * P:(t + 1) * P],
                                   kvraw[:, t, c:c + HD], start=t == 0, stop=t == qt)
                r.then_inc(S["att_pv"], 1)

            pe.wait_ge(S["ck_copied"], 1)
            scores(0)
            for i in range(len(items)):
                if i + 1 < len(items):
                    scores(i + 1)
                if items[i][0] == "out":
                    values(i - 1)
                    turn(i)
                else:
                    turn(i)
                    if i >= 1:
                        values(i - 1)

            R = slice(0, NROW)
            pe.wait_ge(S["smp_dve"], 1)
            pe.wait_ge(S["att_ta"], len(items))
            mm(bank[R, 0, :], qbd[:, :], ckT[:, :], start=True, stop=True)
            for b in (0, 1):
                mm(bank[R, 1, b * NSA:(b + 1) * NSA], qbd[:, :], kT[:, 1 + b, NPR:NT], start=True, stop=True)
            for b in range(3):
                if b:
                    mm(bank[R, 1, 128 + b * P:128 + (b + 1) * P], emat[0:NSA, :], kvraw[0:NSA, QT_N, VC + b * P:VC + (b + 1) * P],
                       start=True, stop=True)
            mm(bank[R, 1, 32:32 + 24], emat[0:NSA, :], kvraw[0:NSA, QT_N, KVC:KVC + 24], start=True, stop=True)\
                .then_inc(S["smp_pe"], 1)
            pe.wait_ge(S["smp_dve"], 2)
            for t in range(4):
                pe.transpose(bank[:, 2, t * NROW:(t + 1) * NROW], sw[R, t * P:(t + 1) * P], ident[R, R])
            mm(bank[R, 3, 0:64], rmat[R, :], sw[R, 512:576], start=True, stop=True).then_inc(S["smp_pe"], 1)
            pe.wait_ge(S["smp_dve"], 3)
            for t in range(4):
                r = mm(bank[R, 4, 0:P], PT[:, 0, 0, t * NROW:(t + 1) * NROW], cv[:, t, :], start=t == 0, stop=t == 3)
            r.then_inc(S["smp_pe"], 1)
            kslc = chunk("kslc", 2)
            pe.wait_ge(S["kslc_in"], 16 * NPAGES)
            for h in range(2):
                for n in range(NSA):
                    r = mm(bank[R, 5 + h, :], qz[:, n * NROW:(n + 1) * NROW], kslc[:, n * PAST + h * 512:n * PAST + (h + 1) * 512],
                           start=n == 0, stop=n == NSA - 1)
            r.then_inc(S["smp_pe"], 1)
            pe.wait_ge(ring_in[slot_of["kwin"]], count_of["kwin"])
            kwin = chunk("kwin")
            for n in range(NSA):
                r = mm(bank[R, 7, :], qz[:, n * NROW:(n + 1) * NROW], kwin[:, n * WIN:(n + 1) * WIN],
                       start=n == 0, stop=n == NSA - 1)
            r.then_inc(S["smp_pe"], 1)
            vslc = chunk("vslc", 2).rearrange("p (g c) -> p g c", g=NPAGES)
            vwin = chunk("vwin").rearrange("p (g c) -> p g c", g=NSA * 4)
            for b, (tiles, vals, dve_at) in enumerate(((NPG, vslc, 4), (4, vwin, 6))):
                pe.wait_ge(S["smp_act"], 2 + b)
                if b:
                    pe.wait_ge(S["smp_dve"], 6)
                for t in range(tiles):
                    r = pe.transpose(bank[:, 2, t * NROW:(t + 1) * NROW], sw[R, t * P:(t + 1) * P], ident[R, R])
                r.then_inc(S["smp_pe"], 1)
                pe.wait_ge(S["smp_dve"], 5 + 2 * b)
                if b == 0:
                    pe.wait_ge(S["vslc_in"], 16 * NPAGES)
                else:
                    pe.wait_ge(S["vwin_in"], 16 * NSA)
                for n in range(NSA):
                    for t in range(tiles):
                        r = mm(bank[R, 3 + n // 4, (n % 4) * P:(n % 4 + 1) * P], PT[:, 0, 0:2, :].rearrange("p a k -> p (a k)")[:, t * NROW:(t + 1) * NROW],
                               vals[:, n * tiles + t, :], start=t == 0, stop=t == tiles - 1)
                r.then_inc(S["smp_pe"], 1)
            pe.wait_ge(S["smp_dve"], 8)
            pe.transpose(bank[0:HD, 0, 0:NROW], oS[R, :], ident[R, R]).then_inc(S["smp_pe"], 1)

            pe.wait_ge(S["smp_dve"], 9)
            for m in range(KD):
                c = slice((m % 4) * P, (m % 4 + 1) * P)
                for x, (name, done, ks) in enumerate((("ga", "ga_done", KD), ("pa", "pa_done", KD),
                                                      ("gb", "gb_done", KD), ("pb", "pb_done", NG))):
                    name += str(m // 4)
                    if m % 4 == 0:
                        pe.wait_ge(ring_in[slot_of[name]], count_of[name])
                    if m >= 1:
                        if x % 2 == 0:
                            pe.wait_ge(S["sg_ready"], 2 * m - 1 + x // 2)
                        else:
                            pe.wait_ge(S["m_ready"], m)
                    w = chunk(name)[:, 0:ks * 512].rearrange("p (k n) -> p k n", k=ks)
                    src = {"pa": Y, "pb": oT}.get(name[:2], xn)
                    for k in range(ks):
                        r = two_halves(x, w[:, k, c], src[:, k, :], k == 0, k == ks - 1)
                    r.then_inc(S[done], 1)

            def out_rows(t):
                if t >= 2:
                    pe.wait_ge(S["xm_ready"], t - 1)
                for h in range(2):
                    w = w8(f"wo{h}")
                    if t == 0:
                        pe.wait_ge(ring_in[slot_of[f"wo{h}"]], count_of[f"wo{h}"])
                    for k in range(KD):
                        r = mm(bank[0:RN, 6 * (t % 2) + h, :], mT[:, k, t * RN:(t + 1) * RN], w[:, k, :],
                               start=k == 0, stop=k == KD - 1)
                r.then_inc(S["wo_done"], 1)

            def places(t):
                pe.wait_ge(S["m4_ready"], t + 1)
                if t == RT - 1:
                    pe.wait_ge(S["ent_ready"], t)
                for u in range(t + 1):
                    lhs = tri if u == t else onesm[:, 0:RN]
                    r = mm(bank[0:RN, 5, P:P + NE], lhs[0:RN, :], m4[0:RN, u, :], start=u == 0, stop=u == t)
                if t == RT - 1:
                    for u in range(RT):
                        r = mm(bank[0:RN, 5, P + NE:P + 2 * NE], onesm[0:RN, 0:RN], m4[0:RN, u, :],
                               start=u == 0, stop=u == RT - 1)
                r.then_inc(S["pos_done"], 1)

            def route_rows(t):
                pe.wait_ge(S["t_ready"], t + 1)
                if t >= 2:
                    pe.wait_ge(S["y0_ready"], t - 1)
                for k in range(KD):
                    r = pe.transpose(bank[:, 2 + k // 4, (k % 4) * P:(k % 4) * P + RN], tn[0:RN, t % 2, k * P:(k + 1) * P],
                                     ident[0:RN, 0:RN])
                r.then_inc(S["t_turned"], 1)
                pe.wait_ge(S["t_copied"], t + 1)
                if t >= 1:
                    pe.wait_ge(S["m4_ready"], t)
                for k in range(KD):
                    r = mm(bank[0:RN, 4, t * NE:(t + 1) * NE], tT[:, k, 0:RN], rwt[:, k, :], start=k == 0, stop=k == KD - 1)
                r.then_inc(S["lg_done"], 1)

            def down_biases(t):
                pe.wait_ge(S["gd_ready"], t + 1)
                pe.wait_ge(S["ent_ready"], t + 1)
                if t == RT - 1:
                    pe.wait_ge(S["ovf_ready"], 1)
                pe.transpose(bank[0:NE, 5, 0:RN], gd[0:RN, :], ident[0:RN, 0:RN]).then_inc(S["gd_turned"], 1)
                pe.wait_ge(S["gd_copied"], t + 1)
                if t == RT - 1:
                    pe.wait_ge(S["y0_ready"], t)
                for h in range(2):
                    r = mm(bank[0:RN, 2 + h, :], gdT[0:NE, 0:RN], bdn[:, h * 512:(h + 1) * 512], start=True, stop=True)
                r.then_inc(S["bd_done"], 1)

            pe.wait_ge(S["m_ready"], KD)
            for t in range(RT + 2):
                if t < RT:
                    out_rows(t)
                if t == 1:
                    pe.wait_ge(S["router_in"], ROUTER_IN)
                if t >= 2:
                    places(t - 2)
                if 1 <= t <= RT:
                    route_rows(t - 1)
                if t >= 2:
                    down_biases(t - 2)

            def turn_rows(n, par):
                pe.wait_ge(S["xg_in"], 16 * n + 16)
                pe.wait_ge(S["xt_ready"], n + 1)
                for k in range(KD):
                    r = pe.transpose(bank[:, 6 + k // 4, (k % 4) * P:(k % 4 + 1) * P], GX[par][:, k * P:(k + 1) * P], ident[:, :])
                r.then_inc(S["x_turned"], 1)

            def block_of(n, par, following):
                for c in range(4):
                    pe.wait_ge(ring_in[eslot[c]], 16 * n + 16 + ebase[c])
                    if c == 0:
                        pe.wait_ge(S["xt_ready"], n + 2)
                    pe.wait_ge(S["up_read"], 4 * n + c + 1)
                    w = ring[:, eslot[c] * SLOT:(eslot[c] + 1) * SLOT].rearrange("p (k n) -> p k n", k=KD)
                    for f in range(4):
                        for k in range(KD):
                            r = mm(bank[:, c, f * P:(f + 1) * P], w[:, k, f * P:(f + 1) * P], XT[par][:, k, :],
                                   start=k == 0, stop=k == KD - 1)
                    r.then_inc(S["ring_used"], 1)
                for c in (4, 5):
                    pe.wait_ge(ring_in[eslot[c]], 16 * n + 16 + ebase[c])
                    pe.wait_ge(S["h_ready"], 2 * n + c - 3)
                    if c == 4:
                        pe.wait_ge(S["y_scaled"], n + 1)
                    elif following:
                        turn_rows(n + 1, 1 - par)
                    w = ring[:, eslot[c] * SLOT:(eslot[c] + 1) * SLOT].rearrange("p (f n) -> p f n", f=4)
                    for f in range(4):
                        for h in range(2):
                            r = mm(bank[:, 4 + h, :], HT[par][:, 4 * (c - 4) + f, :], w[:, f, h * 512:(h + 1) * 512],
                                   start=c == 4 and f == 0, stop=c == 5 and f == 3)
                    r.then_inc(S["ring_used"], 1)

            pe.wait_ge(S["xm_ready"], RT)
            turn_rows(0, 0)
            pe.wait_ge(S["y0_ready"], RT)
            with pe.Fori(0, NE // 2 - 1) as pair:
                block_of(2 * pair, 0, True)
                block_of(2 * pair + 1, 1, True)
            block_of(NE - 2, 0, True)
            block_of(NE - 1, 1, False)
            pe.wait_ge(S["ovf_ready"], 1)
            most = pe.value_load(ovf[0:1, 1:2].bitcast(I32), min_val=0, max_val=NT)
            with pe.If(most > P):
                with pe.Fori(0, NE) as e:
                    for b in range(4):
                        turn_rows(4 * e + (NE + b), b % 2)
                        block_of(4 * e + (NE + b), b % 2, False)

        @block.scalar
        def _(act):
            fn = act.activation
            mine = Steps(act, S["act_steps"])
            act.wait_ge(S["small_in"], SMALL_IN)
            act.wait_ge(S["lam_ready"], 1)
            fn(lt[:, 1, :], lt[:, 0, :], ACT.Exp, scale=-1.0).then_inc(S["lam_exp"], 1)
            act.wait_ge(S["x_in"], 16)
            for k in range(KD):
                fn(xsq[:, k, :], xn[:, k, :], ACT.Square).then_inc(S["x_squared"], 1)
            act.wait_ge(S["x_summed"], 1)
            fn(split(rstd), halves(3), ACT.Sqrt, scale=1.0 / D, bias=eps1[:, 0:1]).then_inc(S["x_root"], 1)
            for t in range(TT):
                m = fraction(t)
                b = 3 * (t % 2)
                act.wait_ge(S["tok_done"], t + 1)
                fn(qraw[0:m, t, :], bank[0:m, b, :], ACT.Copy)
                fn(kvraw[0:m, t, 0:512], bank[0:m, b + 1, :], ACT.Copy)
                fn(kvraw[0:m, t, 512:792], bank[0:m, b + 2, 0:280], ACT.Copy).then_inc(S["tok_copied"], 1)
                act.wait_ge(S["ss_ready"], t + 1)
                fn(rsq[0:m, t, :], ssq[0:m, t, :], ACT.Sqrt, scale=1.0 / HD, bias=eps1[0:m, 0:1]).then_inc(S["rs_root"], 1)
            act.wait_ge(S["qk_turned"], 1)
            for g in range(NG):
                fn(qT[:, g, 0:NPR], bank[:, g, :], ACT.Copy)
            fn(qT[:, :, NPR:NT], bank[:, 7, 0:NG * NSA].rearrange("p (g n) -> p g n", g=NG), ACT.Copy)\
                .then_inc(S["qk_act"], 1)

            def gates_of(m):
                j = m % 4
                act.wait_ge(S["r_done"], m + 1)
                if m >= 4:
                    act.wait_ge(S["y_ready"], j + 1)
                fn(split(A[:, j, :]), halves(2), ACT.Tanh, scale=0.5, bias=hb[:, 0, m:m + 1]).then_inc(S["th_ready"], 1)
                act.wait_ge(S["i_done"], m + 1)
                fn(split(IX[:, j, :]), halves(3), ACT.Tanh, scale=0.5, bias=hb[:, 1, m:m + 1]).then_inc(S["ti_ready"], 1)

            def decays(g):
                act.wait_ge(S["th_ready"], 4 * g + 4)
                for j in range(4):
                    m = 4 * g + j
                    mine(fn(V[:, j, :], A[:, j, :], ACT.Tanh, scale=c2[:, 1, m:m + 1], bias=c2[:, 1, m:m + 1]))
                for j in range(4):
                    m = 4 * g + j
                    mine.settle()
                    fn(A[:, j, :], A[:, j, :], ACT.Exp, scale=c2[:, 0, m:m + 1], bias=c2[:, 0, m:m + 1])\
                        .then_inc(S["decay_ready"], 1)
                for j in range(4):
                    act.wait_ge(S["gap_ready"], 4 * g + j + 1)
                    fn(V[:, j, :], V[:, j, :], ACT.Sqrt, scale=0.25).then_inc(S["gap_root"], 1)

            act.wait_ge(S["lam_ready"], 2)
            for m in range(KD):
                act.wait_ge(S["ar_done"], m + 1)
                if m >= 2:
                    act.wait_ge(S["xc_ready"], m - 1)
                elif m == 0:
                    act.wait_ge(S["qk_turned"], 1)
                fn(xpp[:, m % 2, 3:3 + HN], bank[:, 0, 0:HN], ACT.Copy)
                fn(xpp[:, m % 2, 3 + HN:3 + NPR], bank[:, 1, 0:NPR - HN], ACT.Copy)
                fn(xps[:, m, :, 3], bank[:, 1, NPR - HN:HN], ACT.Copy).then_inc(S["ar_copied"], 1)
                act.wait_ge(S["ag_done"], m + 1)
                fn(split(Y[:, m, :]), halves(1), ACT.Gelu_apprx_tanh).then_inc(S["ag_gelu"], 1)
                if m >= 1:
                    gates_of(m - 1)
                if m == 4:
                    decays(0)
            gates_of(KD - 1)
            decays(1)

            def part_copies(v):
                for u in range(4 * v, 4 * v + 4):
                    act.wait_ge(S["cs_done"], u + 1)
                    if u >= 2:
                        act.wait_ge(S["gh_raw"], u - 1)
                    else:
                        act.wait_ge(S["y_ready"], KD)
                    fn(p1c[:, u % 2, :], bank[:, 2 * (u % 3) + 1, :], ACT.Copy).then_inc(S["p1_copied"], 1)

            def prompt_parts(v):
                for f in range(2):
                    act.wait_ge(S["cp_done"], 2 * v + f + 1)
                    act.wait_ge(S["gh_raw"], 4 * v + 4)
                    if v or f:
                        act.wait_ge(S["ghp_raw"], 2 * v + f)
                    fn(p1c[:, 0, 0:66], bank[:, 6, 66:132], ACT.Copy).then_inc(S["pp_copied"], 1)

            def gelus(v):
                act.wait_ge(S["ghp_raw"], 2 * v + 2)
                for f in range(2):
                    bias = cbias[:, 2 * v + f:2 * v + f + 1]
                    fn(ghp[:, v, f, :], ghp[:, v, f, :], ACT.Gelu_apprx_tanh, bias=bias)
                    x = gh[:, v, f, :, :]
                    fn(x, x, ACT.Gelu_apprx_tanh, bias=bias).then_inc(S["gh_gelu"], 1)

            part_copies(0)
            prompt_parts(0)
            gelus(0)
            part_copies(1)
            prompt_parts(1)
            gelus(1)
            for t in range(TT):
                m = fraction(t)
                r = fn(kvraw[0:m, t, KVC:KVC + 24], kvraw[0:m, t, KVC:KVC + 24], ACT.Tanh, scale=0.5)
            r.then_inc(S["gates_t"], 1)

            def exponentials(i):
                kind, qt, b, g = items[i]
                if kind == "out":
                    return
                if i >= 2:
                    act.wait_ge(S["att_pa"], i - 1)
                if kind == "cmp":
                    act.wait_ge(S["att_ce"], n_cmp[i])
                    fn(PR[:, i % 2, 0, 0:256], PR[:, i % 2, 0, 0:256], ACT.Exp, scale=SCALE).then_inc(S["att_cs"], 1)
                    return
                act.wait_ge(S["att_max"], n_full[i])
                n = (qt + 1) * P
                for kv in range(NKV):
                    r = fn(PR[:, i % 2, kv, 0:n], bank[:, 2 * (i % 2) + kv, 0:n], ACT.Exp, scale=SCALE,
                           bias=stat[:, 4 * (i % 2) + kv:4 * (i % 2) + kv + 1],
                           accum_out=stat[:, 4 * (i % 2) + 2 + kv:4 * (i % 2) + 3 + kv])
                r.then_inc(S["att_p"], 1)

            def turned(i):
                kind, qt, b, g = items[i]
                act.wait_ge(S["att_pa"], i + 1)
                if kind == "out":
                    fn(oT[:, :, qt * P:(qt + 1) * P], bank[:, 4, :].rearrange("p (g t) -> p g t", g=NG), ACT.Copy)\
                        .then_inc(S["att_ta"], 1)
                    return
                if i >= 2:
                    act.wait_ge(S["att_pv"], n_v[i - 2])
                n = 256 if kind == "cmp" else (qt + 1) * P
                fn(PT[:, i % 2, 0, 0:n], bank[:, 4, 0:n], ACT.Copy).then_inc(S["att_ta"], 1)

            act.wait_ge(S["ck_copied"], 1)
            exponentials(0)
            for i in range(len(items)):
                if i + 1 < len(items):
                    exponentials(i + 1)
                turned(i)

            R = slice(0, NROW)
            act.wait_ge(S["smp_max"], 1)
            fn(sw[R, 0:512], sw[R, 0:512], ACT.Exp, scale=SCALE, bias=stat[R, 8:9], accum_out=stat[R, 9:10])\
                .then_inc(S["smp_act"], 1)
            for b in (1, 2):
                act.wait_ge(S["smp_max"], 1 + b)
                fn(stat[R, 12:13], stat[R, 11:12], ACT.Exp, scale=SCALE, bias=stat[R, 8:9])
                if b == 1:
                    src, out = sw[R, :], sw[R, :]
                else:
                    src, out = bank[R, 7, 1:WIN], sw[R, 1:WIN]
                    act.wait_ge(S["smp_pe"], 6)
                fn(out, src, ACT.Exp, scale=SCALE, bias=stat[R, 8:9], accum_out=stat[R, 9:10]).then_inc(S["smp_act"], 1)

            for m in range(KD):
                for x, done in ((0, "ga_done"), (1, "gb_done")):
                    act.wait_ge(S[done], m + 1)
                    if m >= 1:
                        act.wait_ge(S["m_ready"], m)
                    fn(split(sg[:, x, :]), halves(2 * x), ACT.Tanh, scale=0.5).then_inc(S["sg_ready"], 1)
            for t in range(RT + 2):
                if 1 <= t <= RT:
                    act.wait_ge(S["t_turned"], t)
                    if t >= 2:
                        act.wait_ge(S["lg_done"], t - 1)
                    fn(tT[:, :, 0:RN], bank[:, 2:4, :].rearrange("p b (k t) -> p (b k) t", k=4)[:, :, 0:RN], ACT.Copy)\
                        .then_inc(S["t_copied"], 1)
                if t < RT:
                    act.wait_ge(S["xm_ready"], t + 1)
                    fn(sq_rows[0:RN, :], xm[0:RN, t % 3, :], ACT.Square, accum_out=stat[0:RN, 0:1]).then_inc(S["ss2"], 1)
                    act.wait_ge(S["ss2"], t + 1)
                    fn(stat[0:RN, 1:2], stat[0:RN, 0:1], ACT.Sqrt, scale=1.0 / D, bias=eps1[0:RN, 0:1]).then_inc(S["rstd2"], 1)
                if t >= 2:
                    act.wait_ge(S["gd_turned"], t - 1)
                    if t >= 3:
                        act.wait_ge(S["bd_done"], t - 2)
                    fn(gdT[0:NE, 0:RN], bank[0:NE, 5, 0:RN], ACT.Copy).then_inc(S["gd_copied"], 1)
                if 1 <= t <= RT:
                    act.wait_ge(S["ex_in"], t)
                    x = ixf[0:RN, t - 1, :]
                    fn(x, x, ACT.Exp, bias=stat[0:RN, 2:3], accum_out=stat[0:RN, 3:4]).then_inc(S["ex_done"], 1)

            act.sem_inc(S["xt_ready"], 1)
            act.sem_inc(S["y_scaled"], 1)

            def turned_rows(n, par):
                act.wait_ge(S["x_turned"], n + 1)
                fn(XT[par][:, :, :], bank[:, 6:8, :].rearrange("p b (k t) -> p (b k) t", k=4), ACT.Copy)\
                    .then_inc(S["xt_ready"], 1)

            def block_of(n, par, following):
                for hf in range(2):
                    act.wait_ge(S["up_read"], 4 * n + 2 * hf + 5)
                    fn(SG[hf], AA[hf], ACT.Sigmoid, scale=ALPHA).then_inc(S["sig_ready"], 1)
                if following:
                    turned_rows(n + 1, 1 - par)
                act.wait_ge(S["ring_used"], 6 * n + 6)
                fn(YR[par].rearrange("p (b n) -> p b n", b=2), bank[:, 4:6, :], ACT.Copy, scale=entf[par][:, 1:2])\
                    .then_inc(S["y_scaled"], 1)

            turned_rows(0, 0)
            with act.Fori(0, NE // 2 - 1) as pair:
                block_of(2 * pair, 0, True)
                block_of(2 * pair + 1, 1, True)
            block_of(NE - 2, 0, True)
            block_of(NE - 1, 1, False)
            act.wait_ge(S["ovf_ready"], 1)
            most = act.value_load(ovf[0:1, 1:2].bitcast(I32), min_val=0, max_val=NT)
            with act.If(most > P):
                with act.Fori(0, NE) as e:
                    for b in range(4):
                        turned_rows(4 * e + (NE + b), b % 2)
                        block_of(4 * e + (NE + b), b % 2, False)

        @block.vector
        def _(dve):
            v = nc.vector
            mine = Steps(dve, S["dve_steps"])

            def one(ins, sem=None):
                mine(ins, sem)
                mine.settle()

            one(v.memset(eps1[:, :], EPS))
            dve.wait_ge(S["small_in"], SMALL_IN)
            one(v.tensor_scalar(lt[:, 0, :], lruv[:, :, 7], -1.0, None, ALU.mult))
            one(v.tensor_tensor(lt[:, 0, :], lt[:, 0, :], lruv[:, :, 7], ALU.max))
            v.tensor_scalar(negc[:, :, :], cmask[:, :, :], 1.0, -NEG, ALU.subtract, ALU.mult).then_inc(S["lam_ready"], 1)
            dve.wait_ge(S["lam_exp"], 1)
            one(v.tensor_scalar(lt[:, 2, :], lt[:, 1, :], 2.0, None, ALU.add))
            one(v.reciprocal(lt[:, 2, :], lt[:, 2, :]))
            one(v.tensor_tensor(lt[:, 1, :], lt[:, 1, :], lt[:, 2, :], ALU.mult))
            one(v.tensor_tensor(lt[:, 2, :], lt[:, 1, :], lt[:, 1, :], ALU.mult))
            one(v.memset(lt[:, 3, :], 1.0 / 17))
            for k in range(15, 0, -2):
                one(v.tensor_tensor(lt[:, 3, :], lt[:, 3, :], lt[:, 2, :], ALU.mult))
                one(v.tensor_scalar(lt[:, 3, :], lt[:, 3, :], 1.0 / k, None, ALU.add))
            one(v.tensor_tensor(lt[:, 1, :], lt[:, 1, :], lt[:, 3, :], ALU.mult))
            one(v.tensor_scalar(lt[:, 2, :], lruv[:, :, 7], -1.0, 0.0, ALU.mult, ALU.max))
            one(v.scalar_tensor_tensor(lt[:, 1, :], lt[:, 1, :], 2.0, lt[:, 2, :], ALU.mult, ALU.add))
            one(v.tensor_scalar(c2[:, 0, :], lt[:, 1, :], -4.0, None, ALU.mult))
            one(v.tensor_scalar(c2[:, 1, :], lt[:, 1, :], 4.0, None, ALU.mult))
            v.tensor_scalar(hb[:, :, :], lruv[:, :, 5:7].rearrange("p m x -> p x m"), 0.5, None, ALU.mult)\
                .then_inc(S["lam_ready"], 1)
            dve.wait_ge(S["x_root"], 1)
            one(v.reciprocal(rstd, rstd))
            for k in range(KD):
                v.scalar_tensor_tensor(xn[:, k, :], xn[:, k, :], gmix[:, k:k + 1], rstd, ALU.mult, ALU.mult)\
                    .then_inc(S["xn_ready"], 1)
            dve.wait_ge(S["xn_ready"], KD)
            one(v.memset(ssq[:, 0, 0:1], 0.0), S["rms_free"])
            dve.wait_ge(S["gains_in"], 16)
            for t in range(TT):
                m = fraction(t)
                dve.wait_ge(S["tok_copied"], t + 1)
                q = qraw[0:m, t, :].rearrange("p (h c) -> p h c", h=NH)
                kk = kvraw[0:m, t, 0:6 * HD].rearrange("p (h c) -> p h c", h=6)
                mine(v.tensor_tensor(sqt[0:m, 0:NH, :], q, q, ALU.mult))
                one(v.tensor_tensor(sqt[0:m, NH:NHN, :], kk, kk, ALU.mult))
                one(v.tensor_reduce(ssq[0:m, t, :], sqt[0:m, :, :], AX, ALU.add), S["ss_ready"])
                dve.wait_ge(S["rs_root"], t + 1)
                one(v.reciprocal(rsq[0:m, t, :], rsq[0:m, t, :]))
                for x, h0_, h1_ in ((q, 0, NH), (kk, NH, NHN)):
                    nh = h1_ - h0_
                    r = rsq[0:m, t, h0_:h1_].rearrange("p (h o) -> p h o", o=1).to_broadcast([m, nh, HD])
                    one(v.tensor_tensor(x, x, r, ALU.mult))
                    one(v.tensor_tensor(x, x, gain[0:m, h0_:h1_, :], ALU.mult))
                    cos = rope[0:m, t, 0:8].rearrange("p (o c) -> p o c", o=1).to_broadcast([m, nh, 8])
                    sin = rope[0:m, t, 8:16].rearrange("p (o c) -> p o c", o=1).to_broadcast([m, nh, 8])
                    x1, x2 = x[:, :, 0:8], x[:, :, 8:16]
                    tmp = [sqt[0:m, 0:nh, 8 * i:8 * i + 8] for i in range(4)]
                    mine(v.tensor_tensor(tmp[0], x1, cos, ALU.mult))
                    mine(v.tensor_tensor(tmp[1], x2, sin, ALU.mult))
                    mine(v.tensor_tensor(tmp[2], x1, sin, ALU.mult))
                    one(v.tensor_tensor(tmp[3], x2, cos, ALU.mult))
                    mine(v.tensor_tensor(x1, tmp[0], tmp[1], ALU.subtract))
                    one(v.tensor_tensor(x2, tmp[2], tmp[3], ALU.add), S["qk_ready"] if nh == 6 else None)
            dve.wait_ge(S["qk_turned"], 1)
            for b in range(3):
                v.tensor_copy(kT[:, b, 0:NPR], bank[:, NG + b, :])
            dve.wait_ge(S["qk_act"], 1)
            v.tensor_copy(kT[:, :, NPR:NT], bank[:, 7, NG * NSA:7 * NSA].rearrange("p (b n) -> p b n", b=3))\
                .then_inc(S["qk_dve"], 1)

            def convolve(m):
                b = m % 2
                dve.wait_ge(S["ar_copied"], m + 1)
                if m >= 2:
                    dve.wait_ge(S["i_done"], m - 1)
                w = [lruv[:, m, k:k + 1] for k in range(8)]
                mine(v.tensor_copy(pconv[:, m, :], xpp[:, b, NPR:NPR + 3]))
                mine(v.tensor_scalar(xc[:, b, 0:NPR], xpp[:, b, 0:NPR], w[0], w[4], ALU.mult, ALU.add))
                one(v.tensor_scalar(xc[:, b, NPR:NT], xps[:, m, :, 0], w[0], w[4], ALU.mult, ALU.add))
                for k in range(1, 4):
                    mine(v.scalar_tensor_tensor(xc[:, b, 0:NPR], xpp[:, b, k:k + NPR], w[k], xc[:, b, 0:NPR], ALU.mult, ALU.add))
                    one(v.scalar_tensor_tensor(xc[:, b, NPR:NT], xps[:, m, :, k], w[k], xc[:, b, NPR:NT], ALU.mult, ALU.add),
                        S["xc_ready"] if k == 3 else None)

            def gated_input(m):
                dve.wait_ge(S["ti_ready"], m + 1)
                x = IX[:, m % 4, :]
                one(v.scalar_tensor_tensor(x, x, 1.0, xc[:, m % 2, :], ALU.add, ALU.mult))

            def recur(g):
                tmp = qf[:, 2070:2070 + HN]
                for j in range(4):
                    dve.wait_ge(S["decay_ready"], 4 * g + j + 1)
                    for h in range(2):
                        c = slice(h * HN, (h + 1) * HN)
                        one(v.tensor_tensor(tmp, A[:, j, c], A[:, j, c], ALU.mult))
                        one(v.scalar_tensor_tensor(V[:, j, c], tmp, 1.0, V[:, j, c], ALU.add, ALU.mult),
                            S["gap_ready"] if h else None)
                for j in range(4):
                    m = 4 * g + j
                    dve.wait_ge(S["gap_root"], m + 1)
                    one(v.tensor_tensor(IX[:, j, :], IX[:, j, :], V[:, j, :], ALU.mult))
                    one(v.tensor_tensor(h0[:, m, :], h0[:, m, :], A[:, j, NPR:NT], ALU.mult))
                    one(v.tensor_tensor(IX[:, j, NPR:NT], IX[:, j, NPR:NT], h0[:, m, :], ALU.add))
                    one(v.tensor_tensor_scan(V[:, j, 0:NPR], A[:, j, 0:NPR], IX[:, j, 0:NPR], 0.0, ALU.mult, ALU.add))
                    mine(v.tensor_copy(hout[:, m, 0:1], V[:, j, NPR - 1:NPR]))
                    mine(v.tensor_copy(hout[:, m, 1:9], IX[:, j, NPR:NT]))
                    mine(v.tensor_tensor(Y[:, m, 0:NPR], Y[:, m, 0:NPR], V[:, j, 0:NPR], ALU.mult))
                    one(v.tensor_tensor(Y[:, m, NPR:NT], Y[:, m, NPR:NT], IX[:, j, NPR:NT], ALU.mult), S["y_ready"])

            for b in range(2):
                one(v.memset(xpp[:, b, 0:3], 0.0))
            for m in range(KD):
                convolve(m)
                if m >= 1:
                    gated_input(m - 1)
                if m == 4:
                    recur(0)
            gated_input(KD - 1)
            one(v.tensor_copy(lt[:, 0, 0:1], eps1[:, :]))
            recur(1)
            one(v.tensor_copy(lt[:, 0, 0:1], eps1[:, :]), S["rec_free"])

            def prompt_rows(vv):
                src = kT[:, 0, 0:NPR] if vv == 0 else bank[:, 7, :]
                src = src.rearrange("p (c l two) -> p two l c", c=NCH, l=LP)
                for kv in range(2):
                    for l2 in range(2):
                        mine(v.tensor_copy(xp[l2 * HD:(l2 + 1) * HD, vv, :, kv * NCH:(kv + 1) * NCH],
                                           src[kv * HD:(kv + 1) * HD, l2, :, :]))
                one(v.tensor_copy(xp[:, vv, :, 64:66], posc[:, vv, :, :]), S["xp_ready"])

            dve.wait_ge(S["i_done"], KD)
            prompt_rows(0)
            dve.wait_ge(S["vt_done"], 1)
            prompt_rows(1)
            for vv in range(2):
                for u in range(4 * vv, 4 * vv + 4):
                    f, h = divmod(u % 4, 2)
                    dve.wait_ge(S["p1_copied"], u + 1)
                    out = gh[:, vv, f, h, :].rearrange("p (n c) -> p n c", n=NSA)
                    p0 = bank[:, 2 * (u % 3), :].rearrange("p (n c) -> p n c", n=NSA)
                    p1 = p1c[:, u % 2, :].rearrange("p (n c) -> p n c", n=NSA)
                    mine(v.memset(out[:, :, CHS - 1:CHS], 0.0))
                    one(v.tensor_tensor(out[:, :, 0:CHS - 1], p0[:, :, 0:CHS - 1], p1[:, :, 1:CHS], ALU.add), S["gh_raw"])
                for f in range(2):
                    dve.wait_ge(S["pp_copied"], 2 * vv + f + 1)
                    out = ghp[:, vv, f, :].rearrange("p (v c) -> p v c", v=2)
                    p0 = bank[:, 6, 0:64].rearrange("p (v c) -> p v c", v=2)
                    p1 = p1c[:, 0, 0:64].rearrange("p (v c) -> p v c", v=2)
                    mine(v.memset(out[:, :, NCH - 1:NCH], 0.0))
                    mine(v.tensor_tensor(out[:, :, 0:NCH - 1], p0[:, :, 0:NCH - 1], p1[:, :, 1:NCH], ALU.add))
                    x = cbias[:, 2 * vv + f:2 * vv + f + 1]
                    one(v.tensor_tensor(x, bank[:, 6, 64:65], p1c[:, 0, 65:66], ALU.add), S["ghp_raw"])
            dve.wait_ge(S["gh_gelu"], 4)
            for f in range(2):
                for h in range(2):
                    src = ghp[:, 1, f, h * 32:(h + 1) * 32].rearrange("p (o c) -> p o c", o=1).to_broadcast([P, 4, 32])
                    mine(v.tensor_copy(hrep[:, f, h, :, :], src))
            one(v.memset(cvp[:, :, :, :], 0.0), S["hrep_ready"])
            dve.wait_ge(S["ck_done"], 2)
            mine(v.tensor_copy(ckT[:, :], bank[:, 0, :]))
            mine(v.tensor_copy(ckTp[:, :], bank[:, 1, 0:32]))
            mine(v.tensor_copy(cv[:, :, :], bank[:, 2, :].rearrange("p (t c) -> p t c", t=4)))
            for h in range(2):
                for g in range(NG):
                    r = v.tensor_copy(cvp[32 * g:32 * g + 32, h, g, :], bank[32 * g:32 * g + 32, 3, h * HD:(h + 1) * HD])
                    one(r, S["ck_copied"] if h == 1 and g == NG - 1 else None)
            dve.wait_ge(S["gates_t"], 1)
            for t in range(TT):
                m = fraction(t)
                x = kvraw[0:m, t, KVC:KVC + 24]
                one(v.tensor_scalar(x, x, 0.5, 0.5, ALU.mult, ALU.add))

            def maxima(i):
                kind, qt, b, g = items[i]
                if kind == "out":
                    return
                dve.wait_ge(S["att_s"], n_v[i])
                if kind == "cmp":
                    if i >= 2:
                        dve.wait_ge(S["att_pa"], i - 1)
                    x = PR[:, i % 2, 0, 0:256].rearrange("p (h c) -> p h c", h=NH)
                    vis = negc[:, qt, :].rearrange("p (o c) -> p o c", o=1).to_broadcast([P, NG, 32])
                    for kv in range(NKV):
                        s = bank[:, 2 * (i % 2) + kv, 0:P].rearrange("p (h c) -> p h c", h=NG)
                        one(v.tensor_tensor(x[:, kv * NG:(kv + 1) * NG, :], s, vis, ALU.add))
                    one(v.tensor_reduce(stat[:, 16:24], x, AX, ALU.max))
                    mx = stat[:, 16:24].rearrange("p (h o) -> p h o", o=1).to_broadcast([P, NH, 32])
                    one(v.tensor_tensor(x, x, mx, ALU.subtract), S["att_ce"])
                    return
                s = bank[:, 2 * (i % 2):2 * (i % 2) + 2, :]
                diag = s[:, :, qt * P:(qt + 1) * P]
                one(v.tensor_tensor(diag, diag, causal.rearrange("p (o c) -> p o c", o=1).to_broadcast([P, 2, P]), ALU.add))
                st = 4 * (i % 2)
                one(v.tensor_reduce(stat[:, 24:26], s[:, :, 0:(qt + 1) * P], AX, ALU.max))
                if i >= 2 and items[i - 2][0] == "full":
                    dve.wait_ge(S["att_p"], n_full[i - 2])
                one(v.tensor_scalar(stat[:, st:st + 2], stat[:, 24:26], -SCALE, None, ALU.mult), S["att_max"])

            def weights(i):
                kind, qt, b, g = items[i]
                if kind == "cmp":
                    dve.wait_ge(S["att_cs"], n_cmp[i])
                    x = PR[:, i % 2, 0, 0:256].rearrange("p (h c) -> p h c", h=NH)
                    one(v.tensor_tensor(x, x, cmask[:, qt, :].rearrange("p (o c) -> p o c", o=1).to_broadcast([P, NH, 32]), ALU.mult))
                    one(v.tensor_reduce(stat[:, 16:24], x, AX, ALU.add))
                    one(v.tensor_scalar(stat[:, 16:24], stat[:, 16:24], 1e-30, None, ALU.max))
                    one(v.reciprocal(stat[:, 16:24], stat[:, 16:24]))
                    gt = kvraw[:, qt, KVC:KVC + NH].rearrange("p (g v) -> p v g", g=NG)
                    w = stat[:, 16:24].rearrange("p (v g) -> p v g", v=NKV)
                    one(v.tensor_tensor(w, w, gt, ALU.mult))
                    one(v.tensor_tensor(x, x, stat[:, 16:24].rearrange("p (h o) -> p h o", o=1).to_broadcast([P, NH, 32]), ALU.mult),
                        S["att_pc"])
                elif kind == "full":
                    st = 4 * (i % 2)
                    dve.wait_ge(S["att_pa"], i + 1)
                    if i >= 2:
                        dve.wait_ge(S["att_pv"], n_v[i - 2])
                    n = (qt + 1) * P
                    v.tensor_copy(PT[:, i % 2, 1, 0:n], bank[:, 5, 0:n]).then_inc(S["att_td"], 1)
                    one(v.reciprocal(stat[:, 26 + 2 * (i % 2):28 + 2 * (i % 2)], stat[:, st + 2:st + 4]))
                    c = KVC + b * NH + g * NKV
                    w = stat[:, 26 + 2 * (i % 2):28 + 2 * (i % 2)]
                    one(v.tensor_tensor(w, w, kvraw[:, qt, c:c + NKV], ALU.mult))

            def outputs(i):
                kind, qt, b, g = items[i]
                if kind == "out":
                    return
                dve.wait_ge(S["att_pv"], n_v[i])
                o = 6 + n_v[i] % 2
                if kind == "cmp":
                    if i:
                        dve.wait_ge(S["att_pa"], i)
                    one(v.tensor_copy(OA[:, :, :, :].rearrange("p g v e -> p v g e"),
                                      bank[:, o, :].rearrange("p (v g e) -> p v g e", v=NKV, g=NG)), S["att_o"])
                    return
                for kv in range(NKV):
                    w = stat[:, 26 + 2 * (i % 2) + kv:27 + 2 * (i % 2) + kv]
                    one(v.scalar_tensor_tensor(OA[:, g, kv, :], bank[:, o, kv * HD:(kv + 1) * HD], w, OA[:, g, kv, :],
                                               ALU.mult, ALU.add), S["att_o"] if kv else None)

            maxima(0)
            for i in range(len(items)):
                if items[i][0] == "cmp":
                    weights(i)
                if i + 1 < len(items):
                    maxima(i + 1)
                if items[i][0] != "cmp":
                    weights(i)
                if i >= 1:
                    outputs(i - 1)

            R = slice(0, NROW)

            def sel(x, m, w):
                return x.rearrange("p (a o) -> p a o", o=1).to_broadcast([NROW, m, w])

            dve.wait_ge(S["att_ta"], len(items))
            one(v.memset(qbd[:, :], 0.0))
            one(v.memset(qz[:, :], 0.0))
            for kv in range(NKV):
                r0 = slice(kv * HD, (kv + 1) * HD)
                one(v.tensor_copy(qbd[r0, :].rearrange("p (n g v) -> p v g n", n=NSA, g=NG)[:, kv, :, :], qT[r0, :, NPR:NT]))
            for n in range(NSA):
                one(v.tensor_copy(qz[:, n * (NROW + NH):n * (NROW + NH) + NH], qbd[:, n * NH:(n + 1) * NH]),
                    S["smp_dve"] if n == NSA - 1 else None)
            dve.wait_ge(S["smp_pe"], 1)
            aux = sw[R, 576:576 + 24]
            one(v.tensor_tensor(aux.rearrange("p (b h) -> p b h", b=3), bank[R, 1, 32:56].rearrange("p (b h) -> p b h", b=3),
                                selh[R, :].rearrange("p (o h) -> p o h", o=1).to_broadcast([NROW, 3, NH]), ALU.mult))
            one(v.tensor_reduce(stat[R, 0:3], aux.rearrange("p (b h) -> p b h", b=3), AX, ALU.add))
            one(v.tensor_tensor(aux[:, 0:16].rearrange("p (b n) -> p b n", b=2), bank[R, 1, 0:16].rearrange("p (b n) -> p b n", b=2),
                                sel8[R, :].rearrange("p (o n) -> p o n", o=1).to_broadcast([NROW, 2, NSA]), ALU.mult))
            one(v.tensor_reduce(stat[R, 3:5], aux[:, 0:16].rearrange("p (b n) -> p b n", b=2), AX, ALU.add))
            vn = qf[R, 1600:1728].rearrange("p (b e) -> p b e", b=2)
            for b in range(2):
                x = bank[R, 1, 256 + b * P:256 + (b + 1) * P]
                one(v.tensor_scalar(vn[:, b, :], x[:, 0:HD], selv[R, 0:1], None, ALU.mult))
                one(v.scalar_tensor_tensor(vn[:, b, :], x[:, HD:P], selv[R, 1:2], vn[:, b, :], ALU.mult, ALU.add))
            dve.wait_ge(S["smask_in"], 16)
            one(v.tensor_tensor(sw[R, 0:512], bank[R, 0, :], smask[R, :], ALU.add))
            one(v.tensor_reduce(stat[R, 10:11], sw[R, 0:512], AX, ALU.max))
            one(v.tensor_scalar(stat[R, 8:9], stat[R, 10:11], -SCALE, None, ALU.mult), S["smp_max"])
            dve.wait_ge(S["smp_act"], 1)
            one(v.reciprocal(stat[R, 13:14], stat[R, 9:10]))
            one(v.tensor_scalar(sw[R, 0:512], sw[R, 0:512], stat[R, 13:14], None, ALU.mult))
            one(v.tensor_reduce(sw[R, 512:576], sw[R, 0:512].rearrange("p (n c) -> p c n", n=NSA), AX, ALU.add), S["smp_dve"])
            dve.wait_ge(S["smp_pe"], 2)
            pt = PT[:, 0, 0:2, :].rearrange("p a k -> p (a k)")
            one(v.tensor_copy(pt[:, 0:256], bank[:, 2, 0:256]), S["smp_dve"])
            pg = qf[R, 1728:1792]
            four = qf[R, 1792:1808]
            cand = qf[R, 1808:1822]
            one(v.tensor_copy(pg, bank[R, 3, 0:64]))
            one(v.tensor_reduce(four, pg.rearrange("p (j i) -> p j i", i=4), AX, ALU.add))
            one(v.tensor_tensor(cand, four[:, 1:15], pg.rearrange("p (j i) -> p j i", i=4)[:, 0:14, 3], ALU.add))
            one(v.tensor_reduce(stat[R, 14:15], cand, AX, ALU.min))
            one(v.tensor_scalar(cand, cand, stat[R, 14:15], None, ALU.is_le))
            one(v.tensor_tensor(cand, cand, iota16[R, 1:15], ALU.mult))
            one(v.tensor_reduce(stat[R, 14:15], cand, AX, ALU.max))
            one(v.tensor_scalar(four, iota16[R, :], stat[R, 14:15], NEG, ALU.is_equal, ALU.mult))
            dve.wait_ge(S["smp_pe"], 3)
            one(v.tensor_scalar(oS[R, :], bank[R, 4, 0:HD], selv[R, 0:1], None, ALU.mult))
            one(v.scalar_tensor_tensor(oS[R, :], bank[R, 4, HD:P], selv[R, 1:2], oS[R, :], ALU.mult, ALU.add))
            one(v.tensor_scalar(oS[R, :], oS[R, :], stat[R, 0:1], None, ALU.mult))

            def branch_max(b):
                if b == 0:
                    dve.wait_ge(S["smp_pe"], 4)
                    one(v.tensor_tensor(sw[R, :].rearrange("p (h j k) -> p h j k", h=2, j=8),
                                        bank[R, 5:7, :].rearrange("p h (j k) -> p h j k", j=8),
                                        four.rearrange("p (h j o) -> p h j o", h=2, o=1).to_broadcast([NROW, 2, 8, 64]), ALU.add))
                    one(v.tensor_reduce(stat[R, 10:11], sw[R, :], AX, ALU.max))
                else:
                    dve.wait_ge(S["smp_pe"], 5)
                    one(v.tensor_reduce(stat[R, 10:11], bank[R, 7, 1:WIN], AX, ALU.max))
                one(v.tensor_tensor(stat[R, 10:11], stat[R, 10:11], stat[R, 3 + b:4 + b], ALU.max))
                one(v.tensor_copy(stat[R, 11:12], stat[R, 3 + b:4 + b]))
                if b:
                    dve.wait_ge(S["smp_pe"], 6)
                    one(v.memset(sw[R, 0:1], 0.0))
                one(v.tensor_scalar(stat[R, 8:9], stat[R, 10:11], -SCALE, None, ALU.mult), S["smp_max"])

            def branch_out(b, tiles):
                dve.wait_ge(S["smp_act"], 2 + b)
                one(v.tensor_tensor(stat[R, 13:14], stat[R, 9:10], stat[R, 12:13], ALU.add))
                one(v.reciprocal(stat[R, 13:14], stat[R, 13:14]))
                one(v.tensor_tensor(stat[R, 13:14], stat[R, 13:14], stat[R, 1 + b:2 + b], ALU.mult))
                one(v.tensor_tensor(stat[R, 15:16], stat[R, 13:14], stat[R, 12:13], ALU.mult))
                dve.wait_ge(S["smp_pe"], 6 + 2 * b)
                one(v.tensor_copy(pt[:, 0:tiles * NROW], bank[:, 2, 0:tiles * NROW]), S["smp_dve"])
                dve.wait_ge(S["smp_pe"], 7 + 2 * b)
                x = sw2[R, :].rearrange("p (a e) -> p a e", e=HD)
                one(v.tensor_tensor(x.rearrange("p (b a) e -> p b a e", b=2), bank[R, 3:5, :].rearrange("p b (a e) -> p b a e", e=HD),
                                    sel16[R, :].rearrange("p (b a o) -> p b a o", b=2, o=1).to_broadcast([NROW, 2, 8, HD]), ALU.mult))
                one(v.tensor_reduce(sw2o[R, :], sw2[R, :].rearrange("p (a e) -> p e a", e=HD), AX, ALU.add))
                one(v.scalar_tensor_tensor(oS[R, :], sw2o[R, :], stat[R, 13:14], oS[R, :], ALU.mult, ALU.add))
                one(v.scalar_tensor_tensor(oS[R, :], vn[:, b, :], stat[R, 15:16], oS[R, :], ALU.mult, ALU.add))

            branch_max(0)
            one(v.tensor_copy(stat[R, 16:17], stat[R, 8:9]), S["smp_dve"])
            branch_out(0, NPG)
            branch_max(1)
            one(v.tensor_copy(stat[R, 16:17], stat[R, 8:9]), S["smp_dve"])
            branch_out(1, 4)
            one(v.tensor_copy(stat[R, 16:17], stat[R, 8:9]), S["smp_dve"])
            dve.wait_ge(S["smp_pe"], 10)
            for kv in range(NKV):
                one(v.tensor_copy(oT[kv * HD:(kv + 1) * HD, :, NPR:NT],
                                  bank[0:HD, 0, 0:NROW].rearrange("p (n g v) -> p v g n", n=NSA, g=NG)[:, kv, :, :]),
                    S["smp_dve"] if kv else None)

            for m in range(KD):
                dve.wait_ge(S["sg_ready"], 2 * m + 1)
                dve.wait_ge(S["pa_done"], m + 1)
                one(v.scalar_tensor_tensor(split(mT[:, m, :]), split(sg[:, 0, :]), 1.0, halves(1), ALU.add, ALU.mult))
                dve.wait_ge(S["sg_ready"], 2 * m + 2)
                dve.wait_ge(S["pb_done"], m + 1)
                one(v.scalar_tensor_tensor(split(mb), split(sg[:, 1, :]), 1.0, halves(3), ALU.add, ALU.mult))
                one(v.tensor_tensor(mT[:, m, :], mT[:, m, :], mb, ALU.add), S["m_ready"])

            N = slice(0, RN)

            def residual(t):
                dve.wait_ge(S["wo_done"], t + 1)
                dve.wait_ge(x_rows_in[t % 2], 16 * (t // 2 + 1))
                if t >= 3:
                    dve.wait_ge(y0_out[t % 3], 16)
                b = 6 * (t % 2)
                one(v.scalar_tensor_tensor(xm[N, t % 3, :].rearrange("p (h n) -> p h n", h=2), bank[N, b:b + 2, :], 0.5,
                                           xr[N, t % 2, :].rearrange("p (h n) -> p h n", h=2), ALU.mult, ALU.add), S["xm_ready"])

            def normalise(t):
                dve.wait_ge(S["rstd2"], t + 1)
                one(v.reciprocal(stat[N, 4:5], stat[N, 1:2]))
                if t >= 2:
                    dve.wait_ge(t_out[t % 2], 16 * (t // 2))
                    dve.wait_ge(S["t_turned"], t - 1)
                if t == 0:
                    dve.wait_ge(S["router_in"], ROUTER_IN)
                one(v.scalar_tensor_tensor(tn[N, t % 2, :], xm[N, t % 3, :], stat[N, 4:5], gffn[N, :], ALU.mult, ALU.mult),
                    S["t_ready"])

            def choose(t):
                dve.wait_ge(S["lg_done"], t + 1)
                one(v.tensor_tensor(lg[N, t, :], bank[N, 4, t * NE:(t + 1) * NE], rbias[N, :], ALU.add))
                one(v.max(mx8[N, t, :], lg[N, t, :]))
                mine(v.tensor_scalar(stat[N, 2:3], mx8[N, t, 0:1], -1.0, None, ALU.mult))
                one(v.tensor_copy(ixf[N, t, :], mx8[N, t, 0:4]), S["ex_in"])
                one(v.max_index(ix8[N, t, :].bitcast(U32), mx8[N, t, :], lg[N, t, :]))
                one(v.tensor_copy(rs[N, 0:4], ix8[N, t, 0:4].bitcast(U32)))
                for k in range(TOPK):
                    mine(v.tensor_scalar(ohall[N, t, k, :], iota_e[N, :], rs[N, k:k + 1], None, ALU.is_equal))
                mine.settle()
                one(v.tensor_reduce(m4[N, t, :], ohall[N, t, :, :].rearrange("p k e -> p e k"), AX, ALU.add), S["m4_ready"])
                dve.wait_ge(S["ex_done"], t + 1)
                one(v.reciprocal(stat[N, 5:6], stat[N, 3:4]))
                one(v.tensor_scalar(gate[N, t, :], ixf[N, t, :], stat[N, 5:6], None, ALU.mult))
                if t >= 1:
                    dve.wait_ge(S["gd_turned"], t)
                one(v.tensor_scalar(gd[N, :], ohall[N, t, 0, :], gate[N, t, 0:1], None, ALU.mult))
                for k in range(1, TOPK):
                    one(v.scalar_tensor_tensor(gd[N, :], ohall[N, t, k, :], gate[N, t, k:k + 1], gd[N, :], ALU.mult, ALU.add),
                        S["gd_ready"] if k == TOPK - 1 else None)

            def places(t):
                dve.wait_ge(S["pos_done"], t + 1)
                one(v.tensor_tensor(posn[N, t, :], bank[N, 5, P:P + NE], slot_e[N, :], ALU.add))
                x = ohall[N, t, :, :]
                one(v.tensor_tensor(x, x, posn[N, t, :].rearrange("p (o e) -> p o e", o=1).to_broadcast([RN, 4, NE]), ALU.mult))
                mine(v.tensor_copy(pairs[N, t, :, 0].bitcast(I32), tokid[N, t:t + 1].to_broadcast([RN, 4])))
                mine(v.tensor_copy(pairs[N, t, :, 1], gate[N, t, :]))
                one(v.tensor_reduce(dst[N, t, :], x, AX, ALU.add))
                one(v.tensor_copy(dsti[N, t, :].bitcast(I32), dst[N, t, :]), S["ent_ready"])

            def first_rows(t):
                dve.wait_ge(S["bd_done"], t + 1)
                x = xm[N, t % 3, :].rearrange("p (h n) -> p h n", h=2)
                one(v.tensor_tensor(x, x, bank[N, 2:4, :], ALU.add), S["y0_ready"])

            for t in range(RT + 2):
                if t < RT:
                    residual(t)
                if t >= 2:
                    places(t - 2)
                if t == RT + 1:
                    one(v.tensor_reduce(ovf[N, 0:1], bank[N, 5, P + NE:P + 2 * NE], AX, ALU.max))
                    one(v.tensor_copy(ovf[N, 1:2].bitcast(I32), ovf[N, 0:1]), S["ovf_ready"])
                if t < RT:
                    normalise(t)
                if 1 <= t <= RT:
                    choose(t - 1)
                if t >= 2:
                    first_rows(t - 2)

            dve.wait_ge(S["bup_in"], 16)
            dve.sem_inc(S["up_read"], 4)

            def block_of(n, e, par):
                one_bias = bu2[par]
                v.tensor_copy(one_bias, bup[:, bass.ds(e, 1), :].rearrange("p o c -> p (o c)")).then_inc(S["bias_ready"], 1)
                dve.wait_ge(S["bias_ready"], n + 1)
                for hf in range(2):
                    dve.wait_ge(S["ring_used"], 6 * n + 2 * hf + 1)
                    for f in range(4):
                        c = 4 * hf + f
                        r = v.tensor_scalar(AA[hf][:, f * P:(f + 1) * P], bank[:, 2 * hf, f * P:(f + 1) * P],
                                            one_bias[:, c:c + 1], LIMIT, ALU.add, ALU.min)
                    r.then_inc(S["up_read"], 1)
                    dve.wait_ge(S["ring_used"], 6 * n + 2 * hf + 2)
                    for f in range(4):
                        c = KD + 4 * hf + f
                        r = v.tensor_scalar(UU[hf][:, f * P:(f + 1) * P], bank[:, 2 * hf + 1, f * P:(f + 1) * P],
                                            one_bias[:, c:c + 1], LIMIT, ALU.add, ALU.min)
                    r.then_inc(S["up_read"], 1)
                    dve.wait_ge(S["up_read"], 4 * n + 2 * hf + 6)
                    v.tensor_scalar(UU[hf], UU[hf], -LIMIT, 1.0, ALU.max, ALU.add).then_inc(S["u_ready"], 1)
                    dve.wait_ge(S["u_ready"], 2 * n + hf + 1)
                    v.tensor_tensor(UU[hf], UU[hf], AA[hf], ALU.mult).then_inc(S["ua_ready"], 1)
                    dve.wait_ge(S["ua_ready"], 2 * n + hf + 1)
                    dve.wait_ge(S["sig_ready"], 2 * n + hf + 1)
                    v.tensor_tensor(HT[par][:, 4 * hf:4 * hf + 4, :].rearrange("p f t -> p (f t)"), UU[hf], SG[hf], ALU.mult)\
                        .then_inc(S["h_ready"], 1)

            with dve.Fori(0, NE // 2) as pair:
                block_of(2 * pair, 2 * pair, 0)
                block_of(2 * pair + 1, 2 * pair + 1, 1)
            dve.wait_ge(S["ovf_ready"], 1)
            most = dve.value_load(ovf[0:1, 1:2].bitcast(I32), min_val=0, max_val=NT)
            with dve.If(most > P):
                with dve.Fori(0, NE) as e:
                    for b in range(4):
                        block_of(4 * e + (NE + b), e, b % 2)

        @block.gpsimd
        def _(pool):
            dma = pool.dma_start
            dma(small[:, 0:d["small"].shape[1]], d["small"]).then_inc(S["small_in"], 16)
            dma(ident[:, :], d["ident"]).then_inc(S["small_in"], 16)
            dma(pagetab[0:1, :].bitcast(I32), d["pages"]).then_inc(S["page_in"], 16)
            dma(gain.rearrange("p h c -> p (h c)"), d["gains"]).then_inc(S["gains_in"], 16)
            dma(table, d["table0"]).then_inc(S["table_in"], 16)
            dma(trow[NT:NT + P, :], d["zeros"]).then_inc(S["table_in"], 16)
            dma(d["y"][NT:NT + P, :], d["zeros"]).then_inc(S["table_in"], 16)
            dma(d["o_kwin"][:, :, 0:WIN - 1], d["k_win"][:, :, 1:WIN]).then_inc(S["outs_done"], 16)
            dma(d["o_vwin"][:, 0:WIN - 1, :], d["v_win"][:, 1:WIN, :]).then_inc(S["outs_done"], 16)
            pool.wait_ge(S["qk_ready"], TT)
            dma(oT_st[:, 0:2 * KD * P], d["blockw"]).then_inc(S["bd_in"], 16)
            for t in range(TT):
                m = fraction(t)
                dma(d["o_kv"][t * P:t * P + m, :], kvraw[0:m, t, 0:KVC]).then_inc(S["kv_out"], 16)
            dma(d["o_vwin"][:, WIN - 1, :], kvraw[0:NSA, QT_N, VC + 2 * P:VC + 3 * P]).then_inc(S["kv_out"], 16)
            pool.wait_ge(S["qk_dve"], 1)
            dma(d["o_kwin"][:, :, WIN - 1], kT[:, 2, NPR:NT], allow_slow_non_contiguous=True).then_inc(S["outs_done"], 16)
            for other in dict.fromkeys(before["xsv"]):
                pool.wait_ge(*frees[other])
            some_pages(pool, chunk("xsv", 2), d["v_cmp"], S["xsv_in_pool"], NPAGES // 2, NPAGES // 2)
            pool.wait_ge(S["rec_free"], 1)
            pool.wait_ge(S["i_done"], KD)
            dma(w2.rearrange("p v f c -> p (v f c)"), d["w2"]).then_inc(S["w2_in"], 16)
            dma(d["o_h"], hout).then_inc(S["outs_done"], 16)
            dma(d["o_pconv"], pconv).then_inc(S["outs_done"], 16)
            dma(d["o_sconv"], xps).then_inc(S["outs_done"], 16)
            pool.wait_ge(S["ck_copied"], 1)
            dma(smask[0:NROW, :], d["smask"]).then_inc(S["smask_in"], 16)
            pool.wait_ge(S["smp_dve"], 9)
            dma(gffn[:, :], d["g_ffn"]).then_inc(S["router_in"], 16)
            dma(bdn[:, :], d["b_down"]).then_inc(S["router_in"], 16)
            dma(rwt.rearrange("p k e -> p (k e)"), d["router_w"]).then_inc(S["router_in"], 16)
            dma(rcon[:, 0:200], d["rcon"]).then_inc(S["router_in"], 16)
            dma(tokid, d["tokid"]).then_inc(S["router_in"], 16)
            def first_rows_out(t):
                pool.wait_ge(S["y0_ready"], t + 1)
                dma(d["y"][t * RN:(t + 1) * RN, :], xm[0:RN, t % 3, :]).then_inc(y0_out[t % 3], 16)

            pool.wait_ge(S["kv_out"], 16 * (TT + 1))
            for t in range(2):
                dma(xr[0:RN, t, :], d["x_rows"][t * RN:(t + 1) * RN, :]).then_inc(x_rows_in[t], 16)
            pool.wait_ge(S["m_ready"], KD)
            dma(bup.rearrange("p e c -> p (e c)"), d["b_up"]).then_inc(S["bup_in"], 16)
            pool.wait_ge(S["table_in"], 48)
            for t in range(RT + 2):
                if t < RT:
                    pool.wait_ge(S["t_ready"], t + 1)
                    dma(trow[t * RN:(t + 1) * RN, :], tn[0:RN, t % 2, :]).then_inc(t_out[t % 2], 16)
                if t + 2 < RT:
                    dma(xr[0:RN, t % 2, :], d["x_rows"][(t + 2) * RN:(t + 3) * RN, :]).then_inc(x_rows_in[t % 2], 16)
                if t >= 2:
                    pool.wait_ge(S["ent_ready"], t - 1)
                    for k in range(TOPK):
                        pool.indirect_dma_start(out=table, out_offset=bass.IndirectOffsetOnAxis(ap=dsti[0:RN, t - 2, k:k + 1].bitcast(U32), axis=0),
                                                in_=pairs[0:RN, t - 2, k, :].bitcast(I32), in_offset=None)\
                            .then_inc(S["scattered"], 16)
                    if t < RT + 1:
                        first_rows_out(t - 2)
            pool.wait_ge(S["scattered"], 16 * RT * TOPK)
            for b in (0, 1):
                pool.wait_ge(t_out[b], 16 * ((RT + 1 - b) // 2))

            def gather(n, par, row):
                dma(ent[par][:, :], table[bass.ds(row, P), :]).then_inc(S["ent_in"], 16)
                pool.wait_ge(S["ent_in"], 16 * n + 16)
                pool.sem_inc(S["pool_steps"], 1)
                pool.indirect_dma_start(out=GX[par][:, :], out_offset=None, in_=trow[:, :],
                                        in_offset=bass.IndirectOffsetOnAxis(ap=ent[par][:, 0:1].bitcast(U32), axis=0))\
                    .then_inc(S["xg_in"], 16)

            def add_rows(n, par):
                pool.wait_ge(S["y_scaled"], n + 2)
                pool.sem_inc(S["pool_steps"], 1)
                pool.indirect_dma_start(out=d["y"][:, :], out_offset=bass.IndirectOffsetOnAxis(ap=ent[par][:, 0:1].bitcast(U32), axis=0),
                                        in_=YR[par], in_offset=None, compute_op=ALU.add).then_inc(S["y_added"], 16)
                pool.wait_ge(S["y_added"], 16 * n + 16)

            gather(0, 0, 0)
            first_rows_out(RT - 1)
            for b in range(3):
                pool.wait_ge(y0_out[b], 16 * ((RT + 2 - b) // 3))
            gather(1, 1, SLOTS)
            with pool.Fori(0, NE // 2 - 1) as pair:
                for b in range(2):
                    add_rows(2 * pair + b, b)
                    gather(2 * pair + (b + 2), b, (2 * pair + (b + 2)) * SLOTS)
            add_rows(NE - 2, 0)
            add_rows(NE - 1, 1)
            pool.wait_ge(S["ovf_ready"], 1)
            most = pool.value_load(ovf[0:1, 1:2].bitcast(I32), min_val=0, max_val=NT)
            with pool.If(most > P):
                with pool.Fori(0, NE) as e:
                    for b in range(4):
                        gather(4 * e + (NE + b), b % 2, e * SLOTS + (b + 1) * P)
                        add_rows(4 * e + (NE + b), b % 2)
            pool.wait_ge(S["outs_done"], 16 * 6)




def _constants():
    c = {}
    f = np.float32
    q, k = np.arange(P)[:, None], np.arange(P)[None, :]
    c["causal"] = np.where(k <= q, 0.0, NEG).astype(f)
    c["ident"] = np.eye(P, dtype=f)
    cm = np.zeros((P, QT_N, 32), f)
    for t in range(QT_N):
        pos = t * P + np.arange(P)[:, None]
        ch = np.arange(32)[None, :]
        cm[:, t, :] = (ch * 16 + 31 <= pos) & (ch < NCH - 1)
    c["cmask"] = cm.reshape(P, -1)
    half = HD // 8
    inv = (f(500000.0) ** (-np.arange(half, dtype=f) / f(half))).astype(f)
    rope = np.zeros((P, TT, 16), f)
    for t in range(TT):
        pos = (t * P + np.arange(P)).astype(f) if t < QT_N else np.full(P, PAST, f)
        ang = (pos[:, None] * inv[None, :]).astype(f)
        rope[:, t, 0:8], rope[:, t, 8:16] = np.cos(ang), np.sin(ang)
    c["rope"] = rope.reshape(P, -1)
    r = np.arange(NROW)
    rn, rg, rv = r // NH, r % NH // NKV, r % NKV
    pad = lambda a: np.concatenate([a.astype(f), np.zeros((P - a.shape[0], a.shape[1]), f)])
    c["sel16"] = pad((np.arange(16)[None, :] == (rn * 2 + rv)[:, None]))
    c["sel8"] = pad(np.arange(8)[None, :] == rn[:, None])
    c["selh"] = pad(np.arange(8)[None, :] == (rg * 2 + rv)[:, None])
    c["selv"] = pad(np.arange(2)[None, :] == rv[:, None])
    c["rmat"] = pad((rn * 2 + rv)[:, None] == (rn * 2 + rv)[None, :])
    c["emat"] = pad(np.arange(NSA)[:, None] == rn[None, :])
    c["iota16"] = np.tile(np.arange(16, dtype=f), (P, 1))
    n, ch = np.arange(512) // CHS, np.arange(512) % CHS
    c["smask"] = np.where((n[None, :] == rn[:, None]) & (ch < CHS - 1)[None, :], 0.0, NEG).astype(f)
    c["rcon"] = np.concatenate([np.tile(np.arange(NE, dtype=f), (P, 1)), np.tile(np.arange(NE, dtype=f) * SLOTS, (P, 1)),
                                (np.arange(P)[:, None] < np.arange(RN)[None, :]).astype(f)], 1)
    c["tokid"] = (np.arange(RT)[None, :] * RN + np.arange(P)[:, None]).astype(np.int32)
    slots = np.arange(NE * SLOTS)
    c["table0"] = np.stack([TRASH + slots % P, 0 * slots], 1).astype(np.int32)
    return c


def _layouts(x):
    c = _constants()
    f = np.float32
    d = {}
    rows = np.concatenate([x["x_prompt"][0], x["x_sample"][:, 0]], 0)
    chan = lambda v: np.ascontiguousarray(v.reshape(KD, P).T)
    d["x_rows"] = rows
    d["xT"] = rows.T.reshape(KD, P, NT).transpose(1, 0, 2)
    w = x["w_in"][0]
    ar, ag = w[:, 0:D], w[:, D:2 * D]
    o = 2 * D
    q = w[:, o:o + QC].reshape(D, NKV, NG, HD).transpose(0, 2, 1, 3).reshape(D, QC)
    o += QC
    kv = [w[:, o + i * P:o + (i + 1) * P] for i in range(6)]
    o += KVC
    ng = w[:, o:o + 24].reshape(D, NKV, NG, 3).transpose(0, 3, 2, 1).reshape(D, 24)
    o += 24
    ga, gb = w[:, o:o + D], w[:, o + D:o + 2 * D]
    tok = np.concatenate([q] + kv[0::2] + kv[1::2] + [ng], 1)
    d["w_tok"] = tok.reshape(KD, P, TC).transpose(1, 0, 2)

    def cols(a):
        k = a.shape[0] // P
        return a.reshape(k, P, 2, 512).transpose(2, 1, 0, 3).reshape(2, P, k * 512)

    d["w_ch"] = np.concatenate([cols(a) for a in (ar, ag, ga, gb)], 0)
    d["w_pa"] = cols(x["w_proj_a"][0])
    d["w_pb"] = cols(x["w_proj_b"][0].reshape(NKV, NG, HD, D).transpose(1, 0, 2, 3).reshape(QC, D))
    d["w_out"] = cols(x["w_out"][0])
    lru = np.stack([chan(x["conv_w"][0, k]) for k in range(4)] + [chan(x["conv_b"][0]), chan(x["lru_ba"][0].reshape(D)),
                   chan(x["lru_bx"][0].reshape(D)), chan(x["lru_lambda"][0])], 2)
    h0 = x["state_h"][0].reshape(NSA, KD, P).transpose(2, 1, 0)
    conv = np.zeros((P, KD, NSA, 4), f)
    conv[:, :, :, 0:3] = x["state_conv"][0].reshape(NSA, 3, KD, P).transpose(3, 2, 0, 1)
    pos = np.stack([x["cmp_pos_k"][0], x["cmp_pos_v"][0]]).reshape(2, 2, LP, 2, HD)
    flat = lambda a: a.reshape(P, -1)
    pos = pos.transpose(3, 4, 0, 2, 1)
    small = [c["cmask"], c["rope"], chan(x["g_mix"][0]), flat(lru), flat(h0), flat(conv),
             c["causal"], np.ones((P, P), f), c["sel16"], c["sel8"], c["selh"], c["selv"], c["rmat"], c["emat"],
             flat(pos), c["iota16"]]
    d["small"] = np.concatenate(small, 1)
    d["ident"] = c["ident"]
    d["pages"] = x["page_table"].reshape(1, NPAGES).astype(np.int32)
    gains = np.concatenate([np.tile(x["g_q"][0], NH)] + [np.tile(x[n][0], NKV) for n in ("g_k_cmp", "g_k_slc", "g_k_win")])
    d["gains"] = np.broadcast_to(gains, (P, NHN * HD))
    bd = np.zeros((2, KD, P, P), f)
    for i, n in enumerate(("lru_wa", "lru_wx")):
        blocks = x[n][0].reshape(KD, 2, HD, HD)
        bd[i, :, 0:HD, 0:HD], bd[i, :, HD:P, HD:P] = blocks[:, 0], blocks[:, 1]
    d["blockw"] = flat(bd.transpose(2, 0, 1, 3))
    d["w1"] = np.stack([x[n][0].reshape(2, LP, 2, HD, CF).transpose(2, 3, 0, 1, 4).reshape(P, SLOT)
                        for n in ("cmp_w1_k", "cmp_w1_v")])
    w2 = np.zeros((P, 2, 2, 3 * HD), f)
    for i, n in enumerate(("cmp_w2_k", "cmp_w2_v")):
        w2[:, i, :, HD:2 * HD] = x[n][0].reshape(2, P, HD).transpose(1, 0, 2)
    d["w2"] = flat(w2)
    phys = x["cache_k_cmp"].shape[1]
    for n, s in (("k_cmp", "cache_k_cmp"), ("v_cmp", "cache_v_cmp")):
        a = x[s][0].reshape(phys, 8, LP, 2, NKV, HD).transpose(0, 3, 5, 2, 4, 1)
        d[n] = a.reshape(phys * P, P)
    d["k_slc"] = x["cache_k_slc"][0].transpose(0, 2, 3, 1).reshape(phys * P, P)
    d["v_slc"] = x["cache_v_slc"][0].reshape(phys * P, P)
    d["k_win"] = x["cache_k_win"][0].transpose(2, 3, 0, 1).reshape(P, NSA, WIN)
    d["v_win"] = x["cache_v_win"][0].reshape(NSA, WIN, P)
    d["smask"] = c["smask"]
    d["g_ffn"] = np.broadcast_to(x["g_ffn"][0], (P, D))
    d["b_down"] = x["exp_b_down"][0]
    d["router_w"] = flat(x["router_w"][0].reshape(KD, P, NE).transpose(1, 0, 2))
    d["rbias"] = np.broadcast_to(x["router_b"][0], (P, NE))
    d["rcon"] = np.concatenate([d.pop("rbias"), c["rcon"]], 1)
    d["tokid"] = c["tokid"]
    d["table0"] = c["table0"]
    d["zeros"] = np.zeros((P, D), f)
    d["b_up"] = flat(x["exp_b_up"][0].reshape(NE, 2 * KD, P).transpose(2, 0, 1))
    d["w_up"] = x["exp_w_up"][0].reshape(NE * D, 2 * D)
    d["w_down"] = x["exp_w_down"][0].reshape(NE * D, D)
    return {n: np.ascontiguousarray(a) for n, a in d.items()}, phys


_OUTPUTS = {"y": (NT + P, D), "o_kv": (NT, KVC), "o_kwin": (P, NSA, WIN), "o_vwin": (NSA, WIN, P),
            "o_h": (P, KD, 9), "o_pconv": (P, KD, 3), "o_sconv": (P, KD, NSA, 4)}


def kernel(**inputs):
    import concourse.bacc as bacc
    from concourse.bass_utils import run_bass_kernel_spmd as run

    arrays, phys = _layouts({n: np.asarray(a) for n, a in inputs.items()})
    nc = bacc.Bacc("TRN2", target_bir_lowering=False, num_devices=1)
    d = {n: nc.dram_tensor("in_" + n, a.shape, mybir.dt.from_np(a.dtype), kind="ExternalInput").ap() for n, a in arrays.items()}
    d |= {n: nc.dram_tensor("out_" + n, s, F32, kind="ExternalOutput").ap() for n, s in _OUTPUTS.items()}
    d["n_phys"] = phys
    build(nc, d)
    got = run(nc, [{"in_" + n: a for n, a in arrays.items()}], core_ids=[0]).results[0]
    o = {n: got["out_" + n] for n in _OUTPUTS}
    kv = o["o_kv"].reshape(NT, 6, NKV, HD)
    prompt = lambda i: kv[0:NPR, i][None, None]
    sample = lambda i: kv[NPR:NT, i][None, :, None]
    chan = lambda a: a.transpose(1, 0, *range(2, a.ndim)).reshape(D, -1)
    h = chan(o["o_h"]).T
    sconv = chan(o["o_sconv"]).reshape(D, NSA, 4)[:, :, 1:4].transpose(1, 2, 0)
    kwin = o["o_kwin"].reshape(NKV, HD, NSA, WIN).transpose(2, 3, 0, 1)
    return (o["y"][0:NPR][None], o["y"][NPR:NT][:, None],
            prompt(0), prompt(3), prompt(1), prompt(4), prompt(2), prompt(5),
            h[0:1][None], chan(o["o_pconv"]).T[None, None],
            sample(0), sample(3), sample(1), sample(4),
            kwin[None], o["o_vwin"].reshape(NSA, WIN, NKV, HD)[None],
            h[1:9][None], sconv[None])
```

```python
from contextlib import ExitStack
import math

import numpy as np

import concourse.bass as bass
from concourse import mybir

ALU = mybir.AluOpType
ACT = mybir.ActivationFunctionType
AX = mybir.AxisListType.X
F32 = mybir.dt.float32
I32 = mybir.dt.int32
U32 = mybir.dt.uint32
F32R = mybir.dt.float32r

P = 128
D = 1024
KD = D // P
NPR = 512
NSA = 8
NT = NPR + NSA
HN = NT // 2
QT_N = NPR // P
TT = QT_N + 1
PAST = 1024
PAGE = 128
NPG = PAST // PAGE
NPAGES = NSA * NPG
HD = 64
NKV = 2
NG = 4
NH = NKV * NG
NROW = NSA * NH
NHN = NH + 3 * NKV
QC = NH * HD
KVC = 6 * NKV * HD
TC = QC + KVC + 3 * NH
LP = 8
NCH = 32
CHS = PAST // 16
CF = 256
WIN = 512
NE = 32
TOPK = 4
RT = 5
RN = NT // RT
SLOTS = 5 * P
TRASH = NT
SCALE = HD ** -0.5
NEG = -1e30
EPS = 1e-6
LIMIT = 7.0
ALPHA = 1.702
SLOT = 4096
NSLOT = 6
ROUTER_IN = 80
VC = 3 * NKV * HD


class Steps:

    def __init__(self, eng, own):
        self.eng, self.own, self.n, self.last = eng, own, {}, None

    def __call__(self, ins, sem=None):
        sem = self.own if sem is None else sem
        self.n[id(sem)] = self.n.get(id(sem), 0) + 1
        ins.then_inc(sem, 1)
        self.last = (sem, self.n[id(sem)])

    def settle(self):
        self.eng.wait_ge(*self.last)


def ring_plan():
    return [("ar0", 1), ("ag0", 1), ("ar1", 1), ("ag1", 1),
            ("xsk", 2), ("w1k", 1), ("xsv", 2), ("w1v", 1),
            ("kslc", 2), ("vslc", 2), ("kwin", 1), ("vwin", 1),
            ("ga0", 1), ("gb0", 1), ("pa0", 1), ("pb0", 1),
            ("ga1", 1), ("gb1", 1), ("pa1", 1), ("pb1", 1),
            ("wo0", 1), ("wo1", 1)]


def build(nc, d):
    ctx = ExitStack()
    with ctx:
        def sb(name, shape, dt=F32):
            return ctx.enter_context(nc.sbuf_tensor(name, shape, dt))

        def sem(name):
            return ctx.enter_context(nc.semaphore(name))

        def both(name, cols):
            with nc.sbuf_tensor(name, [P, cols], F32) as plain:
                pass
            return plain, ctx.enter_context(nc.sbuf_tensor(name + "_rounded", [P, cols], F32R))

        ring, ring_r = both("ring", NSLOT * SLOT)
        slab, slab_r = both("slab", KD * TC)
        xn_st, xn_r = both("xn", KD * NT)
        xn = xn_st[:, :].rearrange("p (k t) -> p k t", k=KD)
        wide, wide_r = both("wide", TT * (QC + KVC + 3 * NH))
        qraw = wide[:, 0:TT * QC].rearrange("p (t c) -> p t c", t=TT)
        kvraw = wide[:, TT * QC:].rearrange("p (t c) -> p t c", t=TT)
        qT = sb("qT", [P, NG, NT])
        kT = sb("kT", [P, 3, NT])
        oT_st = sb("oT", [P, NG * NT])
        oT = oT_st[:, :].rearrange("p (g t) -> p g t", g=NG)
        ident = sb("ident", [P, P])
        SMALL = 1670
        small = sb("small", [P, SMALL])
        bank = ctx.enter_context(nc.psum_tensor("bank", [P, 8, 512], F32))

        at = [0]

        def part(n):
            at[0] += n
            assert at[0] <= SMALL
            return small[:, at[0] - n:at[0]]

        cmask = part(4 * 32).rearrange("p (q c) -> p q c", q=4)
        rope = part(TT * 16).rearrange("p (t x) -> p t x", t=TT)
        gmix = part(KD)
        lruv = part(KD * 8).rearrange("p (m x) -> p m x", m=KD)
        h0 = part(KD * NSA).rearrange("p (m n) -> p m n", m=KD)
        xps = part(KD * NSA * 4).rearrange("p (m n k) -> p m n k", m=KD, n=NSA)
        causal = part(P)
        onesm = part(P)
        sel16 = part(16)
        sel8 = part(8)
        selh = part(8)
        selv = part(2)
        rmat = part(NROW)
        emat = part(NROW)
        posc = part(4 * LP).rearrange("p (v l x) -> p v l x", v=2, l=LP)
        iota16 = part(16)
        pconv = part(KD * 3).rearrange("p (m k) -> p m k", m=KD)
        hout = part(KD * 9).rearrange("p (m k) -> p m k", m=KD)
        pagetab = part(NPAGES)
        hb = part(2 * KD).rearrange("p (x m) -> p x m", x=2)
        c2 = part(2 * KD).rearrange("p (x m) -> p x m", x=2)
        lt = part(4 * KD).rearrange("p (x m) -> p x m", x=4)
        ssq = part(TT * NHN).rearrange("p (t h) -> p t h", t=TT)
        rsq = part(TT * NHN).rearrange("p (t h) -> p t h", t=TT)
        eps1 = part(1)
        stat = part(32)
        cbias = part(4)
        ovf = part(2)
        entf = [part(2), part(2)]
        negc = part(4 * 32).rearrange("p (q c) -> p q c", q=4)
        ent = [e.bitcast(I32) for e in entf]

        slot_of, count_of, j = {}, {}, 0
        loads = [0] * NSLOT
        for name, n in ring_plan():
            slot_of[name] = j % NSLOT
            assert j % NSLOT + n <= NSLOT
            if n == 1 and name != "vwin":
                loads[j % NSLOT] += 1
                count_of[name] = 16 * loads[j % NSLOT]
            j += n
        NFRONT = j
        eslot = [(NFRONT + c) % NSLOT for c in range(6)]
        ebase = [16 * loads[s] for s in eslot]

        def chunk(name, n=1):
            s = slot_of[name]
            return ring[:, s * SLOT:(s + n) * SLOT]

        def w8(name):
            return chunk(name).rearrange("p (k n) -> p k n", k=KD)

        xsq = ring[:, 4 * SLOT:4 * SLOT + KD * NT].rearrange("p (k t) -> p k t", k=KD)
        rstd = ring[:, 4 * SLOT + KD * NT:4 * SLOT + KD * NT + NT]
        wtok = slab[:, :].rearrange("p (k n) -> p k n", k=KD)
        A = slab[:, 0:4 * NT].rearrange("p (m t) -> p m t", m=4)
        V = slab[:, 4 * NT:8 * NT].rearrange("p (m t) -> p m t", m=4)
        IX = slab[:, 8 * NT:12 * NT].rearrange("p (m t) -> p m t", m=4)
        Y = slab[:, 12 * NT:20 * NT].rearrange("p (m t) -> p m t", m=KD)
        gh = slab[:, 0:4096].rearrange("p (v f h c) -> p v f h c", v=2, f=2, h=2)
        p1c = slab[:, 4096:5120].rearrange("p (b c) -> p b c", b=2)
        hrep = slab[:, 5120:5632].rearrange("p (f h r c) -> p f h r c", f=2, h=2, r=4)
        ghp = slab[:, 5632:6144].rearrange("p (v f c) -> p v f c", v=2, f=2)[:, :, :, 0:64]
        ckT = slab[:, 4096:4608]
        cv = slab[:, 4608:5120].rearrange("p (t c) -> p t c", t=4)
        PR = slab[:, 0:2048].rearrange("p (b h k) -> p b h k", b=2, h=2)
        PT = slab[:, 2048:4096].rearrange("p (b h k) -> p b h k", b=2, h=2)
        qbd = slab[:, 5632:5696]
        qz = slab[:, 5696:6208]
        sqt = oT_st[:, 0:NHN * HD].rearrange("p (h c) -> p h c", h=NHN)
        gain = oT_st[:, NHN * HD:2 * NHN * HD].rearrange("p (h c) -> p h c", h=NHN)
        bd = oT_st[:, 0:2 * KD * P].rearrange("p (x m c) -> p x m c", x=2, m=KD)
        qf = qraw[:, :, :].rearrange("p t c -> p (t c)")
        xpp = qf[:, 0:2 * 515].rearrange("p (b c) -> p b c", b=2)
        xc = qf[:, 1030:1030 + 2 * NT].rearrange("p (b c) -> p b c", b=2)
        xp = qf[:, 0:LP * 66 * 2].rearrange("p (v l c) -> p v l c", v=2, l=LP)
        w2 = qf[:, 1056:1056 + 2 * 2 * 3 * HD].rearrange("p (v f c) -> p v f c", v=2, f=2)
        ckTp = qf[:, 2016:2048]
        cvp = qf[:, 2048:2560].rearrange("p (v g e) -> p v g e", v=2, g=4)
        smask = qf[:, 0:512]
        oS = qf[:, 512:576]
        sw = qf[:, 576:576 + 1024]
        OA = [x.rearrange("p (g v e) -> p g v e", g=NG, v=NKV) for x in (qf[:, 576:1088], slab[:, 5120:5632])]
        sw2 = slab[:, 0:1024]
        sw2o = slab[:, 1024:1088]
        mT = slab[:, 0:KD * NT].rearrange("p (k t) -> p k t", k=KD)
        sg = slab[:, 4160:4160 + 2 * NT].rearrange("p (b t) -> p b t", b=2)
        mb = slab[:, 5200:5200 + NT]
        sq_rows = oT_st[:, 0:D]
        xm = slab[:, 5120:5120 + 3 * D].rearrange("p (b n) -> p b n", b=3)
        tn = slab[:, 8288:8288 + 2048].rearrange("p (b n) -> p b n", b=2)
        kvf = kvraw[:, :, :].rearrange("p t c -> p (t c)")
        tT = kvf[:, 0:KD * P].rearrange("p (k t) -> p k t", k=KD)
        xr = kvf[:, 1024:1024 + 2048].rearrange("p (b n) -> p b n", b=2)
        lg = kvf[:, 3072:3072 + RT * NE].rearrange("p (t e) -> p t e", t=RT)
        gd = [kvf[:, 3360:3360 + NE], kvf[:, 3520:3520 + NE]]
        gdT = kvf[:, 3392:3392 + P]
        gffn = qf[:, 0:D]
        bdn = qf[0:NE, D:2 * D]
        qtf = qT[:, :, :].rearrange("p g t -> p (g t)")
        rwt = qtf[:, 0:KD * NE].rearrange("p (k e) -> p k e", k=KD)
        rcon = qtf[:, 256:256 + 4 * NE + 128 + 8]
        rbias, iota_e, slot_e, tri = rcon[:, 0:32], rcon[:, 32:64], rcon[:, 64:96], rcon[:, 96:96 + RN]
        tokid = rcon[:, 200:200 + RT].bitcast(I32)
        m4 = qtf[:, 520:520 + RT * NE].rearrange("p (t e) -> p t e", t=RT)
        mx8 = qtf[:, 680:680 + RT * 8].rearrange("p (t k) -> p t k", t=RT)
        ix8 = qtf[:, 720:720 + RT * 8].rearrange("p (t k) -> p t k", t=RT)
        ixf = qtf[:, 760:760 + RT * 4].rearrange("p (t k) -> p t k", t=RT)
        gate = qtf[:, 780:780 + RT * 4].rearrange("p (t k) -> p t k", t=RT)
        rs = qtf[:, 800:832]
        posn = qtf[:, 832:832 + RT * NE].rearrange("p (t e) -> p t e", t=RT)
        dst = qtf[:, 992:992 + RT * 4].rearrange("p (t k) -> p t k", t=RT)
        dsti = qtf[:, 1012:1012 + RT * 4].rearrange("p (t k) -> p t k", t=RT)
        pairs = qtf[:, 1032:1032 + RT * 8].rearrange("p (t k x) -> p t k x", t=RT, k=4)
        ohall = xn[:, 0:2, :].rearrange("p k t -> p (k t)")[:, 0:RT * 4 * NE]\
            .rearrange("p (t k e) -> p t k e", t=RT, k=4)
        bup = oT_st[:, D:D + 512].rearrange("p (e c) -> p e c", e=NE)
        GX = [slab[:, b * D:(b + 1) * D] for b in (0, 1)]
        XT = [slab[:, (2 + b) * D:(3 + b) * D].rearrange("p (k t) -> p k t", k=KD) for b in (0, 1)]
        HH, HL = [slab_r[:, (4 + b) * D:(5 + b) * D].rearrange("p (k t) -> p k t", k=KD) for b in (0, 1)]
        HHf = slab_r[:, 4 * D:5 * D].bitcast(F32)
        YR = [slab[:, (6 + b) * D:(7 + b) * D] for b in (0, 1)]
        AA = [slab[:, 8192 + b * 512:8704 + b * 512] for b in (0, 1)]
        UU = [slab[:, 9216 + b * 512:9728 + b * 512] for b in (0, 1)]
        SG = [wide[:, SLOT + b * 512:SLOT + (b + 1) * 512] for b in (0, 1)]
        bu2 = [wide[:, SLOT + 1024 + b * 16:SLOT + 1040 + b * 16] for b in (0, 1)]
        WH = [xn_r[:, 0:SLOT], wide_r[:, 0:SLOT]]
        WHf = [w.bitcast(F32) for w in WH]

        trow = nc.dram_tensor("token_rows", (NT + P, D), F32).ap()
        table = nc.dram_tensor("slot_table", (NE * SLOTS, 2), I32).ap()

        S = {n: sem(n) for n in """
            act_steps dve_steps pool_steps small_in ident_in page_in gains_in bd_in
            x_squared x_summed x_root xn_ready tok_done tok_copied ss_ready rs_root qk_ready qk_turned qk_dve qk_act
            kv_out ar_done ar_copied ag_done ag_gelu r_done i_done th_ready ti_ready xc_ready decay_ready gap_ready
            gap_root y_ready lam_ready lam_exp gates_t
            xsk_in xsv_in xsv_in_pool kslc_in vslc_in w2_in
            cs_done p1_copied gh_raw xp_ready vt_done cp_done pp_copied ghp_raw gh_gelu hrep_ready ck_done ck_copied ck_act
            att_s att_max att_p att_pc att_ce att_cs att_ta att_pa att_pv att_o vwin_in
            smp_pe smp_dve smp_act smp_max smask_in bias_ready u_ready ua_ready
            ga_done pa_done gb_done pb_done sg_ready m_ready
            wo_done router_in xm_ready ss2 rstd2 t_ready t_turned t_copied lg_done ex_in ex_done gd_ready gd_turned
            gd_copied bd_done y0_ready m4_ready pos_done ent_ready table_in scattered bup_in ovf_ready
            xg_in ent_in x_turned xt_ready ring_used up_read sig_ready h_ready hh_ready hl_ready wh_ready wl_ready y_scaled y_added
            outs_done""".split()}
        x_rows_in, t_out = ([sem(f"{n}{b}") for b in (0, 1)] for n in ("x_rows_in", "t_out"))
        y0_out = [sem(f"y0_out{b}") for b in range(3)]
        x_in, wtok_in = ([sem(f"{n}{c}") for c in range(4)] for n in ("x_in", "wtok_in"))
        ring_in = [sem(f"ring_in{i}") for i in range(NSLOT)]

        block = ctx.enter_context(nc.Block())
        items = []
        for qt in range(QT_N):
            items.append(("cmp", qt, 0, 0))
            full = [("full", qt, b, g) for b in (1, 2) for g in range(NG)]
            items += full[0:1] + ([("out", qt - 1, 0, 0)] if qt else []) + full[1:]
        items.append(("out", QT_N - 1, 0, 0))

        n_full = [sum(x[0] == "full" for x in items[:i + 1]) for i in range(len(items))]
        n_cmp = [sum(x[0] == "cmp" for x in items[:i + 1]) for i in range(len(items))]
        n_v = [a + b for a, b in zip(n_full, n_cmp)]
        turned_at = {x[1]: i for i, x in enumerate(items) if x[0] == "out"}

        def halves(pair, n=HN):
            return bank[:, 2 * pair:2 * pair + 2, 0:n]

        def expert_slot(c):
            return ring[:, eslot[c] * SLOT:(eslot[c] + 1) * SLOT]

        def expert_slot_low(c):
            return ring_r[:, eslot[c] * SLOT:(eslot[c] + 1) * SLOT]

        def split(x):
            return x.rearrange("p (h t) -> p h t", h=2)

        def fraction(k):
            return P if k < QT_N else NSA

        frees = {"ar0": (S["ar_done"], 4), "ag0": (S["ag_done"], 4), "ar1": (S["ar_done"], 8), "ag1": (S["ag_done"], 8),
                 "xsk": (S["cs_done"], 4), "w1k": (S["cp_done"], 2), "xsv": (S["cs_done"], 8), "w1v": (S["cp_done"], 4),
                 "kslc": (S["smp_pe"], 2), "vslc": (S["smp_pe"], 9), "kwin": (S["smp_pe"], 3), "vwin": (S["smp_pe"], 7),
                 "ga0": (S["ga_done"], 4), "gb0": (S["gb_done"], 4), "pa0": (S["pa_done"], 4), "pb0": (S["pb_done"], 4),
                 "ga1": (S["ga_done"], 8), "gb1": (S["gb_done"], 8), "pa1": (S["pa_done"], 8), "pb1": (S["pb_done"], 8),
                 "wo0": (S["wo_done"], RT), "wo1": (S["wo_done"], RT)}
        owner = {}
        before = {}
        jj = 0
        for name, n in ring_plan():
            sl = [(jj + i) % NSLOT for i in range(n)]
            before[name] = [owner[x] for x in sl if x in owner]
            for x in sl:
                owner[x] = name
            jj += n

        def some_pages(eng, dst, pool, signal, first, n):
            with eng.Fori(first // 4, (first + n) // 4) as i:
                rows = [eng.value_load(pagetab[0:1, bass.ds(4 * i + u, 1)].bitcast(I32), min_val=0, max_val=d["n_phys"] - 1)
                        for u in range(4)]
                for u, page in enumerate(rows):
                    eng.dma_start(dst[:, bass.ds((4 * i + u) * P, P)], pool[bass.ds(page * P, P), :]).then_inc(signal, 16)

        @block.sync
        def _(sp):
            for c in range(4):
                sp.dma_start(xn[:, 2 * c:2 * c + 2, :], d["xT"][:, 2 * c:2 * c + 2, :]).then_inc(x_in[c], 16)
            for c in range(4):
                sp.dma_start(wtok[:, 2 * c:2 * c + 2, :], d["w_tok"][:, 2 * c:2 * c + 2, :]).then_inc(wtok_in[c], 16)

            def slots_free(name):
                for other in dict.fromkeys(before[name]):
                    sp.wait_ge(*frees[other])

            def load(name, src):
                slots_free(name)
                sp.dma_start(chunk(name)[:, 0:src.shape[1]], src).then_inc(ring_in[slot_of[name]], 16)

            def load_pages(name, pool, signal, pages=NPAGES):
                slots_free(name)
                some_pages(sp, chunk(name, 2), pool, signal, 0, pages)

            load("ar0", d["w_ch"][0])
            load("ag0", d["w_ch"][2])
            load("ar1", d["w_ch"][1])
            load("ag1", d["w_ch"][3])
            sp.wait_ge(S["page_in"], 16)
            sp.wait_ge(S["xn_ready"], KD)
            load_pages("xsk", d["k_cmp"], S["xsk_in"])
            load("w1k", d["w1"][0])
            load_pages("xsv", d["v_cmp"], S["xsv_in"], NPAGES // 2)
            load("w1v", d["w1"][1])
            load_pages("kslc", d["k_slc"], S["kslc_in"])
            load_pages("vslc", d["v_slc"], S["vslc_in"])
            slots_free("kwin")
            sp.dma_start(chunk("kwin").rearrange("p (n k) -> p n k", n=NSA), d["k_win"])\
                .then_inc(ring_in[slot_of["kwin"]], 16)
            slots_free("vwin")
            for n in range(NSA):
                sp.dma_start(chunk("vwin")[:, n * WIN:(n + 1) * WIN].rearrange("p (t c) -> p t c", t=4),
                             d["v_win"][n].rearrange("(t p) c -> p t c", p=P)).then_inc(S["vwin_in"], 16)
            for c in range(2):
                load(f"ga{c}", d["w_ch"][4 + c])
                load(f"gb{c}", d["w_ch"][6 + c])
                load(f"pa{c}", d["w_pa"][c])
                load(f"pb{c}", d["w_pb"][c])
            load("wo0", d["w_out"][0])
            load("wo1", d["w_out"][1])

            order = (0, 2, 1, 3)

            def expert_chunk(e, c):
                dst = ring[:, eslot[c] * SLOT:(eslot[c] + 1) * SLOT]
                if c < 4:
                    q = order[c]
                    src = d["w_up"][bass.ds(e * D, D), q * 512:(q + 1) * 512].rearrange("(k p) n -> p k n", p=P)
                    dst = dst.rearrange("p (k n) -> p k n", k=KD)
                else:
                    src = d["w_down"][bass.ds(e * D + (c - 4) * 512, 512), :].rearrange("(f p) n -> p f n", p=P)
                    dst = dst.rearrange("p (f n) -> p f n", f=4)
                sp.dma_start(dst, src).then_inc(ring_in[eslot[c]], 16)

            for c in range(6):
                sp.wait_ge(*frees[owner[eslot[c]]])
                expert_chunk(0, c)
            with sp.Fori(1, NE) as e:
                for c in range(6):
                    sp.wait_ge(S["ring_used"], 6 * e + c - 5)
                    expert_chunk(e, c)
            sp.wait_ge(S["ovf_ready"], 1)
            most = sp.value_load(ovf[0:1, 1:2].bitcast(I32), min_val=0, max_val=NT)
            with sp.If(most > P):
                with sp.Fori(0, NE) as e:
                    for b in range(4):
                        for c in range(6):
                            sp.wait_ge(S["ring_used"], 24 * e + 6 * (NE + b) + c - 5)
                            expert_chunk(e, c)

        @block.tensor
        def _(pe):
            mm = pe.matmul

            def two_halves(pair, lhsT, rhs, first, last):
                for h in (0, 1):
                    r = mm(bank[:, 2 * pair + h, 0:HN], lhsT, rhs[:, h * HN:(h + 1) * HN], start=first, stop=last)
                return r

            pe.wait_ge(S["small_in"], 16)
            for k in range(KD):
                pe.wait_ge(S["x_squared"], k + 1)
                r = two_halves(3, onesm, xsq[:, k, :], k == 0, k == KD - 1)
            r.then_inc(S["x_summed"], 1)
            def turn_heads(t):
                pe.wait_ge(S["qk_ready"], t + 1)
                if t == 0:
                    pe.wait_ge(S["ident_in"], 16)
                else:
                    pe.wait_ge(S["qk_act"], t)
                    pe.wait_ge(S["qk_dve"], t)
                m = fraction(t)
                for c in range(7):
                    x, b = (qraw, 6) if c < NG else (kvraw, 7)
                    c %= NG
                    r = pe.transpose(bank[:, b, c * m:(c + 1) * m], x[0:m, t, c * P:(c + 1) * P], ident[0:m, 0:m])
                r.then_inc(S["qk_turned"], 1)

            for t in range(TT):
                if t >= 2:
                    pe.wait_ge(S["tok_copied"], t - 1)
                m = fraction(t)
                for k in range(KD):
                    if t == 0:
                        pe.wait_ge(S["xn_ready"], k + 1)
                        pe.wait_ge(wtok_in[k // 2], 16)
                    for c, (a, b) in enumerate(((0, 512), (512, 1024), (1024, TC))):
                        r = mm(bank[0:m, 3 * (t % 2) + c, 0:b - a], xn[:, k, t * P:t * P + m], wtok[:, k, a:b],
                               start=k == 0, stop=k == KD - 1)
                r.then_inc(S["tok_done"], 1)
                if t >= 1:
                    turn_heads(t - 1)

            def block_gates(m):
                for x, done in ((0, "r_done"), (1, "i_done")):
                    if x == 0:
                        if m == 0:
                            pe.wait_ge(S["bd_in"], 16)
                            pe.wait_ge(S["qk_act"], TT)
                            pe.wait_ge(S["qk_dve"], TT)
                        pe.wait_ge(S["xc_ready"], m + 1)
                        if m >= 1:
                            pe.wait_ge(S["th_ready"], m)
                    elif m >= 1:
                        pe.wait_ge(S["ti_ready"], m)
                    two_halves(2 + x, bd[:, x, m, :], xc[:, m % 2, :], True, True).then_inc(S[done], 1)

            for m in range(KD):
                for name, pair, done, freed in (("ar", 0, "ar_done", "ar_copied"), ("ag", 1, "ag_done", "ag_gelu")):
                    name += str(m // 4)
                    if m % 4 == 0:
                        pe.wait_ge(ring_in[slot_of[name]], count_of[name])
                    if m >= 1:
                        pe.wait_ge(S[freed], m)
                    elif pair == 0:
                        pe.wait_ge(S["tok_copied"], TT)
                    else:
                        turn_heads(TT - 1)
                    for k in range(KD):
                        r = two_halves(pair, w8(name)[:, k, (m % 4) * P:(m % 4 + 1) * P], xn[:, k, :],
                                       k == 0, k == KD - 1)
                    r.then_inc(S[done], 1)
                if m >= 1:
                    block_gates(m - 1)
            block_gates(KD - 1)

            def hidden_samples(v):
                xs = chunk(("xsk", "xsv")[v], 2).rearrange("p (g l c) -> p g l c", g=NPAGES, l=2 * LP)
                w1 = chunk(("w1k", "w1v")[v]).rearrange("p (x l f) -> p x l f", x=2, l=LP)
                if v == 0:
                    pe.wait_ge(S["xsk_in"], 16 * NPAGES)
                else:
                    pe.wait_ge(S["xsv_in"], 8 * NPAGES)
                    pe.wait_ge(S["xsv_in_pool"], 8 * NPAGES)
                name = ("w1k", "w1v")[v]
                pe.wait_ge(ring_in[slot_of[name]], count_of[name])
                for f in range(2):
                    for h in range(2):
                        u = 4 * v + 2 * f + h
                        q = u % 3
                        if u >= 3:
                            pe.wait_ge(S["gh_raw"], u - 2)
                        for x in range(2):
                            for l in range(LP):
                                r = mm(bank[:, 2 * q + x, :], w1[:, x, l, f * P:(f + 1) * P], xs[:, :, 2 * l + h, :],
                                       start=l == 0, stop=l == LP - 1)
                        r.then_inc(S["cs_done"], 1)

            def hidden_prompt(v):
                w1 = chunk(("w1k", "w1v")[v]).rearrange("p (x l f) -> p x l f", x=2, l=LP)
                pe.wait_ge(S["xp_ready"], v + 1)
                for f in range(2):
                    if v or f:
                        pe.wait_ge(S["ghp_raw"], 2 * v + f)
                    for x in range(2):
                        for l in range(LP):
                            r = mm(bank[:, 6, 66 * x:66 * x + 66], w1[:, x, l, f * P:(f + 1) * P], xp[:, v, l, :],
                                   start=l == 0, stop=l == LP - 1)
                    r.then_inc(S["cp_done"], 1)

            pe.wait_ge(S["ti_ready"], KD)
            pe.wait_ge(S["th_ready"], KD)
            pe.wait_ge(S["ag_gelu"], KD)
            for t in range(QT_N):
                r = pe.transpose(bank[:, 7, t * P:(t + 1) * P], kvraw[:, t, VC:VC + P], ident[:, :])
            r.then_inc(S["vt_done"], 1)
            hidden_samples(0)
            hidden_prompt(0)
            hidden_samples(1)
            hidden_prompt(1)
            pe.wait_ge(S["w2_in"], 16)
            pe.wait_ge(S["gh_gelu"], 2)
            pe.wait_ge(S["gh_raw"], 8)
            pads = ((HD, 3 * HD), (0, 2 * HD))
            for x in range(4):
                f, h = divmod(x, 2)
                a, b = pads[h]
                mm(bank[:, 0, :], w2[:, 0, f, a:b], gh[:, 0, f, h, :], start=x == 0, stop=x == 3)
            for x in range(4):
                f, h = divmod(x, 2)
                a, b = pads[h]
                r = mm(bank[:, 1, 0:32], w2[:, 0, f, a:b], ghp[:, 0, f, h * 32:(h + 1) * 32], start=x == 0, stop=x == 3)
            r.then_inc(S["ck_done"], 1)
            pe.wait_ge(S["gh_gelu"], 4)
            for t in range(4):
                for h in range(2):
                    for f in range(2):
                        mm(bank[:, 2, t * P + h * HD:t * P + (h + 1) * HD], gh[:, 1, f, h, t * P:(t + 1) * P],
                           w2[:, 1, f, HD:2 * HD], start=f == 0, stop=f == 1)
            pe.wait_ge(S["hrep_ready"], 1)
            for h in range(2):
                for f in range(2):
                    r = mm(bank[:, 3, h * HD:(h + 1) * HD], hrep[:, f, h, :, :].rearrange("p r c -> p (r c)"),
                           w2[:, 1, f, HD:2 * HD], start=f == 0, stop=f == 1)
            r.then_inc(S["ck_done"], 1)

            def scores(i):
                kind, qt, b, g = items[i]
                if kind == "out":
                    return
                if i >= 2 and items[i - 2][0] == "full":
                    pe.wait_ge(S["att_p"], n_full[i - 2])
                elif i >= 2 and items[i - 2][0] == "cmp":
                    pe.wait_ge(S["att_pc"], n_cmp[i - 2])
                s0 = 2 * (i % 2)
                q = slice(qt * P, (qt + 1) * P)
                for kv in range(NKV):
                    r0 = slice(HD * kv, HD * (kv + 1))
                    if kind == "cmp":
                        for gg in range(NG):
                            r = mm(bank[:, s0 + kv, gg * 32:gg * 32 + 32], qT[r0, gg, q], ckTp[r0, :], start=True, stop=True)
                    else:
                        r = mm(bank[:, s0 + kv, 0:(qt + 1) * P], qT[r0, g, q], kT[r0, b, 0:(qt + 1) * P],
                               start=True, stop=True)
                r.then_inc(S["att_s"], 1)

            def turn(i):
                kind, qt, b, g = items[i]
                if kind == "out":
                    pe.wait_ge(S["att_o"], (1 + 2 * NG) * (qt + 1))
                elif kind == "full":
                    pe.wait_ge(S["att_p"], n_full[i])
                else:
                    pe.wait_ge(S["att_pc"], n_cmp[i])
                if i >= 1:
                    pe.wait_ge(S["att_ta"], i)
                if kind == "out":
                    for gg in range(NG):
                        r = pe.transpose(bank[:, 4, gg * P:(gg + 1) * P], OA[qt % 2][:, gg, :, :].rearrange("p v e -> p (v e)"),
                                         ident[:, :])
                elif kind == "cmp":
                    for kv in range(NKV):
                        r = pe.transpose(bank[:, 4, kv * P:(kv + 1) * P], PR[:, i % 2, 0, kv * P:(kv + 1) * P], ident[:, :])
                else:
                    for kv in range(NKV):
                        for t in range(qt + 1):
                            r = pe.transpose(bank[:, 4 + kv, t * P:(t + 1) * P], PR[:, i % 2, kv, t * P:(t + 1) * P],
                                             ident[:, :])
                r.then_inc(S["att_pa"], 1)

            def values(i):
                kind, qt, b, g = items[i]
                if kind == "out":
                    return
                pe.wait_ge(S["att_ta"], i + 1)
                if n_v[i] >= 3:
                    pe.wait_ge(S["att_o"], n_v[i] - 2)
                o = 6 + n_v[i] % 2
                if kind == "cmp":
                    for kv in range(NKV):
                        r = mm(bank[:, o, kv * 256:(kv + 1) * 256], PT[:, i % 2, 0, kv * P:(kv + 1) * P],
                               cvp[:, kv, :, :].rearrange("p g e -> p (g e)"), start=True, stop=True)
                else:
                    for kv in range(NKV):
                        for t in range(qt + 1):
                            c = VC + b * P + kv * HD
                            r = mm(bank[:, o, kv * HD:(kv + 1) * HD], PT[:, i % 2, kv, t * P:(t + 1) * P],
                                   kvraw[:, t, c:c + HD], start=t == 0, stop=t == qt)
                r.then_inc(S["att_pv"], 1)

            R = slice(0, NROW)

            def sample_scores():
                pe.wait_ge(S["smp_dve"], 1)
                mm(bank[R, 0, :], qbd[:, :], ckT[:, :], start=True, stop=True)
                for b in (0, 1):
                    mm(bank[R, 1, b * NSA:(b + 1) * NSA], qbd[:, :], kT[:, 1 + b, NPR:NT], start=True, stop=True)
                for b in range(3):
                    if b:
                        mm(bank[R, 1, 128 + b * P:128 + (b + 1) * P], emat[0:NSA, :], kvraw[0:NSA, QT_N, VC + b * P:VC + (b + 1) * P],
                           start=True, stop=True)
                mm(bank[R, 1, 32:32 + 24], emat[0:NSA, :], kvraw[0:NSA, QT_N, KVC:KVC + 24], start=True, stop=True)\
                    .then_inc(S["smp_pe"], 1)
                kslc = chunk("kslc", 2)
                pe.wait_ge(S["kslc_in"], 16 * NPAGES)
                for h in range(2):
                    for n in range(NSA):
                        r = mm(bank[R, 2 + h, :], qz[:, n * NROW:(n + 1) * NROW], kslc[:, n * PAST + h * 512:n * PAST + (h + 1) * 512],
                               start=n == 0, stop=n == NSA - 1)
                r.then_inc(S["smp_pe"], 1)
                pe.wait_ge(ring_in[slot_of["kwin"]], count_of["kwin"])
                kwin = chunk("kwin")
                for n in range(NSA):
                    r = mm(bank[R, 5, :], qz[:, n * NROW:(n + 1) * NROW], kwin[:, n * WIN:(n + 1) * WIN],
                           start=n == 0, stop=n == NSA - 1)
                r.then_inc(S["smp_pe"], 1)

            pe.wait_ge(S["ck_copied"], 2 * NG)
            pe.wait_ge(S["ck_act"], 1)
            scores(0)
            for i in range(len(items)):
                if i + 1 < len(items):
                    scores(i + 1)
                if i == len(items) - 1:
                    values(i - 1)
                    sample_scores()
                    turn(i)
                else:
                    turn(i)
                    if i >= 1:
                        values(i - 1)

            pe.wait_ge(S["att_ta"], len(items))
            pe.wait_ge(S["smp_dve"], 2)
            for t in range(4):
                pe.transpose(bank[:, 6, t * NROW:(t + 1) * NROW], sw[R, t * P:(t + 1) * P], ident[R, R])
            mm(bank[R, 4, 0:64], rmat[R, :], sw[R, 512:576], start=True, stop=True).then_inc(S["smp_pe"], 1)
            pe.wait_ge(S["smp_dve"], 3)
            for t in range(4):
                r = mm(bank[R, 7, 0:P], PT[:, 0, 0, t * NROW:(t + 1) * NROW], cv[:, t, :], start=t == 0, stop=t == 3)
            r.then_inc(S["smp_pe"], 1)
            vslc = chunk("vslc", 2).rearrange("p (g c) -> p g c", g=NPAGES)
            vwin = chunk("vwin").rearrange("p (g c) -> p g c", g=NSA * 4)
            for b, (tiles, vals) in enumerate(((4, vwin), (NPG, vslc))):
                pe.wait_ge(S["smp_act"], 2 + b)
                for t in range(tiles):
                    r = pe.transpose(bank[:, 6, t * NROW:(t + 1) * NROW], sw[R, t * P:(t + 1) * P], ident[R, R])
                r.then_inc(S["smp_pe"], 1)
                pe.wait_ge(S["smp_dve"], 4 + b)
                if b == 0:
                    pe.wait_ge(S["vwin_in"], 16 * NSA)
                else:
                    pe.wait_ge(S["vslc_in"], 16 * NPAGES)
                for n in range(NSA):
                    for t in range(tiles):
                        r = mm(bank[R, 2 * b + n // 4, (n % 4) * P:(n % 4 + 1) * P], PT[:, 0, 0:2, :].rearrange("p a k -> p (a k)")[:, t * NROW:(t + 1) * NROW],
                               vals[:, n * tiles + t, :], start=t == 0, stop=t == tiles - 1)
                r.then_inc(S["smp_pe"], 1)

            for m in range(KD):
                c = slice((m % 4) * P, (m % 4 + 1) * P)
                for x, (name, done, ks) in enumerate((("ga", "ga_done", KD), ("pa", "pa_done", KD),
                                                      ("gb", "gb_done", KD), ("pb", "pb_done", NG))):
                    name += str(m // 4)
                    if m % 4 == 0:
                        pe.wait_ge(ring_in[slot_of[name]], count_of[name])
                    if m >= 1:
                        if x % 2 == 0:
                            pe.wait_ge(S["sg_ready"], 2 * m - 1 + x // 2)
                        else:
                            pe.wait_ge(S["m_ready"], m)
                    if m == 0 and x == 3:
                        pe.wait_ge(S["smp_dve"], 8)
                    elif m == 0 and x == 0:
                        pe.wait_ge(S["smp_dve"], 6)
                    w = chunk(name)[:, 0:ks * 512].rearrange("p (k n) -> p k n", k=ks)
                    src = {"pa": Y, "pb": oT}.get(name[:2], xn)
                    for k in range(ks):
                        r = two_halves(x, w[:, k, c], src[:, k, :], k == 0, k == ks - 1)
                    r.then_inc(S[done], 1)
                    if m == 0 and x == 0:
                        pe.wait_ge(S["smp_dve"], 7)
                        pe.transpose(bank[0:HD, 7, 0:NROW], oS[R, :], ident[R, R]).then_inc(S["smp_pe"], 1)

            def out_rows(t):
                if t >= 2:
                    pe.wait_ge(S["xm_ready"], t - 1)
                for h in range(2):
                    w = w8(f"wo{h}")
                    if t == 0:
                        pe.wait_ge(ring_in[slot_of[f"wo{h}"]], count_of[f"wo{h}"])
                    for k in range(KD):
                        r = mm(bank[0:RN, 6 * (t % 2) + h, :], mT[:, k, t * RN:(t + 1) * RN], w[:, k, :],
                               start=k == 0, stop=k == KD - 1)
                r.then_inc(S["wo_done"], 1)

            def places(t):
                pe.wait_ge(S["m4_ready"], t + 1)
                if t == RT - 1:
                    pe.wait_ge(S["ent_ready"], t)
                for u in range(t + 1):
                    lhs = tri if u == t else onesm[:, 0:RN]
                    r = mm(bank[0:RN, 5, P:P + NE], lhs[0:RN, :], m4[0:RN, u, :], start=u == 0, stop=u == t)
                if t == RT - 1:
                    for u in range(RT):
                        r = mm(bank[0:RN, 5, P + NE:P + 2 * NE], onesm[0:RN, 0:RN], m4[0:RN, u, :],
                               start=u == 0, stop=u == RT - 1)
                r.then_inc(S["pos_done"], 1)

            def turn_tile(t):
                pe.wait_ge(S["t_ready"], t + 1)
                if t >= 2:
                    pe.wait_ge(S["y0_ready"], t - 1)
                for k in range(KD):
                    r = pe.transpose(bank[:, 2 + k // 4, (k % 4) * P:(k % 4) * P + RN], tn[0:RN, t % 2, k * P:(k + 1) * P],
                                     ident[0:RN, 0:RN])
                r.then_inc(S["t_turned"], 1)

            def logits(t):
                pe.wait_ge(S["t_copied"], t + 1)
                if t >= 1:
                    pe.wait_ge(S["m4_ready"], t)
                for k in range(KD):
                    r = mm(bank[0:RN, 4, t * NE:(t + 1) * NE], tT[:, k, 0:RN], rwt[:, k, :], start=k == 0, stop=k == KD - 1)
                r.then_inc(S["lg_done"], 1)

            def turn_gates(t):
                pe.wait_ge(S["gd_ready"], t + 1)
                pe.wait_ge(S["ent_ready"], t + 1)
                if t >= RT - 2:
                    pe.wait_ge(S["ovf_ready"], 1)
                pe.transpose(bank[0:NE, 5, 0:RN], gd[t % 2][0:RN, :], ident[0:RN, 0:RN]).then_inc(S["gd_turned"], 1)

            def down_biases(t):
                pe.wait_ge(S["gd_copied"], t + 1)
                if t == RT - 1:
                    pe.wait_ge(S["y0_ready"], t)
                for h in range(2):
                    r = mm(bank[0:RN, 2 + h, :], gdT[0:NE, 0:RN], bdn[:, h * 512:(h + 1) * 512], start=True, stop=True)
                r.then_inc(S["bd_done"], 1)

            pe.wait_ge(S["m_ready"], KD)
            for t in range(RT + 2):
                if t < RT:
                    out_rows(t)
                if t == 1:
                    pe.wait_ge(S["router_in"], ROUTER_IN)
                if 2 <= t <= RT:
                    places(t - 2)
                if 1 <= t <= RT:
                    turn_tile(t - 1)
                if 2 <= t < RT:
                    turn_gates(t - 2)
                if 1 <= t <= RT:
                    logits(t - 1)
                if t == RT:
                    places(RT - 1)
                if t >= RT:
                    turn_gates(t - 2)
                if t >= 2:
                    down_biases(t - 2)

            def turn_rows(n, par):
                pe.wait_ge(S["xg_in"], 16 * n + 16)
                pe.wait_ge(S["xt_ready"], n + 1)
                for k in range(KD):
                    r = pe.transpose(bank[:, 6 + k // 4, (k % 4) * P:(k % 4 + 1) * P], GX[par][:, k * P:(k + 1) * P], ident[:, :])
                r.then_inc(S["x_turned"], 1)

            def block_of(n, par, following):
                for c in range(4):
                    pe.wait_ge(ring_in[eslot[c]], 16 * n + 16 + ebase[c])
                    if c == 0:
                        pe.wait_ge(S["xt_ready"], n + 2)
                    pe.wait_ge(S["up_read"], 4 * n + c + 1)
                    w = ring[:, eslot[c] * SLOT:(eslot[c] + 1) * SLOT].rearrange("p (k n) -> p k n", k=KD)
                    for f in range(4):
                        for k in range(KD):
                            r = mm(bank[:, c, f * P:(f + 1) * P], w[:, k, f * P:(f + 1) * P], XT[par][:, k, :],
                                   start=k == 0, stop=k == KD - 1)
                    r.then_inc(S["ring_used"], 1)
                for c in (4, 5):
                    pe.wait_ge(S["wl_ready"], 2 * n + c - 3)
                    pe.wait_ge(S["hl_ready"], 2 * n + c - 3)
                    if c == 4:
                        pe.wait_ge(S["y_scaled"], n + 1)
                    elif following:
                        turn_rows(n + 1, 1 - par)
                    wl = expert_slot_low(c).rearrange("p (f n) -> p f n", f=4)
                    wh = WH[c - 4].rearrange("p (f n) -> p f n", f=4)
                    for f in range(4):
                        k = 4 * (c - 4) + f
                        for h in range(2):
                            cols = slice(h * 512, (h + 1) * 512)
                            for x, (a, w) in enumerate(((HH, wh), (HH, wl), (HL, wh))):
                                r = mm(bank[:, 4 + h, :], a[:, k, :], w[:, f, cols],
                                       start=k == 0 and x == 0, stop=k == KD - 1 and x == 2)
                    r.then_inc(S["ring_used"], 1)

            pe.wait_ge(S["xm_ready"], RT)
            turn_rows(0, 0)
            pe.wait_ge(S["y0_ready"], RT)
            with pe.Fori(0, NE // 2 - 1) as pair:
                block_of(2 * pair, 0, True)
                block_of(2 * pair + 1, 1, True)
            block_of(NE - 2, 0, True)
            block_of(NE - 1, 1, False)
            pe.wait_ge(S["ovf_ready"], 1)
            most = pe.value_load(ovf[0:1, 1:2].bitcast(I32), min_val=0, max_val=NT)
            with pe.If(most > P):
                with pe.Fori(0, NE) as e:
                    for b in range(4):
                        turn_rows(4 * e + (NE + b), b % 2)
                        block_of(4 * e + (NE + b), b % 2, False)

        @block.scalar
        def _(act):
            fn = act.activation
            mine = Steps(act, S["act_steps"])
            act.dma_start(small[:, 0:d["small"].shape[1]], d["small"]).then_inc(S["small_in"], 16)
            for k in range(KD):
                if k % 2 == 0:
                    act.wait_ge(x_in[k // 2], 16)
                fn(xsq[:, k, :], xn[:, k, :], ACT.Square).then_inc(S["x_squared"], 1)
            act.wait_ge(S["x_summed"], 1)
            act.wait_ge(S["lam_ready"], 1)
            fn(split(rstd), halves(3), ACT.Sqrt, scale=1.0 / D, bias=eps1[:, 0:1]).then_inc(S["x_root"], 1)
            fn(lt[:, 1, :], lt[:, 0, :], ACT.Exp, scale=-1.0).then_inc(S["lam_exp"], 1)
            def turned_queries(t):
                act.wait_ge(S["qk_turned"], t + 1)
                m = fraction(t)
                fn(qT[:, :, t * P:t * P + m], bank[:, 6, 0:NG * m].rearrange("p (g n) -> p g n", g=NG), ACT.Copy)\
                    .then_inc(S["qk_act"], 1)

            for t in range(TT):
                m = fraction(t)
                b = 3 * (t % 2)
                act.wait_ge(S["tok_done"], t + 1)
                fn(qraw[0:m, t, :], bank[0:m, b, :], ACT.Copy)
                fn(kvraw[0:m, t, 0:512], bank[0:m, b + 1, :], ACT.Copy)
                fn(kvraw[0:m, t, 512:792], bank[0:m, b + 2, 0:280], ACT.Copy).then_inc(S["tok_copied"], 1)
                act.wait_ge(S["ss_ready"], t + 1)
                fn(rsq[0:m, t, :], ssq[0:m, t, :], ACT.Sqrt, scale=1.0 / HD, bias=eps1[0:m, 0:1]).then_inc(S["rs_root"], 1)
                if t >= 1:
                    turned_queries(t - 1)

            def gates_of(m):
                j = m % 4
                act.wait_ge(S["r_done"], m + 1)
                if m >= 4:
                    act.wait_ge(S["y_ready"], j + 1)
                fn(split(A[:, j, :]), halves(2), ACT.Tanh, scale=0.5, bias=hb[:, 0, m:m + 1]).then_inc(S["th_ready"], 1)
                act.wait_ge(S["i_done"], m + 1)
                fn(split(IX[:, j, :]), halves(3), ACT.Tanh, scale=0.5, bias=hb[:, 1, m:m + 1]).then_inc(S["ti_ready"], 1)

            def decays(g):
                act.wait_ge(S["th_ready"], 4 * g + 4)
                for j in range(4):
                    m = 4 * g + j
                    mine(fn(V[:, j, :], A[:, j, :], ACT.Tanh, scale=c2[:, 1, m:m + 1], bias=c2[:, 1, m:m + 1]))
                for j in range(4):
                    m = 4 * g + j
                    mine.settle()
                    fn(A[:, j, :], A[:, j, :], ACT.Exp, scale=c2[:, 0, m:m + 1], bias=c2[:, 0, m:m + 1])\
                        .then_inc(S["decay_ready"], 1)
                for j in range(4):
                    act.wait_ge(S["gap_ready"], 4 * g + j + 1)
                    fn(V[:, j, :], V[:, j, :], ACT.Sqrt, scale=0.25).then_inc(S["gap_root"], 1)

            act.wait_ge(S["lam_ready"], 2)
            for m in range(KD):
                act.wait_ge(S["ar_done"], m + 1)
                if m >= 2:
                    act.wait_ge(S["xc_ready"], m - 1)
                fn(xpp[:, m % 2, 3:3 + HN], bank[:, 0, 0:HN], ACT.Copy)
                fn(xpp[:, m % 2, 3 + HN:3 + NPR], bank[:, 1, 0:NPR - HN], ACT.Copy)
                fn(xps[:, m, :, 3], bank[:, 1, NPR - HN:HN], ACT.Copy).then_inc(S["ar_copied"], 1)
                if m == 0:
                    turned_queries(TT - 1)
                act.wait_ge(S["ag_done"], m + 1)
                fn(split(Y[:, m, :]), halves(1), ACT.Gelu_apprx_tanh).then_inc(S["ag_gelu"], 1)
                if m >= 1:
                    gates_of(m - 1)
                if m == 4:
                    decays(0)
            gates_of(KD - 1)
            decays(1)

            def part_copies(v):
                for u in range(4 * v, 4 * v + 4):
                    act.wait_ge(S["cs_done"], u + 1)
                    if u >= 2:
                        act.wait_ge(S["gh_raw"], u - 1)
                    else:
                        act.wait_ge(S["y_ready"], KD)
                    fn(p1c[:, u % 2, :], bank[:, 2 * (u % 3) + 1, :], ACT.Copy).then_inc(S["p1_copied"], 1)

            def prompt_parts(v):
                for f in range(2):
                    act.wait_ge(S["cp_done"], 2 * v + f + 1)
                    act.wait_ge(S["gh_raw"], 4 * v + 4)
                    if v or f:
                        act.wait_ge(S["ghp_raw"], 2 * v + f)
                    fn(p1c[:, 0, 0:66], bank[:, 6, 66:132], ACT.Copy).then_inc(S["pp_copied"], 1)

            def gelus(v):
                act.wait_ge(S["ghp_raw"], 2 * v + 2)
                for f in range(2):
                    bias = cbias[:, 2 * v + f:2 * v + f + 1]
                    fn(ghp[:, v, f, :], ghp[:, v, f, :], ACT.Gelu_apprx_tanh, bias=bias)
                    x = gh[:, v, f, :, :]
                    fn(x, x, ACT.Gelu_apprx_tanh, bias=bias).then_inc(S["gh_gelu"], 1)

            part_copies(0)
            prompt_parts(0)
            gelus(0)
            part_copies(1)
            prompt_parts(1)
            gelus(1)
            for t in range(TT):
                m = fraction(t)
                r = fn(kvraw[0:m, t, KVC:KVC + 24], kvraw[0:m, t, KVC:KVC + 24], ACT.Tanh, scale=0.5)
            r.then_inc(S["gates_t"], 1)

            def exponentials(i):
                kind, qt, b, g = items[i]
                if kind == "out":
                    return
                if i >= 2:
                    act.wait_ge(S["att_pa"], i - 1)
                if kind == "cmp":
                    act.wait_ge(S["att_ce"], n_cmp[i])
                    fn(PR[:, i % 2, 0, 0:256], PR[:, i % 2, 0, 0:256], ACT.Exp, scale=SCALE).then_inc(S["att_cs"], 1)
                    return
                act.wait_ge(S["att_max"], n_full[i])
                n = (qt + 1) * P
                for kv in range(NKV):
                    r = fn(PR[:, i % 2, kv, 0:n], bank[:, 2 * (i % 2) + kv, 0:n], ACT.Exp, scale=SCALE,
                           bias=stat[:, 4 * (i % 2) + kv:4 * (i % 2) + kv + 1],
                           accum_out=stat[:, 4 * (i % 2) + 2 + kv:4 * (i % 2) + 3 + kv])
                r.then_inc(S["att_p"], 1)

            def turned(i):
                kind, qt, b, g = items[i]
                act.wait_ge(S["att_pa"], i + 1)
                if kind == "out":
                    fn(oT[:, :, qt * P:(qt + 1) * P], bank[:, 4, :].rearrange("p (g t) -> p g t", g=NG), ACT.Copy)\
                        .then_inc(S["att_ta"], 1)
                    return
                if i >= 2:
                    act.wait_ge(S["att_pv"], n_v[i - 2])
                if kind == "cmp":
                    fn(PT[:, i % 2, 0, 0:256], bank[:, 4, 0:256], ACT.Copy).then_inc(S["att_ta"], 1)
                else:
                    n = (qt + 1) * P
                    fn(PT[:, i % 2, :, 0:n], bank[:, 4:6, 0:n], ACT.Copy).then_inc(S["att_ta"], 1)

            act.wait_ge(S["ck_done"], 2)
            fn(ckT[:, :], bank[:, 0, :], ACT.Copy)
            fn(cv[:, :, :], bank[:, 2, :].rearrange("p (t c) -> p t c", t=4), ACT.Copy).then_inc(S["ck_act"], 1)
            act.wait_ge(S["ck_copied"], 2 * NG)
            exponentials(0)
            R = slice(0, NROW)
            for i in range(len(items)):
                if i == len(items) - 1:
                    act.wait_ge(S["smp_max"], 1)
                    fn(sw[R, 0:512], sw[R, 0:512], ACT.Exp, scale=SCALE, bias=stat[R, 8:9], accum_out=stat[R, 9:10])\
                        .then_inc(S["smp_act"], 1)
                turned(i)
                if i + 1 < len(items):
                    exponentials(i + 1)

            for b in (2, 1):
                act.wait_ge(S["smp_max"], 4 - b)
                fn(stat[R, 12:13], stat[R, 11:12], ACT.Exp, scale=SCALE, bias=stat[R, 8:9])
                if b == 1:
                    src, out = sw[R, :], sw[R, :]
                else:
                    src, out = bank[R, 5, 1:WIN], sw[R, 1:WIN]
                fn(out, src, ACT.Exp, scale=SCALE, bias=stat[R, 8:9], accum_out=stat[R, 9:10]).then_inc(S["smp_act"], 1)

            for m in range(KD):
                for x, done in ((0, "ga_done"), (1, "gb_done")):
                    act.wait_ge(S[done], m + 1)
                    if m >= 1:
                        act.wait_ge(S["m_ready"], m)
                    fn(split(sg[:, x, :]), halves(2 * x), ACT.Tanh, scale=0.5).then_inc(S["sg_ready"], 1)
            def turned_gates(t):
                act.wait_ge(S["gd_turned"], t + 1)
                if t >= 1:
                    act.wait_ge(S["bd_done"], t)
                fn(gdT[0:NE, 0:RN], bank[0:NE, 5, 0:RN], ACT.Copy).then_inc(S["gd_copied"], 1)

            for t in range(RT + 2):
                if 1 <= t <= RT:
                    act.wait_ge(S["t_turned"], t)
                    if t >= 2:
                        act.wait_ge(S["lg_done"], t - 1)
                    fn(tT[:, :, 0:RN], bank[:, 2:4, :].rearrange("p b (k t) -> p (b k) t", k=4)[:, :, 0:RN], ACT.Copy)\
                        .then_inc(S["t_copied"], 1)
                if 2 <= t < RT:
                    turned_gates(t - 2)
                if t < RT:
                    act.wait_ge(S["xm_ready"], t + 1)
                    fn(sq_rows[0:RN, :], xm[0:RN, t % 3, :], ACT.Square, accum_out=stat[0:RN, 0:1]).then_inc(S["ss2"], 1)
                    act.wait_ge(S["ss2"], t + 1)
                    fn(stat[0:RN, 1:2], stat[0:RN, 0:1], ACT.Sqrt, scale=1.0 / D, bias=eps1[0:RN, 0:1]).then_inc(S["rstd2"], 1)
                if 1 <= t <= RT:
                    act.wait_ge(S["ex_in"], t)
                    x = ixf[0:RN, t - 1, :]
                    fn(x, x, ACT.Exp, bias=stat[0:RN, 2:3], accum_out=stat[0:RN, 3:4]).then_inc(S["ex_done"], 1)
                if t >= RT:
                    turned_gates(t - 2)

            act.sem_inc(S["xt_ready"], 1)
            act.sem_inc(S["y_scaled"], 1)

            def turned_rows(n, par):
                act.wait_ge(S["x_turned"], n + 1)
                fn(XT[par][:, :, :], bank[:, 6:8, :].rearrange("p b (k t) -> p (b k) t", k=4), ACT.Copy)\
                    .then_inc(S["xt_ready"], 1)

            def block_of(n, par, following):
                for hf in range(2):
                    act.wait_ge(S["up_read"], 4 * n + 2 * hf + 5)
                    fn(SG[hf], AA[hf], ACT.Sigmoid, scale=ALPHA).then_inc(S["sig_ready"], 1)
                    if hf == 0:
                        act.wait_ge(ring_in[eslot[4]], 16 * n + 16 + ebase[4])
                        fn(WH[0], expert_slot(4), ACT.Copy).then_inc(S["wh_ready"], 1)
                    act.wait_ge(S["h_ready"], 2 * n + hf + 1)
                    fn(HH[:, 4 * hf:4 * hf + 4, :].rearrange("p f t -> p (f t)"), UU[hf], ACT.Copy)\
                        .then_inc(S["hh_ready"], 1)
                    if hf == 0:
                        act.wait_ge(ring_in[eslot[5]], 16 * n + 16 + ebase[5])
                        fn(WH[1], expert_slot(5), ACT.Copy).then_inc(S["wh_ready"], 1)
                if following:
                    turned_rows(n + 1, 1 - par)
                act.wait_ge(S["ring_used"], 6 * n + 6)
                fn(YR[par].rearrange("p (b n) -> p b n", b=2), bank[:, 4:6, :], ACT.Copy, scale=entf[par][:, 1:2])\
                    .then_inc(S["y_scaled"], 1)

            turned_rows(0, 0)
            with act.Fori(0, NE // 2 - 1) as pair:
                block_of(2 * pair, 0, True)
                block_of(2 * pair + 1, 1, True)
            block_of(NE - 2, 0, True)
            block_of(NE - 1, 1, False)
            act.wait_ge(S["ovf_ready"], 1)
            most = act.value_load(ovf[0:1, 1:2].bitcast(I32), min_val=0, max_val=NT)
            with act.If(most > P):
                with act.Fori(0, NE) as e:
                    for b in range(4):
                        turned_rows(4 * e + (NE + b), b % 2)
                        block_of(4 * e + (NE + b), b % 2, False)

        @block.vector
        def _(dve):
            v = nc.vector
            mine = Steps(dve, S["dve_steps"])

            def one(ins, sem=None):
                mine(ins, sem)
                mine.settle()

            one(v.memset(eps1[:, :], EPS))
            dve.wait_ge(S["small_in"], 16)
            one(v.tensor_scalar(lt[:, 0, :], lruv[:, :, 7], -1.0, None, ALU.mult))
            one(v.tensor_tensor(lt[:, 0, :], lt[:, 0, :], lruv[:, :, 7], ALU.max))
            v.tensor_scalar(negc[:, :, :], cmask[:, :, :], 1.0, -NEG, ALU.subtract, ALU.mult).then_inc(S["lam_ready"], 1)
            dve.wait_ge(S["x_root"], 1)
            one(v.reciprocal(rstd, rstd))
            for k in range(KD):
                v.scalar_tensor_tensor(xn[:, k, :], xn[:, k, :], gmix[:, k:k + 1], rstd, ALU.mult, ALU.mult)\
                    .then_inc(S["xn_ready"], 1)
            dve.wait_ge(S["lam_exp"], 1)
            one(v.tensor_scalar(lt[:, 2, :], lt[:, 1, :], 2.0, None, ALU.add))
            one(v.reciprocal(lt[:, 2, :], lt[:, 2, :]))
            one(v.tensor_tensor(lt[:, 1, :], lt[:, 1, :], lt[:, 2, :], ALU.mult))
            one(v.tensor_tensor(lt[:, 2, :], lt[:, 1, :], lt[:, 1, :], ALU.mult))
            one(v.memset(lt[:, 3, :], 1.0 / 17))
            for k in range(15, 0, -2):
                one(v.tensor_tensor(lt[:, 3, :], lt[:, 3, :], lt[:, 2, :], ALU.mult))
                one(v.tensor_scalar(lt[:, 3, :], lt[:, 3, :], 1.0 / k, None, ALU.add))
            one(v.tensor_tensor(lt[:, 1, :], lt[:, 1, :], lt[:, 3, :], ALU.mult))
            one(v.tensor_scalar(lt[:, 2, :], lruv[:, :, 7], -1.0, 0.0, ALU.mult, ALU.max))
            one(v.scalar_tensor_tensor(lt[:, 1, :], lt[:, 1, :], 2.0, lt[:, 2, :], ALU.mult, ALU.add))
            one(v.tensor_scalar(c2[:, 0, :], lt[:, 1, :], -4.0, None, ALU.mult))
            one(v.tensor_scalar(c2[:, 1, :], lt[:, 1, :], 4.0, None, ALU.mult))
            v.tensor_scalar(hb[:, :, :], lruv[:, :, 5:7].rearrange("p m x -> p x m"), 0.5, None, ALU.mult)\
                .then_inc(S["lam_ready"], 1)
            def turned_keys(t):
                dve.wait_ge(S["qk_turned"], t + 1)
                m = fraction(t)
                v.tensor_copy(kT[:, :, t * P:t * P + m], bank[:, 7, 0:3 * m].rearrange("p (b n) -> p b n", b=3))\
                    .then_inc(S["qk_dve"], 1)

            dve.wait_ge(S["gains_in"], 16)
            for t in range(TT):
                m = fraction(t)
                dve.wait_ge(S["tok_copied"], t + 1)
                q = qraw[0:m, t, :].rearrange("p (h c) -> p h c", h=NH)
                kk = kvraw[0:m, t, 0:6 * HD].rearrange("p (h c) -> p h c", h=6)
                mine(v.tensor_tensor(sqt[0:m, 0:NH, :], q, q, ALU.mult))
                one(v.tensor_tensor(sqt[0:m, NH:NHN, :], kk, kk, ALU.mult))
                one(v.tensor_reduce(ssq[0:m, t, :], sqt[0:m, :, :], AX, ALU.add), S["ss_ready"])
                dve.wait_ge(S["rs_root"], t + 1)
                one(v.reciprocal(rsq[0:m, t, :], rsq[0:m, t, :]))
                for x, h0_, h1_ in ((q, 0, NH), (kk, NH, NHN)):
                    nh = h1_ - h0_
                    r = rsq[0:m, t, h0_:h1_].rearrange("p (h o) -> p h o", o=1).to_broadcast([m, nh, HD])
                    one(v.tensor_tensor(x, x, r, ALU.mult))
                    one(v.tensor_tensor(x, x, gain[0:m, h0_:h1_, :], ALU.mult))
                    cos = rope[0:m, t, 0:8].rearrange("p (o c) -> p o c", o=1).to_broadcast([m, nh, 8])
                    sin = rope[0:m, t, 8:16].rearrange("p (o c) -> p o c", o=1).to_broadcast([m, nh, 8])
                    x1, x2 = x[:, :, 0:8], x[:, :, 8:16]
                    tmp = [sqt[0:m, 0:nh, 8 * i:8 * i + 8] for i in range(4)]
                    mine(v.tensor_tensor(tmp[0], x1, cos, ALU.mult))
                    mine(v.tensor_tensor(tmp[1], x2, sin, ALU.mult))
                    mine(v.tensor_tensor(tmp[2], x1, sin, ALU.mult))
                    one(v.tensor_tensor(tmp[3], x2, cos, ALU.mult))
                    mine(v.tensor_tensor(x1, tmp[0], tmp[1], ALU.subtract))
                    one(v.tensor_tensor(x2, tmp[2], tmp[3], ALU.add), S["qk_ready"] if nh == 6 else None)
                if t >= 1:
                    turned_keys(t - 1)
            turned_keys(TT - 1)

            def convolve(m):
                b = m % 2
                dve.wait_ge(S["ar_copied"], m + 1)
                if m >= 2:
                    dve.wait_ge(S["i_done"], m - 1)
                w = [lruv[:, m, k:k + 1] for k in range(8)]
                mine(v.tensor_copy(pconv[:, m, :], xpp[:, b, NPR:NPR + 3]))
                mine(v.tensor_scalar(xc[:, b, 0:NPR], xpp[:, b, 0:NPR], w[0], w[4], ALU.mult, ALU.add))
                one(v.tensor_scalar(xc[:, b, NPR:NT], xps[:, m, :, 0], w[0], w[4], ALU.mult, ALU.add))
                for k in range(1, 4):
                    mine(v.scalar_tensor_tensor(xc[:, b, 0:NPR], xpp[:, b, k:k + NPR], w[k], xc[:, b, 0:NPR], ALU.mult, ALU.add))
                    one(v.scalar_tensor_tensor(xc[:, b, NPR:NT], xps[:, m, :, k], w[k], xc[:, b, NPR:NT], ALU.mult, ALU.add),
                        S["xc_ready"] if k == 3 else None)

            def gated_input(m):
                dve.wait_ge(S["ti_ready"], m + 1)
                x = IX[:, m % 4, :]
                one(v.scalar_tensor_tensor(x, x, 1.0, xc[:, m % 2, :], ALU.add, ALU.mult))

            def recur(g):
                tmp = qf[:, 2070:2070 + HN]
                for j in range(4):
                    dve.wait_ge(S["decay_ready"], 4 * g + j + 1)
                    for h in range(2):
                        c = slice(h * HN, (h + 1) * HN)
                        one(v.tensor_tensor(tmp, A[:, j, c], A[:, j, c], ALU.mult))
                        one(v.scalar_tensor_tensor(V[:, j, c], tmp, 1.0, V[:, j, c], ALU.add, ALU.mult),
                            S["gap_ready"] if h else None)
                for j in range(4):
                    m = 4 * g + j
                    dve.wait_ge(S["gap_root"], m + 1)
                    one(v.tensor_tensor(IX[:, j, :], IX[:, j, :], V[:, j, :], ALU.mult))
                    one(v.tensor_tensor(h0[:, m, :], h0[:, m, :], A[:, j, NPR:NT], ALU.mult))
                    one(v.tensor_tensor(IX[:, j, NPR:NT], IX[:, j, NPR:NT], h0[:, m, :], ALU.add))
                    one(v.tensor_tensor_scan(V[:, j, 0:NPR], A[:, j, 0:NPR], IX[:, j, 0:NPR], 0.0, ALU.mult, ALU.add))
                    mine(v.tensor_copy(hout[:, m, 0:1], V[:, j, NPR - 1:NPR]))
                    mine(v.tensor_copy(hout[:, m, 1:9], IX[:, j, NPR:NT]))
                    mine(v.tensor_tensor(Y[:, m, 0:NPR], Y[:, m, 0:NPR], V[:, j, 0:NPR], ALU.mult))
                    one(v.tensor_tensor(Y[:, m, NPR:NT], Y[:, m, NPR:NT], IX[:, j, NPR:NT], ALU.mult), S["y_ready"])

            for b in range(2):
                one(v.memset(xpp[:, b, 0:3], 0.0))
            for m in range(KD):
                convolve(m)
                if m >= 1:
                    gated_input(m - 1)
                if m == 4:
                    recur(0)
            gated_input(KD - 1)
            recur(1)

            def prompt_rows(vv):
                src = kT[:, 0, 0:NPR] if vv == 0 else bank[:, 7, :]
                src = src.rearrange("p (c l two) -> p two l c", c=NCH, l=LP)
                for kv in range(2):
                    for l2 in range(2):
                        mine(v.tensor_copy(xp[l2 * HD:(l2 + 1) * HD, vv, :, kv * NCH:(kv + 1) * NCH],
                                           src[kv * HD:(kv + 1) * HD, l2, :, :]))
                one(v.tensor_copy(xp[:, vv, :, 64:66], posc[:, vv, :, :]), S["xp_ready"])

            dve.wait_ge(S["i_done"], KD)
            prompt_rows(0)
            dve.wait_ge(S["vt_done"], 1)
            prompt_rows(1)
            for vv in range(2):
                for u in range(4 * vv, 4 * vv + 4):
                    f, h = divmod(u % 4, 2)
                    dve.wait_ge(S["p1_copied"], u + 1)
                    out = gh[:, vv, f, h, :].rearrange("p (n c) -> p n c", n=NSA)
                    p0 = bank[:, 2 * (u % 3), :].rearrange("p (n c) -> p n c", n=NSA)
                    p1 = p1c[:, u % 2, :].rearrange("p (n c) -> p n c", n=NSA)
                    mine(v.memset(out[:, :, CHS - 1:CHS], 0.0))
                    one(v.tensor_tensor(out[:, :, 0:CHS - 1], p0[:, :, 0:CHS - 1], p1[:, :, 1:CHS], ALU.add), S["gh_raw"])
                for f in range(2):
                    dve.wait_ge(S["pp_copied"], 2 * vv + f + 1)
                    out = ghp[:, vv, f, :].rearrange("p (v c) -> p v c", v=2)
                    p0 = bank[:, 6, 0:64].rearrange("p (v c) -> p v c", v=2)
                    p1 = p1c[:, 0, 0:64].rearrange("p (v c) -> p v c", v=2)
                    mine(v.memset(out[:, :, NCH - 1:NCH], 0.0))
                    mine(v.tensor_tensor(out[:, :, 0:NCH - 1], p0[:, :, 0:NCH - 1], p1[:, :, 1:NCH], ALU.add))
                    x = cbias[:, 2 * vv + f:2 * vv + f + 1]
                    one(v.tensor_tensor(x, bank[:, 6, 64:65], p1c[:, 0, 65:66], ALU.add), S["ghp_raw"])
            dve.wait_ge(S["gh_gelu"], 4)
            for f in range(2):
                for h in range(2):
                    src = ghp[:, 1, f, h * 32:(h + 1) * 32].rearrange("p (o c) -> p o c", o=1).to_broadcast([P, 4, 32])
                    mine(v.tensor_copy(hrep[:, f, h, :, :], src))
            one(v.memset(cvp[:, :, :, :], 0.0), S["hrep_ready"])
            dve.wait_ge(S["ck_done"], 2)
            mine(v.tensor_copy(ckTp[:, :], bank[:, 1, 0:32]))
            for h in range(2):
                for g in range(NG):
                    r = v.tensor_copy(cvp[32 * g:32 * g + 32, h, g, :], bank[32 * g:32 * g + 32, 3, h * HD:(h + 1) * HD])
                    mine(r, S["ck_copied"])
            mine.settle()
            dve.wait_ge(S["gates_t"], 1)
            for t in range(TT):
                m = fraction(t)
                x = kvraw[0:m, t, KVC:KVC + 24]
                one(v.tensor_scalar(x, x, 0.5, 0.5, ALU.mult, ALU.add))

            def maxima(i):
                kind, qt, b, g = items[i]
                if kind == "out":
                    return
                dve.wait_ge(S["att_s"], n_v[i])
                if kind == "cmp":
                    if i >= 2:
                        dve.wait_ge(S["att_pa"], i - 1)
                    x = PR[:, i % 2, 0, 0:256].rearrange("p (h c) -> p h c", h=NH)
                    vis = negc[:, qt, :].rearrange("p (a o c) -> p a o c", a=1, o=1).to_broadcast([P, NKV, NG, 32])
                    s = bank[:, 2 * (i % 2):2 * (i % 2) + 2, 0:P].rearrange("p v (h c) -> p v h c", h=NG)
                    one(v.tensor_tensor(x.rearrange("p (v h) c -> p v h c", v=NKV), s, vis, ALU.add))
                    one(v.tensor_reduce(stat[:, 16:24], x, AX, ALU.max))
                    mx = stat[:, 16:24].rearrange("p (h o) -> p h o", o=1).to_broadcast([P, NH, 32])
                    one(v.tensor_tensor(x, x, mx, ALU.subtract), S["att_ce"])
                    return
                s = bank[:, 2 * (i % 2):2 * (i % 2) + 2, :]
                diag = s[:, :, qt * P:(qt + 1) * P]
                one(v.tensor_tensor(diag, diag, causal.rearrange("p (o c) -> p o c", o=1).to_broadcast([P, 2, P]), ALU.add))
                st = 4 * (i % 2)
                one(v.tensor_reduce(stat[:, 24:26], s[:, :, 0:(qt + 1) * P], AX, ALU.max))
                if i >= 2 and items[i - 2][0] == "full":
                    dve.wait_ge(S["att_p"], n_full[i - 2])
                one(v.tensor_scalar(stat[:, st:st + 2], stat[:, 24:26], -SCALE, None, ALU.mult), S["att_max"])

            def weights(i):
                kind, qt, b, g = items[i]
                if kind == "cmp":
                    dve.wait_ge(S["att_cs"], n_cmp[i])
                    x = PR[:, i % 2, 0, 0:256].rearrange("p (h c) -> p h c", h=NH)
                    one(v.tensor_tensor(x, x, cmask[:, qt, :].rearrange("p (o c) -> p o c", o=1).to_broadcast([P, NH, 32]), ALU.mult))
                    one(v.tensor_reduce(stat[:, 16:24], x, AX, ALU.add))
                    one(v.tensor_scalar(stat[:, 16:24], stat[:, 16:24], 1e-30, None, ALU.max))
                    one(v.reciprocal(stat[:, 16:24], stat[:, 16:24]))
                    gt = kvraw[:, qt, KVC:KVC + NH].rearrange("p (g v) -> p v g", g=NG)
                    w = stat[:, 16:24].rearrange("p (v g) -> p v g", v=NKV)
                    one(v.tensor_tensor(w, w, gt, ALU.mult))
                    one(v.tensor_tensor(x, x, stat[:, 16:24].rearrange("p (h o) -> p h o", o=1).to_broadcast([P, NH, 32]), ALU.mult),
                        S["att_pc"])
                elif kind == "full":
                    st = 4 * (i % 2)
                    dve.wait_ge(S["att_p"], n_full[i])
                    one(v.reciprocal(stat[:, 26 + 2 * (i % 2):28 + 2 * (i % 2)], stat[:, st + 2:st + 4]))
                    c = KVC + b * NH + g * NKV
                    w = stat[:, 26 + 2 * (i % 2):28 + 2 * (i % 2)]
                    one(v.tensor_tensor(w, w, kvraw[:, qt, c:c + NKV], ALU.mult))

            def outputs(i):
                kind, qt, b, g = items[i]
                if kind == "out":
                    return
                dve.wait_ge(S["att_pv"], n_v[i])
                o = 6 + n_v[i] % 2
                if kind == "cmp":
                    if qt >= 2:
                        dve.wait_ge(S["att_pa"], turned_at[qt - 2] + 1)
                    one(v.tensor_copy(OA[qt % 2][:, :, :, :].rearrange("p g v e -> p v g e"),
                                      bank[:, o, :].rearrange("p (v g e) -> p v g e", v=NKV, g=NG)), S["att_o"])
                    return
                for kv in range(NKV):
                    w = stat[:, 26 + 2 * (i % 2) + kv:27 + 2 * (i % 2) + kv]
                    one(v.scalar_tensor_tensor(OA[qt % 2][:, g, kv, :], bank[:, o, kv * HD:(kv + 1) * HD], w, OA[qt % 2][:, g, kv, :],
                                               ALU.mult, ALU.add), S["att_o"] if kv else None)

            def sample_queries():
                one(v.memset(qbd[:, :], 0.0))
                one(v.memset(qz[:, :], 0.0))
                for kv in range(NKV):
                    r0 = slice(kv * HD, (kv + 1) * HD)
                    one(v.tensor_copy(qbd[r0, :].rearrange("p (n g v) -> p v g n", n=NSA, g=NG)[:, kv, :, :], qT[r0, :, NPR:NT]))
                for n in range(NSA):
                    one(v.tensor_copy(qz[:, n * (NROW + NH):n * (NROW + NH) + NH], qbd[:, n * NH:(n + 1) * NH]),
                        S["smp_dve"] if n == NSA - 1 else None)

            maxima(0)
            for i in range(len(items)):
                if i == len(items) - 4:
                    sample_queries()
                if items[i][0] == "cmp":
                    weights(i)
                if i + 1 < len(items):
                    maxima(i + 1)
                if items[i][0] != "cmp":
                    weights(i)
                if i >= 1:
                    outputs(i - 1)

            R = slice(0, NROW)

            def sel(x, m, w):
                return x.rearrange("p (a o) -> p a o", o=1).to_broadcast([NROW, m, w])

            dve.wait_ge(S["smp_pe"], 1)
            aux = sw[R, 576:576 + 24]
            one(v.tensor_tensor(aux.rearrange("p (b h) -> p b h", b=3), bank[R, 1, 32:56].rearrange("p (b h) -> p b h", b=3),
                                selh[R, :].rearrange("p (o h) -> p o h", o=1).to_broadcast([NROW, 3, NH]), ALU.mult))
            one(v.tensor_reduce(stat[R, 0:3], aux.rearrange("p (b h) -> p b h", b=3), AX, ALU.add))
            one(v.tensor_tensor(aux[:, 0:16].rearrange("p (b n) -> p b n", b=2), bank[R, 1, 0:16].rearrange("p (b n) -> p b n", b=2),
                                sel8[R, :].rearrange("p (o n) -> p o n", o=1).to_broadcast([NROW, 2, NSA]), ALU.mult))
            one(v.tensor_reduce(stat[R, 3:5], aux[:, 0:16].rearrange("p (b n) -> p b n", b=2), AX, ALU.add))
            vn = qf[R, 1600:1728].rearrange("p (b e) -> p b e", b=2)
            for b in range(2):
                x = bank[R, 1, 256 + b * P:256 + (b + 1) * P]
                one(v.tensor_scalar(vn[:, b, :], x[:, 0:HD], selv[R, 0:1], None, ALU.mult))
                one(v.scalar_tensor_tensor(vn[:, b, :], x[:, HD:P], selv[R, 1:2], vn[:, b, :], ALU.mult, ALU.add))
            dve.wait_ge(S["smask_in"], 16)
            one(v.tensor_tensor(sw[R, 0:512], bank[R, 0, :], smask[R, :], ALU.add))
            one(v.tensor_reduce(stat[R, 10:11], sw[R, 0:512], AX, ALU.max))
            one(v.tensor_scalar(stat[R, 8:9], stat[R, 10:11], -SCALE, None, ALU.mult), S["smp_max"])
            dve.wait_ge(S["smp_act"], 1)
            one(v.reciprocal(stat[R, 13:14], stat[R, 9:10]))
            one(v.tensor_scalar(sw[R, 0:512], sw[R, 0:512], stat[R, 13:14], None, ALU.mult))
            one(v.tensor_reduce(sw[R, 512:576], sw[R, 0:512].rearrange("p (n c) -> p c n", n=NSA), AX, ALU.add), S["smp_dve"])

            def branch_max(b):
                if b == 0:
                    dve.wait_ge(S["smp_pe"], 6)
                    one(v.tensor_tensor(sw[R, :].rearrange("p (h j k) -> p h j k", h=2, j=8),
                                        bank[R, 2:4, :].rearrange("p h (j k) -> p h j k", j=8),
                                        four.rearrange("p (h j o) -> p h j o", h=2, o=1).to_broadcast([NROW, 2, 8, 64]), ALU.add))
                    one(v.tensor_reduce(stat[R, 10:11], sw[R, :], AX, ALU.max))
                else:
                    dve.wait_ge(S["smp_pe"], 3)
                    one(v.tensor_reduce(stat[R, 10:11], bank[R, 5, 1:WIN], AX, ALU.max))
                one(v.tensor_tensor(stat[R, 10:11], stat[R, 10:11], stat[R, 3 + b:4 + b], ALU.max))
                one(v.tensor_copy(stat[R, 11:12], stat[R, 3 + b:4 + b]))
                if b:
                    dve.wait_ge(S["smp_pe"], 4)
                    one(v.memset(sw[R, 0:1], 0.0))
                one(v.tensor_scalar(stat[R, 8:9], stat[R, 10:11], -SCALE, None, ALU.mult), S["smp_max"])

            def branch_turned(b, tiles):
                dve.wait_ge(S["smp_act"], 3 - b)
                w, wn = stat[R, 17 + b:18 + b], stat[R, 19 + b:20 + b]
                one(v.tensor_tensor(w, stat[R, 9:10], stat[R, 12:13], ALU.add))
                one(v.reciprocal(w, w))
                one(v.tensor_tensor(w, w, stat[R, 1 + b:2 + b], ALU.mult))
                one(v.tensor_tensor(wn, w, stat[R, 12:13], ALU.mult))
                dve.wait_ge(S["smp_pe"], 8 - 2 * b)
                one(v.tensor_copy(pt[:, 0:tiles * NROW], bank[:, 6, 0:tiles * NROW]), S["smp_dve"])

            def branch_out(b):
                dve.wait_ge(S["smp_pe"], 9 - 2 * b)
                x = sw2[R, :].rearrange("p (a e) -> p a e", e=HD)
                one(v.tensor_tensor(x.rearrange("p (b a) e -> p b a e", b=2), bank[R, 2 - 2 * b:4 - 2 * b, :].rearrange("p b (a e) -> p b a e", e=HD),
                                    sel16[R, :].rearrange("p (b a o) -> p b a o", b=2, o=1).to_broadcast([NROW, 2, 8, HD]), ALU.mult))
                one(v.tensor_reduce(sw2o[R, :], sw2[R, :].rearrange("p (a e) -> p e a", e=HD), AX, ALU.add))
                one(v.scalar_tensor_tensor(oS[R, :], vn[:, b, :], stat[R, 19 + b:20 + b], oS[R, :], ALU.mult, ALU.add))
                one(v.scalar_tensor_tensor(oS[R, :], sw2o[R, :], stat[R, 17 + b:18 + b], oS[R, :], ALU.mult, ALU.add), S["smp_dve"])

            branch_max(1)
            dve.wait_ge(S["smp_pe"], 4)
            pt = PT[:, 0, 0:2, :].rearrange("p a k -> p (a k)")
            one(v.tensor_copy(pt[:, 0:256], bank[:, 6, 0:256]), S["smp_dve"])
            pg = qf[R, 1728:1792]
            four = qf[R, 1792:1808]
            cand = qf[R, 1808:1822]
            one(v.tensor_copy(pg, bank[R, 4, 0:64]))
            dve.wait_ge(S["smp_pe"], 5)
            one(v.tensor_scalar(oS[R, :], bank[R, 7, 0:HD], selv[R, 0:1], None, ALU.mult))
            one(v.scalar_tensor_tensor(oS[R, :], bank[R, 7, HD:P], selv[R, 1:2], oS[R, :], ALU.mult, ALU.add))
            one(v.tensor_scalar(oS[R, :], oS[R, :], stat[R, 0:1], None, ALU.mult))
            branch_turned(1, 4)
            one(v.tensor_reduce(four, pg.rearrange("p (j i) -> p j i", i=4), AX, ALU.add))
            one(v.tensor_tensor(cand, four[:, 1:15], pg.rearrange("p (j i) -> p j i", i=4)[:, 0:14, 3], ALU.add))
            one(v.tensor_reduce(stat[R, 14:15], cand, AX, ALU.min))
            one(v.tensor_scalar(cand, cand, stat[R, 14:15], None, ALU.is_le))
            one(v.tensor_tensor(cand, cand, iota16[R, 1:15], ALU.mult))
            one(v.tensor_reduce(stat[R, 14:15], cand, AX, ALU.max))
            one(v.tensor_scalar(four, iota16[R, :], stat[R, 14:15], NEG, ALU.is_equal, ALU.mult))
            branch_max(0)
            branch_turned(0, NPG)
            branch_out(1)
            branch_out(0)
            dve.wait_ge(S["smp_pe"], 10)
            for kv in range(NKV):
                one(v.tensor_copy(oT[kv * HD:(kv + 1) * HD, :, NPR:NT],
                                  bank[0:HD, 7, 0:NROW].rearrange("p (n g v) -> p v g n", n=NSA, g=NG)[:, kv, :, :]),
                    S["smp_dve"] if kv else None)

            for m in range(KD):
                dve.wait_ge(S["sg_ready"], 2 * m + 1)
                dve.wait_ge(S["pa_done"], m + 1)
                one(v.scalar_tensor_tensor(split(mT[:, m, :]), split(sg[:, 0, :]), 1.0, halves(1), ALU.add, ALU.mult))
                dve.wait_ge(S["sg_ready"], 2 * m + 2)
                dve.wait_ge(S["pb_done"], m + 1)
                one(v.scalar_tensor_tensor(split(mb), split(sg[:, 1, :]), 1.0, halves(3), ALU.add, ALU.mult))
                one(v.tensor_tensor(mT[:, m, :], mT[:, m, :], mb, ALU.add), S["m_ready"])

            N = slice(0, RN)

            def residual(t):
                dve.wait_ge(S["wo_done"], t + 1)
                dve.wait_ge(x_rows_in[t % 2], 16 * (t // 2 + 1))
                if t >= 3:
                    dve.wait_ge(y0_out[t % 3], 16)
                b = 6 * (t % 2)
                one(v.scalar_tensor_tensor(xm[N, t % 3, :].rearrange("p (h n) -> p h n", h=2), bank[N, b:b + 2, :], 0.5,
                                           xr[N, t % 2, :].rearrange("p (h n) -> p h n", h=2), ALU.mult, ALU.add), S["xm_ready"])

            def normalise(t):
                dve.wait_ge(S["rstd2"], t + 1)
                one(v.reciprocal(stat[N, 4:5], stat[N, 1:2]))
                if t >= 2:
                    dve.wait_ge(t_out[t % 2], 16 * (t // 2))
                    dve.wait_ge(S["t_turned"], t - 1)
                if t == 0:
                    dve.wait_ge(S["router_in"], ROUTER_IN)
                one(v.scalar_tensor_tensor(tn[N, t % 2, :], xm[N, t % 3, :], stat[N, 4:5], gffn[N, :], ALU.mult, ALU.mult),
                    S["t_ready"])

            def choose(t):
                dve.wait_ge(S["lg_done"], t + 1)
                one(v.tensor_tensor(lg[N, t, :], bank[N, 4, t * NE:(t + 1) * NE], rbias[N, :], ALU.add))
                one(v.max(mx8[N, t, :], lg[N, t, :]))
                mine(v.tensor_scalar(stat[N, 2:3], mx8[N, t, 0:1], -1.0, None, ALU.mult))
                one(v.tensor_copy(ixf[N, t, :], mx8[N, t, 0:4]), S["ex_in"])
                one(v.max_index(ix8[N, t, :].bitcast(U32), mx8[N, t, :], lg[N, t, :]))
                one(v.tensor_copy(rs[N, 0:4], ix8[N, t, 0:4].bitcast(U32)))
                for k in range(TOPK):
                    mine(v.tensor_scalar(ohall[N, t, k, :], iota_e[N, :], rs[N, k:k + 1], None, ALU.is_equal))
                mine.settle()
                one(v.tensor_reduce(m4[N, t, :], ohall[N, t, :, :].rearrange("p k e -> p e k"), AX, ALU.add), S["m4_ready"])
                dve.wait_ge(S["ex_done"], t + 1)
                one(v.reciprocal(stat[N, 5:6], stat[N, 3:4]))
                one(v.tensor_scalar(gate[N, t, :], ixf[N, t, :], stat[N, 5:6], None, ALU.mult))
                if t >= 2:
                    dve.wait_ge(S["gd_turned"], t - 1)
                g = gd[t % 2][N, :]
                one(v.tensor_scalar(g, ohall[N, t, 0, :], gate[N, t, 0:1], None, ALU.mult))
                for k in range(1, TOPK):
                    one(v.scalar_tensor_tensor(g, ohall[N, t, k, :], gate[N, t, k:k + 1], g, ALU.mult, ALU.add),
                        S["gd_ready"] if k == TOPK - 1 else None)

            def places(t):
                dve.wait_ge(S["pos_done"], t + 1)
                one(v.tensor_tensor(posn[N, t, :], bank[N, 5, P:P + NE], slot_e[N, :], ALU.add))
                x = ohall[N, t, :, :]
                one(v.tensor_tensor(x, x, posn[N, t, :].rearrange("p (o e) -> p o e", o=1).to_broadcast([RN, 4, NE]), ALU.mult))
                mine(v.tensor_copy(pairs[N, t, :, 0].bitcast(I32), tokid[N, t:t + 1].to_broadcast([RN, 4])))
                mine(v.tensor_copy(pairs[N, t, :, 1], gate[N, t, :]))
                one(v.tensor_reduce(dst[N, t, :], x, AX, ALU.add))
                one(v.tensor_copy(dsti[N, t, :].bitcast(I32), dst[N, t, :]), S["ent_ready"])

            def first_rows(t):
                dve.wait_ge(S["bd_done"], t + 1)
                x = xm[N, t % 3, :].rearrange("p (h n) -> p h n", h=2)
                one(v.tensor_tensor(x, x, bank[N, 2:4, :], ALU.add), S["y0_ready"])

            for t in range(RT + 2):
                if t < RT:
                    residual(t)
                if 2 <= t <= RT:
                    places(t - 2)
                if t < RT:
                    normalise(t)
                if 1 <= t <= RT:
                    choose(t - 1)
                if t == RT:
                    places(RT - 1)
                    one(v.tensor_reduce(ovf[N, 0:1], bank[N, 5, P + NE:P + 2 * NE], AX, ALU.max))
                    one(v.tensor_copy(ovf[N, 1:2].bitcast(I32), ovf[N, 0:1]), S["ovf_ready"])
                if t >= 2:
                    first_rows(t - 2)

            dve.wait_ge(S["bup_in"], 16)
            dve.wait_ge(y0_out[0], 32)
            dve.sem_inc(S["up_read"], 4)

            def block_of(n, e, par):
                one_bias = bu2[par]
                v.tensor_copy(one_bias, bup[:, bass.ds(e, 1), :].rearrange("p o c -> p (o c)")).then_inc(S["bias_ready"], 1)
                dve.wait_ge(S["bias_ready"], n + 1)
                for hf in range(2):
                    dve.wait_ge(S["ring_used"], 6 * n + 2 * hf + 1)
                    for f in range(4):
                        c = 4 * hf + f
                        r = v.tensor_scalar(AA[hf][:, f * P:(f + 1) * P], bank[:, 2 * hf, f * P:(f + 1) * P],
                                            one_bias[:, c:c + 1], LIMIT, ALU.add, ALU.min)
                    r.then_inc(S["up_read"], 1)
                    dve.wait_ge(S["ring_used"], 6 * n + 2 * hf + 2)
                    for f in range(4):
                        c = KD + 4 * hf + f
                        r = v.tensor_scalar(UU[hf][:, f * P:(f + 1) * P], bank[:, 2 * hf + 1, f * P:(f + 1) * P],
                                            one_bias[:, c:c + 1], LIMIT, ALU.add, ALU.min)
                    r.then_inc(S["up_read"], 1)
                    dve.wait_ge(S["up_read"], 4 * n + 2 * hf + 6)
                    v.tensor_scalar(UU[hf], UU[hf], -LIMIT, 1.0, ALU.max, ALU.add).then_inc(S["u_ready"], 1)
                    dve.wait_ge(S["u_ready"], 2 * n + hf + 1)
                    v.tensor_tensor(UU[hf], UU[hf], AA[hf], ALU.mult).then_inc(S["ua_ready"], 1)
                    dve.wait_ge(S["ua_ready"], 2 * n + hf + 1)
                    dve.wait_ge(S["sig_ready"], 2 * n + hf + 1)
                    v.tensor_tensor(UU[hf], UU[hf], SG[hf], ALU.mult).then_inc(S["h_ready"], 1)
                    dve.wait_ge(S["hh_ready"], 2 * n + hf + 1)
                    half = slice(4 * hf, 4 * hf + 4)
                    v.tensor_tensor(HL[:, half, :].rearrange("p f t -> p (f t)"), UU[hf],
                                    HHf[:, hf * 512:(hf + 1) * 512], ALU.subtract).then_inc(S["hl_ready"], 1)
                    if hf == 0:
                        for c in (4, 5):
                            dve.wait_ge(S["wh_ready"], 2 * n + c - 3)
                            v.tensor_tensor(expert_slot_low(c), expert_slot(c), WHf[c - 4], ALU.subtract).then_inc(S["wl_ready"], 1)

            with dve.Fori(0, NE // 2) as pair:
                block_of(2 * pair, 2 * pair, 0)
                block_of(2 * pair + 1, 2 * pair + 1, 1)
            dve.wait_ge(S["ovf_ready"], 1)
            most = dve.value_load(ovf[0:1, 1:2].bitcast(I32), min_val=0, max_val=NT)
            with dve.If(most > P):
                with dve.Fori(0, NE) as e:
                    for b in range(4):
                        block_of(4 * e + (NE + b), e, b % 2)

        @block.gpsimd
        def _(pool):
            dma = pool.dma_start
            dma(ident[:, :], d["ident"]).then_inc(S["ident_in"], 16)
            dma(pagetab[0:1, :].bitcast(I32), d["pages"]).then_inc(S["page_in"], 16)
            dma(gain.rearrange("p h c -> p (h c)"), d["gains"]).then_inc(S["gains_in"], 16)
            pool.wait_ge(S["qk_ready"], TT)
            dma(oT_st[:, 0:2 * KD * P], d["blockw"]).then_inc(S["bd_in"], 16)
            for t in range(TT):
                m = fraction(t)
                dma(d["o_kv"][t * P:t * P + m, :], kvraw[0:m, t, 0:KVC]).then_inc(S["kv_out"], 16)
            dma(d["o_vwin"][:, WIN - 1, :], kvraw[0:NSA, QT_N, VC + 2 * P:VC + 3 * P]).then_inc(S["kv_out"], 16)
            dma(table, d["table0"]).then_inc(S["table_in"], 16)
            dma(trow[NT:NT + P, :], d["zeros"]).then_inc(S["table_in"], 16)
            dma(d["y"][NT:NT + P, :], d["zeros"]).then_inc(S["table_in"], 16)
            dma(d["o_kwin"][:, :, 0:WIN - 1], d["k_win"][:, :, 1:WIN]).then_inc(S["outs_done"], 16)
            dma(d["o_vwin"][:, 0:WIN - 1, :], d["v_win"][:, 1:WIN, :]).then_inc(S["outs_done"], 16)
            pool.wait_ge(S["qk_dve"], TT)
            dma(d["o_kwin"][:, :, WIN - 1], kT[:, 2, NPR:NT], allow_slow_non_contiguous=True).then_inc(S["outs_done"], 16)
            for other in dict.fromkeys(before["xsv"]):
                pool.wait_ge(*frees[other])
            some_pages(pool, chunk("xsv", 2), d["v_cmp"], S["xsv_in_pool"], NPAGES // 2, NPAGES // 2)
            pool.wait_ge(S["y_ready"], KD)
            pool.wait_ge(S["i_done"], KD)
            dma(w2.rearrange("p v f c -> p (v f c)"), d["w2"]).then_inc(S["w2_in"], 16)
            dma(d["o_h"], hout).then_inc(S["outs_done"], 16)
            dma(d["o_pconv"], pconv).then_inc(S["outs_done"], 16)
            dma(d["o_sconv"], xps).then_inc(S["outs_done"], 16)
            pool.wait_ge(S["ck_copied"], 2 * NG)
            dma(smask[0:NROW, :], d["smask"]).then_inc(S["smask_in"], 16)
            pool.wait_ge(S["smp_dve"], 8)
            dma(gffn[:, :], d["g_ffn"]).then_inc(S["router_in"], 16)
            dma(bdn[:, :], d["b_down"]).then_inc(S["router_in"], 16)
            dma(rwt.rearrange("p k e -> p (k e)"), d["router_w"]).then_inc(S["router_in"], 16)
            dma(rcon[:, 0:200], d["rcon"]).then_inc(S["router_in"], 16)
            dma(tokid, d["tokid"]).then_inc(S["router_in"], 16)
            def first_rows_out(t):
                pool.wait_ge(S["y0_ready"], t + 1)
                dma(d["y"][t * RN:(t + 1) * RN, :], xm[0:RN, t % 3, :]).then_inc(y0_out[t % 3], 16)

            pool.wait_ge(S["kv_out"], 16 * (TT + 1))
            for t in range(2):
                dma(xr[0:RN, t, :], d["x_rows"][t * RN:(t + 1) * RN, :]).then_inc(x_rows_in[t], 16)
            pool.wait_ge(S["m_ready"], KD)
            dma(bup.rearrange("p e c -> p (e c)"), d["b_up"]).then_inc(S["bup_in"], 16)
            pool.wait_ge(S["table_in"], 48)
            for t in range(RT + 2):
                if t < RT:
                    pool.wait_ge(S["t_ready"], t + 1)
                    dma(trow[t * RN:(t + 1) * RN, :], tn[0:RN, t % 2, :]).then_inc(t_out[t % 2], 16)
                if t + 2 < RT:
                    dma(xr[0:RN, t % 2, :], d["x_rows"][(t + 2) * RN:(t + 3) * RN, :]).then_inc(x_rows_in[t % 2], 16)
                if t >= 2:
                    pool.wait_ge(S["ent_ready"], t - 1)
                    for k in range(TOPK):
                        pool.indirect_dma_start(out=table, out_offset=bass.IndirectOffsetOnAxis(ap=dsti[0:RN, t - 2, k:k + 1].bitcast(U32), axis=0),
                                                in_=pairs[0:RN, t - 2, k, :].bitcast(I32), in_offset=None)\
                            .then_inc(S["scattered"], 16)
                    if t < RT:
                        first_rows_out(t - 2)
            pool.wait_ge(S["scattered"], 16 * RT * TOPK)
            for b in (0, 1):
                pool.wait_ge(t_out[b], 16 * ((RT + 1 - b) // 2))

            def gather(n, par, row):
                dma(ent[par][:, :], table[bass.ds(row, P), :]).then_inc(S["ent_in"], 16)
                pool.wait_ge(S["ent_in"], 16 * n + 16)
                pool.sem_inc(S["pool_steps"], 1)
                pool.indirect_dma_start(out=GX[par][:, :], out_offset=None, in_=trow[:, :],
                                        in_offset=bass.IndirectOffsetOnAxis(ap=ent[par][:, 0:1].bitcast(U32), axis=0))\
                    .then_inc(S["xg_in"], 16)

            def add_rows(n, par):
                pool.wait_ge(S["y_scaled"], n + 2)
                pool.sem_inc(S["pool_steps"], 1)
                pool.indirect_dma_start(out=d["y"][:, :], out_offset=bass.IndirectOffsetOnAxis(ap=ent[par][:, 0:1].bitcast(U32), axis=0),
                                        in_=YR[par], in_offset=None, compute_op=ALU.add).then_inc(S["y_added"], 16)
                pool.wait_ge(S["y_added"], 16 * n + 16)

            gather(0, 0, 0)
            first_rows_out(RT - 2)
            first_rows_out(RT - 1)
            for b in range(3):
                pool.wait_ge(y0_out[b], 16 * ((RT + 2 - b) // 3))
            gather(1, 1, SLOTS)
            with pool.Fori(0, NE // 2 - 1) as pair:
                for b in range(2):
                    add_rows(2 * pair + b, b)
                    gather(2 * pair + (b + 2), b, (2 * pair + (b + 2)) * SLOTS)
            add_rows(NE - 2, 0)
            add_rows(NE - 1, 1)
            pool.wait_ge(S["ovf_ready"], 1)
            most = pool.value_load(ovf[0:1, 1:2].bitcast(I32), min_val=0, max_val=NT)
            with pool.If(most > P):
                with pool.Fori(0, NE) as e:
                    for b in range(4):
                        gather(4 * e + (NE + b), b % 2, e * SLOTS + (b + 1) * P)
                        add_rows(4 * e + (NE + b), b % 2)
            pool.wait_ge(S["outs_done"], 16 * 6)




def _constants():
    c = {}
    f = np.float32
    q, k = np.arange(P)[:, None], np.arange(P)[None, :]
    c["causal"] = np.where(k <= q, 0.0, NEG).astype(f)
    c["ident"] = np.eye(P, dtype=f)
    cm = np.zeros((P, QT_N, 32), f)
    for t in range(QT_N):
        pos = t * P + np.arange(P)[:, None]
        ch = np.arange(32)[None, :]
        cm[:, t, :] = (ch * 16 + 31 <= pos) & (ch < NCH - 1)
    c["cmask"] = cm.reshape(P, -1)
    half = HD // 8
    inv = (f(500000.0) ** (-np.arange(half, dtype=f) / f(half))).astype(f)
    rope = np.zeros((P, TT, 16), f)
    for t in range(TT):
        pos = (t * P + np.arange(P)).astype(f) if t < QT_N else np.full(P, PAST, f)
        ang = (pos[:, None] * inv[None, :]).astype(f)
        rope[:, t, 0:8], rope[:, t, 8:16] = np.cos(ang), np.sin(ang)
    c["rope"] = rope.reshape(P, -1)
    r = np.arange(NROW)
    rn, rg, rv = r // NH, r % NH // NKV, r % NKV
    pad = lambda a: np.concatenate([a.astype(f), np.zeros((P - a.shape[0], a.shape[1]), f)])
    c["sel16"] = pad((np.arange(16)[None, :] == (rn * 2 + rv)[:, None]))
    c["sel8"] = pad(np.arange(8)[None, :] == rn[:, None])
    c["selh"] = pad(np.arange(8)[None, :] == (rg * 2 + rv)[:, None])
    c["selv"] = pad(np.arange(2)[None, :] == rv[:, None])
    c["rmat"] = pad((rn * 2 + rv)[:, None] == (rn * 2 + rv)[None, :])
    c["emat"] = pad(np.arange(NSA)[:, None] == rn[None, :])
    c["iota16"] = np.tile(np.arange(16, dtype=f), (P, 1))
    n, ch = np.arange(512) // CHS, np.arange(512) % CHS
    c["smask"] = np.where((n[None, :] == rn[:, None]) & (ch < CHS - 1)[None, :], 0.0, NEG).astype(f)
    c["rcon"] = np.concatenate([np.tile(np.arange(NE, dtype=f), (P, 1)), np.tile(np.arange(NE, dtype=f) * SLOTS, (P, 1)),
                                (np.arange(P)[:, None] < np.arange(RN)[None, :]).astype(f)], 1)
    c["tokid"] = (np.arange(RT)[None, :] * RN + np.arange(P)[:, None]).astype(np.int32)
    slots = np.arange(NE * SLOTS)
    c["table0"] = np.stack([TRASH + slots % P, 0 * slots], 1).astype(np.int32)
    return c


def _layouts(x):
    c = _constants()
    f = np.float32
    d = {}
    rows = np.concatenate([x["x_prompt"][0], x["x_sample"][:, 0]], 0)
    chan = lambda v: np.ascontiguousarray(v.reshape(KD, P).T)
    d["x_rows"] = rows
    d["xT"] = rows.T.reshape(KD, P, NT).transpose(1, 0, 2)
    w = x["w_in"][0]
    ar, ag = w[:, 0:D], w[:, D:2 * D]
    o = 2 * D
    q = w[:, o:o + QC].reshape(D, NKV, NG, HD).transpose(0, 2, 1, 3).reshape(D, QC)
    o += QC
    kv = [w[:, o + i * P:o + (i + 1) * P] for i in range(6)]
    o += KVC
    ng = w[:, o:o + 24].reshape(D, NKV, NG, 3).transpose(0, 3, 2, 1).reshape(D, 24)
    o += 24
    ga, gb = w[:, o:o + D], w[:, o + D:o + 2 * D]
    tok = np.concatenate([q] + kv[0::2] + kv[1::2] + [ng], 1)
    d["w_tok"] = tok.reshape(KD, P, TC).transpose(1, 0, 2)

    def cols(a):
        k = a.shape[0] // P
        return a.reshape(k, P, 2, 512).transpose(2, 1, 0, 3).reshape(2, P, k * 512)

    d["w_ch"] = np.concatenate([cols(a) for a in (ar, ag, ga, gb)], 0)
    d["w_pa"] = cols(x["w_proj_a"][0])
    d["w_pb"] = cols(x["w_proj_b"][0].reshape(NKV, NG, HD, D).transpose(1, 0, 2, 3).reshape(QC, D))
    d["w_out"] = cols(x["w_out"][0])
    lru = np.stack([chan(x["conv_w"][0, k]) for k in range(4)] + [chan(x["conv_b"][0]), chan(x["lru_ba"][0].reshape(D)),
                   chan(x["lru_bx"][0].reshape(D)), chan(x["lru_lambda"][0])], 2)
    h0 = x["state_h"][0].reshape(NSA, KD, P).transpose(2, 1, 0)
    conv = np.zeros((P, KD, NSA, 4), f)
    conv[:, :, :, 0:3] = x["state_conv"][0].reshape(NSA, 3, KD, P).transpose(3, 2, 0, 1)
    pos = np.stack([x["cmp_pos_k"][0], x["cmp_pos_v"][0]]).reshape(2, 2, LP, 2, HD)
    flat = lambda a: a.reshape(P, -1)
    pos = pos.transpose(3, 4, 0, 2, 1)
    small = [c["cmask"], c["rope"], chan(x["g_mix"][0]), flat(lru), flat(h0), flat(conv),
             c["causal"], np.ones((P, P), f), c["sel16"], c["sel8"], c["selh"], c["selv"], c["rmat"], c["emat"],
             flat(pos), c["iota16"]]
    d["small"] = np.concatenate(small, 1)
    d["ident"] = c["ident"]
    d["pages"] = x["page_table"].reshape(1, NPAGES).astype(np.int32)
    gains = np.concatenate([np.tile(x["g_q"][0], NH)] + [np.tile(x[n][0], NKV) for n in ("g_k_cmp", "g_k_slc", "g_k_win")])
    d["gains"] = np.broadcast_to(gains, (P, NHN * HD))
    bd = np.zeros((2, KD, P, P), f)
    for i, n in enumerate(("lru_wa", "lru_wx")):
        blocks = x[n][0].reshape(KD, 2, HD, HD)
        bd[i, :, 0:HD, 0:HD], bd[i, :, HD:P, HD:P] = blocks[:, 0], blocks[:, 1]
    d["blockw"] = flat(bd.transpose(2, 0, 1, 3))
    d["w1"] = np.stack([x[n][0].reshape(2, LP, 2, HD, CF).transpose(2, 3, 0, 1, 4).reshape(P, SLOT)
                        for n in ("cmp_w1_k", "cmp_w1_v")])
    w2 = np.zeros((P, 2, 2, 3 * HD), f)
    for i, n in enumerate(("cmp_w2_k", "cmp_w2_v")):
        w2[:, i, :, HD:2 * HD] = x[n][0].reshape(2, P, HD).transpose(1, 0, 2)
    d["w2"] = flat(w2)
    phys = x["cache_k_cmp"].shape[1]
    for n, s in (("k_cmp", "cache_k_cmp"), ("v_cmp", "cache_v_cmp")):
        a = x[s][0].reshape(phys, 8, LP, 2, NKV, HD).transpose(0, 3, 5, 2, 4, 1)
        d[n] = a.reshape(phys * P, P)
    d["k_slc"] = x["cache_k_slc"][0].transpose(0, 2, 3, 1).reshape(phys * P, P)
    d["v_slc"] = x["cache_v_slc"][0].reshape(phys * P, P)
    d["k_win"] = x["cache_k_win"][0].transpose(2, 3, 0, 1).reshape(P, NSA, WIN)
    d["v_win"] = x["cache_v_win"][0].reshape(NSA, WIN, P)
    d["smask"] = c["smask"]
    d["g_ffn"] = np.broadcast_to(x["g_ffn"][0], (P, D))
    d["b_down"] = x["exp_b_down"][0]
    d["router_w"] = flat(x["router_w"][0].reshape(KD, P, NE).transpose(1, 0, 2))
    d["rbias"] = np.broadcast_to(x["router_b"][0], (P, NE))
    d["rcon"] = np.concatenate([d.pop("rbias"), c["rcon"]], 1)
    d["tokid"] = c["tokid"]
    d["table0"] = c["table0"]
    d["zeros"] = np.zeros((P, D), f)
    d["b_up"] = flat(x["exp_b_up"][0].reshape(NE, 2 * KD, P).transpose(2, 0, 1))
    d["w_up"] = x["exp_w_up"][0].reshape(NE * D, 2 * D)
    d["w_down"] = x["exp_w_down"][0].reshape(NE * D, D)
    return {n: np.ascontiguousarray(a) for n, a in d.items()}, phys


_OUTPUTS = {"y": (NT + P, D), "o_kv": (NT, KVC), "o_kwin": (P, NSA, WIN), "o_vwin": (NSA, WIN, P),
            "o_h": (P, KD, 9), "o_pconv": (P, KD, 3), "o_sconv": (P, KD, NSA, 4)}


def kernel(**inputs):
    import concourse.bacc as bacc
    from concourse.bass_utils import run_bass_kernel_spmd as run

    arrays, phys = _layouts({n: np.asarray(a) for n, a in inputs.items()})
    nc = bacc.Bacc("TRN2", target_bir_lowering=False, num_devices=1)
    d = {n: nc.dram_tensor("in_" + n, a.shape, mybir.dt.from_np(a.dtype), kind="ExternalInput").ap() for n, a in arrays.items()}
    d |= {n: nc.dram_tensor("out_" + n, s, F32, kind="ExternalOutput").ap() for n, s in _OUTPUTS.items()}
    d["n_phys"] = phys
    build(nc, d)
    got = run(nc, [{"in_" + n: a for n, a in arrays.items()}], core_ids=[0]).results[0]
    o = {n: got["out_" + n] for n in _OUTPUTS}
    kv = o["o_kv"].reshape(NT, 6, NKV, HD)
    prompt = lambda i: kv[0:NPR, i][None, None]
    sample = lambda i: kv[NPR:NT, i][None, :, None]
    chan = lambda a: a.transpose(1, 0, *range(2, a.ndim)).reshape(D, -1)
    h = chan(o["o_h"]).T
    sconv = chan(o["o_sconv"]).reshape(D, NSA, 4)[:, :, 1:4].transpose(1, 2, 0)
    kwin = o["o_kwin"].reshape(NKV, HD, NSA, WIN).transpose(2, 3, 0, 1)
    return (o["y"][0:NPR][None], o["y"][NPR:NT][:, None],
            prompt(0), prompt(3), prompt(1), prompt(4), prompt(2), prompt(5),
            h[0:1][None], chan(o["o_pconv"]).T[None, None],
            sample(0), sample(3), sample(1), sample(4),
            kwin[None], o["o_vwin"].reshape(NSA, WIN, NKV, HD)[None],
            h[1:9][None], sconv[None])
```
